# Optimizing a Trainium2 kernel written in Bass

```python
import math
import jax, jax.numpy as jnp
from jax import lax
import numpy as np

D_MODEL = 1024
BATCH = 1
SEQ = 256
DEPTH = 2

PLE_DIM = 256
N_MIXERS = 2
N_EVEN = (DEPTH + 1) // 2
N_ODD = DEPTH // 2

DH = 64
N_HEADS = D_MODEL // (2 * DH)
QK_WIDTH = N_HEADS * 2 * DH
V_WIDTH = N_HEADS * 2 * DH
QKV_WIDTH = 2 * QK_WIDTH + V_WIDTH
ATTN_SCALE = 1.0 / math.sqrt(DH)
ROPE_THETA = 10000.0
Q_BLOCK = 128

POOL_WINDOWS = (2, 4, 8, 16)
N_GROUPS = len(POOL_WINDOWS)
GROUP_W = D_MODEL // N_GROUPS

D_FF = 2816
N_EXPERTS = 8
TOP_K = 2
D_FF_EXPERT = 3584

RMS_EPS = 1e-6

kernel_name = "hybrid_diffattn_pool_moe_ple"

def rms_norm(x, g, eps=RMS_EPS):
    xf = x.astype(jnp.float32)
    y = xf * lax.rsqrt(jnp.mean(xf * xf, axis=-1, keepdims=True) + eps)
    return (y * g.astype(jnp.float32)).astype(x.dtype)

def rope_tables(seq, dim):
    inv = 1.0 / (ROPE_THETA ** (jnp.arange(0, dim, 2, dtype=jnp.float32) / dim))
    ang = jnp.arange(seq, dtype=jnp.float32)[:, None] * inv[None, :]
    return jnp.cos(ang), jnp.sin(ang)

def apply_rope(x, cos, sin):
    c = cos[None, :, None, None, :].astype(x.dtype)
    s = sin[None, :, None, None, :].astype(x.dtype)
    x1, x2 = jnp.split(x, 2, axis=-1)
    return jnp.concatenate([x1 * c - x2 * s, x2 * c + x1 * s], axis=-1)

def diff_attention(xn, w_qkv, w_o, q_norm, k_norm, lq1, lk1, lq2, lk2, subln_g, lam_init):
    B, S, _ = xn.shape
    qkv = xn @ w_qkv
    q, k, v = jnp.split(qkv, [QK_WIDTH, 2 * QK_WIDTH], axis=-1)
    q = q.reshape(B, S, N_HEADS, 2, DH)
    k = k.reshape(B, S, N_HEADS, 2, DH)
    v = v.reshape(B, S, N_HEADS, 2 * DH)
    cos, sin = rope_tables(S, DH)
    q = apply_rope(rms_norm(q, q_norm), cos, sin)
    k = apply_rope(rms_norm(k, k_norm), cos, sin)
    lam = (jnp.exp(jnp.sum(lq1.astype(jnp.float32) * lk1.astype(jnp.float32)))
           - jnp.exp(jnp.sum(lq2.astype(jnp.float32) * lk2.astype(jnp.float32)))
           + lam_init)
    outs = []
    for blk in range(S // Q_BLOCK):
        q0 = blk * Q_BLOCK
        q1 = q0 + Q_BLOCK
        qb = q[:, q0:q1]
        kb = k[:, :q1]
        vb = v[:, :q1]
        s = jnp.einsum('bqhcd,bkhcd->bhcqk', qb, kb).astype(jnp.float32) * ATTN_SCALE
        mask = jnp.arange(q1)[None, :] <= jnp.arange(q0, q1)[:, None]
        s = jnp.where(mask, s, -jnp.inf)
        a = jax.nn.softmax(s, axis=-1)
        a = a[:, :, 0] - lam * a[:, :, 1]
        outs.append(jnp.einsum('bhqk,bkhe->bqhe', a.astype(vb.dtype), vb))
    o = jnp.concatenate(outs, axis=1)
    o = rms_norm(o, subln_g) * (1.0 - lam_init)
    return o.reshape(B, S, V_WIDTH) @ w_o

def pool_mixer(xn, w_pool, b_pool, scale):
    B, S, D = xn.shape
    xg = xn.reshape(B, S, N_GROUPS, GROUP_W).astype(jnp.float32)
    csum = jnp.cumsum(xg, axis=1)
    t = jnp.arange(S)
    outs = []
    for g, w in enumerate(POOL_WINDOWS):
        cg = csum[:, :, g]
        prev = jnp.pad(cg, ((0, 0), (w, 0), (0, 0)))[:, :S]
        cnt = jnp.minimum(t + 1, w).astype(jnp.float32)[None, :, None]
        outs.append((cg - prev) / cnt - xg[:, :, g])
    y = jnp.stack(outs, axis=2).astype(xn.dtype)
    y = jnp.einsum('bsgc,gce->bsge', y, w_pool) + b_pool
    return y.reshape(B, S, D) * scale

def swiglu(xn, w_gate, w_up, w_down):
    return (jax.nn.silu(xn @ w_gate) * (xn @ w_up)) @ w_down

def moe_swiglu(xn, w_router, w_gate, w_up, w_down):
    logits = (xn @ w_router).astype(jnp.float32)
    top_v, top_i = lax.top_k(logits, TOP_K)
    top_w = jax.nn.softmax(top_v, axis=-1)
    gates = jnp.sum(jax.nn.one_hot(top_i, N_EXPERTS, dtype=jnp.float32) * top_w[..., None], axis=-2)
    out = jnp.zeros_like(xn)
    for e in range(N_EXPERTS):
        ye = swiglu(xn, w_gate[e], w_up[e], w_down[e])
        out = out + gates[..., e:e + 1].astype(xn.dtype) * ye
    return out

def setup_inputs(seed: int = 0) -> dict:
    key = jax.random.key(seed)
    ks = iter(jax.random.split(key, 40))
    f32 = jnp.float32

    def w(shape, fan_in):
        return jax.random.normal(next(ks), shape, f32) * (fan_in ** -0.5)

    def gain(shape):
        return 1.0 + 0.02 * jax.random.normal(next(ks), shape, f32)

    return {
        "x": jax.random.normal(next(ks), (BATCH, SEQ, D_MODEL), f32),
        "p": jax.random.normal(next(ks), (DEPTH, BATCH, SEQ, PLE_DIM), f32),
        "norm_mix": gain((DEPTH, D_MODEL)),
        "norm_ffn": gain((DEPTH, D_MODEL)),
        "norm_ple": gain((DEPTH, D_MODEL)),
        "attn_w_qkv": w((N_EVEN, D_MODEL, QKV_WIDTH), D_MODEL),
        "attn_w_o": w((N_EVEN, V_WIDTH, D_MODEL), V_WIDTH),
        "attn_q_norm": gain((N_EVEN, DH)),
        "attn_k_norm": gain((N_EVEN, DH)),
        "attn_lambda_q1": 0.1 * jax.random.normal(next(ks), (N_EVEN, DH), f32),
        "attn_lambda_k1": 0.1 * jax.random.normal(next(ks), (N_EVEN, DH), f32),
        "attn_lambda_q2": 0.1 * jax.random.normal(next(ks), (N_EVEN, DH), f32),
        "attn_lambda_k2": 0.1 * jax.random.normal(next(ks), (N_EVEN, DH), f32),
        "attn_subln": gain((N_EVEN, 2 * DH)),
        "pool_w": w((N_ODD, N_GROUPS, GROUP_W, GROUP_W), GROUP_W),
        "pool_b": 0.02 * jax.random.normal(next(ks), (N_ODD, N_GROUPS, GROUP_W), f32),
        "pool_scale": 1.0 + 0.1 * jax.random.normal(next(ks), (N_ODD, D_MODEL), f32),
        "ffn_w_gate": w((N_EVEN, D_MODEL, D_FF), D_MODEL),
        "ffn_w_up": w((N_EVEN, D_MODEL, D_FF), D_MODEL),
        "ffn_w_down": w((N_EVEN, D_FF, D_MODEL), D_FF),
        "moe_router": w((N_ODD, D_MODEL, N_EXPERTS), D_MODEL),
        "moe_w_gate": w((N_ODD, N_EXPERTS, D_MODEL, D_FF_EXPERT), D_MODEL),
        "moe_w_up": w((N_ODD, N_EXPERTS, D_MODEL, D_FF_EXPERT), D_MODEL),
        "moe_w_down": w((N_ODD, N_EXPERTS, D_FF_EXPERT, D_MODEL), D_FF_EXPERT),
        "ple_w_proj": w((DEPTH, PLE_DIM, D_MODEL), PLE_DIM),
        "ple_w_gate": w((DEPTH, D_MODEL, D_MODEL), D_MODEL),
    }

def reference(x, p, norm_mix, norm_ffn, norm_ple,
              attn_w_qkv, attn_w_o, attn_q_norm, attn_k_norm,
              attn_lambda_q1, attn_lambda_k1, attn_lambda_q2, attn_lambda_k2, attn_subln,
              pool_w, pool_b, pool_scale,
              ffn_w_gate, ffn_w_up, ffn_w_down,
              moe_router, moe_w_gate, moe_w_up, moe_w_down,
              ple_w_proj, ple_w_gate):
    h = x
    for i in range(DEPTH):
        j = i // 2
        xn = rms_norm(h, norm_mix[i])
        if i % N_MIXERS == 0:
            lam_init = 0.8 - 0.6 * math.exp(-0.3 * i)
            mix = diff_attention(xn, attn_w_qkv[j], attn_w_o[j], attn_q_norm[j], attn_k_norm[j],
                                 attn_lambda_q1[j], attn_lambda_k1[j],
                                 attn_lambda_q2[j], attn_lambda_k2[j], attn_subln[j], lam_init)
        else:
            mix = pool_mixer(xn, pool_w[j], pool_b[j], pool_scale[j])
        h = h + mix
        xn = rms_norm(h, norm_ffn[i])
        if i % 2 == 0:
            ff = swiglu(xn, ffn_w_gate[j], ffn_w_up[j], ffn_w_down[j])
        else:
            ff = moe_swiglu(xn, moe_router[j], moe_w_gate[j], moe_w_up[j], moe_w_down[j])
        h = h + ff
        gate = jax.nn.sigmoid(rms_norm(h, norm_ple[i]) @ ple_w_gate[i])
        h = h + gate * (p[i].astype(h.dtype) @ ple_w_proj[i])
    return h


_drawn_inputs = setup_inputs


def setup_inputs(seed=0):
    import zlib

    import numpy as np

    out = dict(_drawn_inputs(seed))
    spreads = {}
    factors = {'norm_ple': 200.0,
     'attn_q_norm': 2.793,
     'attn_lambda_q1': 2.957,
     'attn_lambda_k1': 6.682,
     'attn_subln': 3.013,
     'pool_b': 19.354,
     'norm_ffn': 3.566,
     'attn_lambda_k2': 3.128,
     'pool_scale': 3.483}
    for name, (base, spread) in spreads.items():
        noise = np.random.default_rng([zlib.crc32(name.encode()), seed]).standard_normal(out[name].shape)
        drawn = base * np.exp(spread * noise) if base else spread * noise
        out[name] = __import__('jax').numpy.asarray(drawn.astype(out[name].dtype))
    for name, factor in factors.items():
        out[name] = (out[name] * factor).astype(out[name].dtype)
    return out
```

```python
from contextlib import ExitStack

import concourse.bass as bass
from concourse import mybir

F32 = mybir.dt.float32
F32R = mybir.dt.float32r
I32 = mybir.dt.int32
U32 = mybir.dt.uint32
ALU = mybir.AluOpType
ACT = mybir.ActivationFunctionType
AX_X = mybir.AxisListType.X

P = 128
SEQ = 256
TT = SEQ // P
D = 1024
KD = D // P
DH = 64
HEADS = D // (2 * DH)
SUB = 2 * HEADS
NE = 8
FF = 2816
FE = 3584
PLE = 256
EPS = 1e-6
LAM_INIT = 0.2
SCALE = DH ** -0.5
MASKED = -1e30

UNIT = 2048
RAW = 7
SPLIT = 3
AHEAD = 2

U_QKV = 0
U_WO = 12
U_FFN = 16
JF = FF // 256
U_PLE0 = U_FFN + 3 * JF
U_POOL = U_PLE0 + 5
U_MOE = U_POOL + 1
FB = FE // 512
PER_EXPERT = 6 * FB
U_TURN = U_MOE + PER_EXPERT - 2
SLOTS = P


def trunk(nc, dram):
    ctx = ExitStack()
    with ctx:
        def sb(name, shape, dt=F32):
            return ctx.enter_context(nc.sbuf_tensor(name, shape, dt))

        def sem(name):
            return ctx.enter_context(nc.semaphore(name))

        raw = sb("raw", [P, RAW, UNIT])
        w_hi = sb("w_hi", [P, SPLIT, UNIT], F32R)
        w_lo = sb("w_lo", [P, SPLIT, UNIT], F32R)
        resid = sb("resid", [P, TT, D])
        xs = sb("xs", [P, TT, D])
        a_hi = sb("a_hi", [P, UNIT], F32R)
        a_lo = sb("a_lo", [P, UNIT], F32R)
        wide = sb("wide", [P, 6144])
        h_t_hi = sb("h_t_hi", [P, 512], F32R)
        h_t_lo = sb("h_t_lo", [P, 512], F32R)
        xe_hi = sb("xe_hi", [P, D], F32R)
        xe_lo = sb("xe_lo", [P, D], F32R)
        y_hi = sb("y_hi", [P, D], F32R)
        y_lo = sb("y_lo", [P, D], F32R)
        tmp = sb("tmp", [P, UNIT])
        p_t_hi = sb("p_t_hi", [P, 2, 512], F32R)
        p_t_lo = sb("p_t_lo", [P, 2, 512], F32R)
        ident = sb("ident", [P, P])
        ones = sb("ones", [P, P])
        before = sb("before", [P, P])
        causal = sb("causal", [P, P])
        iota_slot = sb("iota_slot", [P, SLOTS])
        iota_expert = sb("iota_expert", [P, NE])
        gains = sb("gains", [P, 6 * KD + 1])
        rope = sb("rope", [P, TT, 2, DH // 2])
        qk_gain = sb("qk_gain", [P, 2, DH])
        rope_g = sb("rope_g", [P, 2, TT, 4, DH // 2])
        lam_sum = sb("lam_sum", [P, 2])
        neg_lam = sb("neg_lam", [P, 1])
        sub_gain = sb("sub_gain", [P, 1])
        minus_half = sb("minus_half", [P, 16])
        mean_sq = sb("mean_sq", [P, 96])
        rstd = sb("rstd", [P, 96])
        smax = sb("smax", [P, 2, 4])
        esum = sb("esum", [P, 2, 4])
        inv_count = sb("inv_count", [P, 16])
        router = sb("router", [P, KD * NE])
        router_hi = sb("router_hi", [P, KD * NE], F32R)
        router_lo = sb("router_lo", [P, KD * NE], F32R)
        logits = sb("logits", [P, TT, NE])
        top_v = sb("top_v", [P, TT, 8])
        top_i = sb("top_i", [P, TT, 8], U32)
        top_f = sb("top_f", [P, TT, 8])
        top_w = sb("top_w", [P, TT, 4])
        chose = sb("chose", [P, TT, 2, NE])
        mask = sb("mask", [P, 3, NE])
        gate = sb("gate", [P, TT, 2 * NE])
        place = sb("place", [P, TT, 2 * NE + 1])
        tokens = sb("tokens", [P, NE])
        more = sb("more", [P, 1], I32)
        pick = sb("pick", [P, TT * SLOTS], F32R)
        pick_t = sb("pick_t", [P, TT * P], F32R)
        ps = ctx.enter_context(nc.psum_tensor("ps", [P, 8, 512], F32))

        qkv = wide[:, :].rearrange("p (t n) -> p t n", t=TT)
        q_t = xs[:, :, :].rearrange("p t n -> p (t n)").rearrange("p (h s) -> p h s", h=HEADS)
        gain_bc = wide[:, 0:D]
        bias_bc = wide[:, D:2 * D]
        scale_bc = wide[:, 2 * D:3 * D]
        sums = wide[:, 3 * D:5 * D]
        part = [wide[:, 5 * D:5 * D + 512], wide[:, 5 * D + 512:6 * D]]
        p_sb = tmp[:, 0:D].rearrange("p (l t n) -> p l t n", l=2, t=TT)
        gain_rows = tmp[0:6 * KD + 1, D:D + P]
        lam_in = tmp[:, D + P:D + P + 4 * DH].rearrange("p (a d) -> p a d", a=4)
        lam_prod = tmp[:, D + P + 4 * DH:D + P + 6 * DH].rearrange("p (a d) -> p a d", a=2)
        squares = tmp[:, 0:D]
        turned = [tmp[:, D:D + 512], tmp[:, D + 512:2 * D]]
        probs = tmp[:, 0:D].rearrange("p (b n) -> p b n", b=2)
        probs_t = tmp[:, D:D + 512].rearrange("p (b n) -> p b n", b=2)
        hidden = tmp[:, 0:512]
        silu = tmp[:, 512:1024]
        sig = [tmp[:, 1024:1536], tmp[:, 1536:2048]]

        landed = [sem(f"landed{i}") for i in range(RAW)]
        (hi_ready, lo_ready, unit_used,
         x_landed, p_landed, rows_landed, small_landed, bc_landed, consts_ready,
         dve_chain, pool_chain, gains_transposed, gains_ready,
         p_transposed, p_hi_ready, p_lo_ready,
         squares_ready, mean_ready, rstd_ready, xs_ready, xs_transposed, xt_hi_ready, xt_lo_ready,
         resid_ready, block_copied,
         rope_g_ready, qk_squares, qk_mean, qk_rstd, qk_normed, qk_half, qk_rotated, qk_transposed, qk_t_copied,
         lam_summed, lam_exp, lam_ready,
         scores_ready, shift_ready, exp_ready, probs_ready, probs_transposed, probs_t_copied,
         av_ready, av_copied,
         o_squares, o_mean, o_rstd, o_normed, o_transposed, o_hi_ready, o_lo_ready,
         silu_ready, hidden_ready, hidden_transposed, ht_hi_ready, ht_lo_ready, sig_ready, gated,
         pool_x_ready, pool_y, pool_hi, pool_lo, pool_biased, pool_scaled,
         router_hi_ready, router_lo_ready, logits_ready, gap_ready, gap_exp, mask_ready, counted, more_ready,
         rows_ready, rows_hi, rows_lo,
         pick_ready, gathered, xe_hi_ready, xe_lo_ready, pick_transposed, pick_t_copied,
         y_hi_ready, y_lo_ready, scattered, added, stored) = (sem(n) for n in """
         hi_ready lo_ready unit_used
         x_landed p_landed rows_landed small_landed bc_landed consts_ready
         dve_chain pool_chain gains_transposed gains_ready
         p_transposed p_hi_ready p_lo_ready
         squares_ready mean_ready rstd_ready xs_ready xs_transposed xt_hi_ready xt_lo_ready
         resid_ready block_copied
         rope_g_ready qk_squares qk_mean qk_rstd qk_normed qk_half qk_rotated qk_transposed qk_t_copied
         lam_summed lam_exp lam_ready
         scores_ready shift_ready exp_ready probs_ready probs_transposed probs_t_copied
         av_ready av_copied
         o_squares o_mean o_rstd o_normed o_transposed o_hi_ready o_lo_ready
         silu_ready hidden_ready hidden_transposed ht_hi_ready ht_lo_ready sig_ready gated
         pool_x_ready pool_y pool_hi pool_lo pool_biased pool_scaled
         router_hi_ready router_lo_ready logits_ready gap_ready gap_exp mask_ready counted more_ready
         rows_ready rows_hi rows_lo
         pick_ready gathered xe_hi_ready xe_lo_ready pick_transposed pick_t_copied
         y_hi_ready y_lo_ready scattered added stored""".split())

        def raw_slot(u):
            return raw[:, u % RAW, :]

        def load_wait(eng, u, k=0):
            eng.wait_ge(landed[u % RAW], 16 * (u // RAW + 1) + 16 * (PER_EXPERT // RAW) * k)

        def split_hi(u, k=0):
            load_wait(nc.scalar, u, k)
            if u >= SPLIT:
                nc.scalar.wait_ge(unit_used, u - SPLIT + 1 + PER_EXPERT * k)
            nc.scalar.activation(w_hi[:, u % SPLIT, :], raw_slot(u), ACT.Copy).then_inc(hi_ready, 1)

        def split_lo(u, k=0):
            nc.vector.wait_ge(hi_ready, u + 1 + PER_EXPERT * k)
            nc.vector.tensor_tensor(w_lo[:, u % SPLIT, :], raw_slot(u), w_hi[:, u % SPLIT, :].bitcast(F32),
                                    ALU.subtract).then_inc(lo_ready, 1)

        def load(eng, u, view, k=0):
            if u >= RAW:
                eng.wait_ge(lo_ready, u - RAW + 1 + PER_EXPERT * k)
            dst = raw_slot(u).rearrange("p (c n) -> p c n", c=view.shape[1])
            eng.dma_start(dst, view).then_inc(landed[u % RAW], 16)

        def product(out, x, w, first, last):
            nc.tensor.matmul(out, x[0], w[0], start=first, stop=False)
            nc.tensor.matmul(out, x[0], w[1], start=False, stop=False)
            return nc.tensor.matmul(out, x[1], w[0], start=False, stop=last)

        def weights(u, c, n0, n, width):
            at = c * width + n0
            return w_hi[:, u % SPLIT, at:at + n], w_lo[:, u % SPLIT, at:at + n]

        def acts(c, tt):
            at = c * SEQ + tt * P
            return a_hi[:, at:at + P], a_lo[:, at:at + P]

        block = ctx.enter_context(nc.Block())

        @block.sync
        def _(sp):
            def chunks(w, c0, c, n0, n):
                return w.rearrange("(c p) n -> p c n", p=P)[:, c0:c0 + c, n0:n0 + n]

            sp.dma_start(resid[:, :, :], dram["x"][0].rearrange("(t p) d -> p t d", p=P)).then_inc(x_landed, 16)
            u = U_QKV
            for nb in range(6):
                for half in range(2):
                    load(sp, u, chunks(dram["attn_w_qkv"][0], 4 * half, 4, 512 * nb, 512))
                    u += 1
            for nb in range(2):
                for half in range(2):
                    load(sp, u, chunks(dram["attn_w_o"][0], 4 * half, 4, 512 * nb, 512))
                    u += 1
            wg, wu, wd = (dram[n][0] for n in ("ffn_w_gate", "ffn_w_up", "ffn_w_down"))
            for j in range(JF):
                for w in (wg, wu):
                    load(sp, u, chunks(w, 0, KD, 256 * j, 256))
                    u += 1
                if j:
                    load(sp, u, chunks(wd, 2 * (j - 1), 2, 0, D))
                    u += 1
            load(sp, u, chunks(wd, 2 * (JF - 1), 2, 0, D))
            u += 1

            def load_ple(layer, u, k=0):
                load(sp, u, chunks(dram["ple_w_proj"][layer], 0, 2, 0, D), k)
                for n in range(4):
                    load(sp, u + 1 + n, chunks(dram["ple_w_gate"][layer], 4 * (n % 2), 4, 512 * (n // 2), 512), k)

            load_ple(0, u)
            load(sp, U_POOL, dram["pool_w"][0].rearrange("g (c p) e -> p (g c) e", p=P))

            ge, ue, de = (dram[n][0] for n in ("moe_w_gate", "moe_w_up", "moe_w_down"))

            def expert_rows(w, e, c0, c, n0, n):
                m = w.rearrange("e (c p) n -> e p c n", p=P)[bass.ds(e, 1), :, c0:c0 + c, n0:n0 + n]
                return m.rearrange("a p c n -> (a p) c n")

            def load_expert(e, e_before, u, k, first=False):
                for f in range(FB):
                    for w in (ge, ue):
                        for half in range(2):
                            load(sp, u, expert_rows(w, e, 4 * half, 4, 512 * f, 512), k)
                            u += 1
                    if f or not first:
                        for half in range(2):
                            load(sp, u, expert_rows(de, e if f else e_before, 4 * ((f - 1) % FB) + 2 * half, 2, 0, D), k)
                            u += 1

            load_expert(0, None, U_MOE, 0, first=True)
            with sp.Fori(1, NE) as it:
                load_expert(it, it - 1, U_TURN, it - 1)
            sp.wait_ge(more_ready, 1)
            extra = sp.value_load(more[0:1, 0:1], min_val=0, max_val=NE)
            with sp.If(extra > 0):
                load_expert(0, NE - 1, U_TURN, NE - 1)
                with sp.Fori(1, NE) as it:
                    load_expert(it, it - 1, U_TURN, it + (NE - 1))
            turns = extra + (NE - 1)
            for half in range(2):
                load(sp, U_TURN + half, expert_rows(de, NE - 1, 4 * (FB - 1) + 2 * half, 2, 0, D), turns)
            load_ple(1, U_TURN + 2, turns)
            out = dram["out"][0].rearrange("(t p) d -> p t d", p=P)
            for n in range(4):
                half, tt = n // 2, n % 2
                sp.wait_ge(resid_ready, 4 * 4 + n + 1)
                cols = slice(512 * half, 512 * half + 512)
                sp.dma_start(out[:, tt, cols], resid[:, tt, cols]).then_inc(stored, 16)
            sp.wait_ge(stored, 64)

        def dense_group(j):
            return U_FFN if j == 0 else U_FFN - 1 + 3 * j

        def dense_down(j):
            return U_PLE0 - 1 if j == JF - 1 else dense_group(j + 1) + 2

        def turn_unit(t0, f):
            return U_TURN + PER_EXPERT * (t0 - 1) + 6 * f + (2 if t0 == 0 and f == 0 else 0)

        def norm_gain(n, c):
            at = ((n % 3) * 2 + n // 3) * KD + c
            return gains[:, at:at + 1]

        XT_OF = {0: 0, 1: 1, 2: 2, 4: 3, 5: 4}
        HEAD_TILES = TT * HEADS

        def keys_of(i):
            return P * (i // HEADS + 1)

        @block.tensor
        def _(pe):
            def unit(u, k=0):
                pe.wait_ge(lo_ready, u + 1 + PER_EXPERT * k)

            def transpose_norm(n):
                pe.wait_ge(xs_ready, 2 * (n + 1))
                for pair in range(4):
                    for c in (2 * pair, 2 * pair + 1):
                        for tt in range(TT):
                            at = (c % 2) * SEQ + tt * P
                            last = nc.tensor.transpose(ps[:, 4 + pair, at:at + P], xs[:, tt, c * P:(c + 1) * P],
                                                       ident[:, :])
                    last.then_inc(xs_transposed, 1)

            def block512(u, half, banks, k=0):
                unit(u, k)
                for tt in range(TT):
                    for c in range(4):
                        last = product(ps[:, banks[tt], :], acts(4 * half + c, tt), weights(u, c, 0, 512, 512),
                                       half == 0 and c == 0, half == 1 and c == 3)
                last.then_inc(unit_used, 1)

            def per_layer(layer, u, k=0):
                pe.wait_ge(xt_lo_ready, KD * (XT_OF[3 * layer + 2] + 1))
                unit(u, k)
                for tt in range(TT):
                    for half in range(2):
                        for c in range(2):
                            at = c * SEQ + tt * P
                            last = product(ps[:, 4 + 2 * tt + half, :],
                                           (p_t_hi[:, layer, at:at + P], p_t_lo[:, layer, at:at + P]),
                                           weights(u, c, 512 * half, 512, D), c == 0, c == 1)
                last.then_inc(unit_used, 1)
                for n in range(4):
                    block512(u + 1 + n, n % 2, (2 * (n // 2), 2 * (n // 2) + 1), k)

            pe.wait_ge(consts_ready, 1)
            pe.wait_ge(rows_landed, 64)
            nc.tensor.transpose(ps[:, 2, 0:6 * KD + 1], gain_rows, ident[0:6 * KD + 1, 0:6 * KD + 1]).then_inc(
                gains_transposed, 1)
            transpose_norm(0)
            pe.wait_ge(p_landed, 32)
            for layer in range(2):
                for c in range(2):
                    for tt in range(TT):
                        at = c * SEQ + tt * P
                        last = nc.tensor.transpose(ps[:, layer, at:at + P], p_sb[:, layer, tt, c * P:(c + 1) * P],
                                                   ident[:, :])
                last.then_inc(p_transposed, 1)

            pe.wait_ge(p_lo_ready, 2)
            for nb in range(6):
                if nb < 2:
                    pe.wait_ge(xt_lo_ready, KD)
                if nb >= 4:
                    pe.wait_ge(block_copied, 2 * (nb - 3))
                for half in range(2):
                    block512(U_QKV + 2 * nb + half, half, (2 * (nb % 4), 2 * (nb % 4) + 1))
                if nb >= 4:
                    s = nb - 4
                    pe.wait_ge(qk_rotated, 2 * (s + 1))
                    if s == 0:
                        pe.wait_ge(block_copied, 8)
                    for pair in range(4):
                        if s == 1:
                            pe.wait_ge(qk_t_copied, pair + 1)
                        for h in (2 * pair, 2 * pair + 1):
                            for tt in range(TT):
                                at = (h % 2) * SEQ + tt * P
                                last = nc.tensor.transpose(ps[:, 4 + pair, at:at + P],
                                                           qkv[:, tt, s * D + h * P:s * D + (h + 1) * P], ident[:, :])
                        last.then_inc(qk_transposed, 1)

            pe.wait_ge(block_copied, 12)
            pe.wait_ge(qk_t_copied, 8)
            for i in range(HEAD_TILES + 2):
                if i < HEAD_TILES:
                    qt, h, nk = i // HEADS, i % HEADS, keys_of(i)
                    if i >= 2:
                        pe.wait_ge(exp_ready, 2 * (i - 1))
                    for c in range(2):
                        bank, rows = 2 * (i % 2) + c, slice(DH * c, DH * c + DH)
                        nc.tensor.matmul(ps[:, bank, 0:nk], q_t[rows, h, qt * P:(qt + 1) * P],
                                         qkv[rows, 0:qt + 1, h * P:(h + 1) * P], start=True, stop=False)
                        last = nc.tensor.matmul(ps[:, bank, nk - P:nk], ident[:, :], causal[:, :],
                                                start=False, stop=True)
                    last.then_inc(scores_ready, 1)
                if 1 <= i <= HEAD_TILES:
                    j = i - 1
                    pe.wait_ge(probs_ready, j + 1)
                    if j >= 2:
                        pe.wait_ge(probs_t_copied, j - 1)
                    for kc in range(keys_of(j) // P):
                        last = nc.tensor.transpose(ps[:, 4 + j % 2, kc * P:(kc + 1) * P],
                                                   probs[:, j % 2, kc * P:(kc + 1) * P], ident[:, :])
                    last.then_inc(probs_transposed, 1)
                if i >= 2:
                    j = i - 2
                    h, nt = j % HEADS, keys_of(j) // P
                    pe.wait_ge(probs_t_copied, j + 1)
                    if j % 4 == 0 and j >= 8:
                        pe.wait_ge(av_copied, j // 4 - 1)
                    at = (j % 4) * P
                    for kc in range(nt):
                        last = nc.tensor.matmul(ps[:, 6 + (j // 4) % 2, at:at + P],
                                                probs_t[:, j % 2, kc * P:(kc + 1) * P],
                                                qkv[:, kc, 2 * D + h * P:2 * D + (h + 1) * P],
                                                start=kc == 0, stop=kc == nt - 1)
                    last.then_inc(av_ready, 1)

            pe.wait_ge(probs_t_copied, HEAD_TILES)
            pe.wait_ge(av_copied, 4)
            for tt in range(TT):
                pe.wait_ge(o_normed, tt + 1)
                for b in range(2):
                    for h in range(4 * b, 4 * b + 4):
                        at = (h % 4) * P
                        last = nc.tensor.transpose(ps[:, 4 + 2 * tt + b, at:at + P],
                                                   qkv[:, tt, D + h * P:D + (h + 1) * P], ident[:, :])
                    last.then_inc(o_transposed, 1)
            pe.wait_ge(o_lo_ready, 4)
            for n in range(4):
                block512(U_WO + n, n % 2, (2 * (n // 2), 2 * (n // 2) + 1))

            def transpose_hidden(g, k=0):
                pe.wait_ge(hidden_ready, g + 1 + FB * k)
                if g:
                    pe.wait_ge(ht_lo_ready, g + FB * k)
                for n in range(4):
                    src = (n % 2) * 256 + (n // 2) * P if g < JF else n * P
                    last = nc.tensor.transpose(ps[:, 2, n * P:(n + 1) * P], hidden[:, src:src + P], ident[:, :])
                last.then_inc(hidden_transposed, 1)

            def dense_in(j):
                for n, freed in ((0, silu_ready), (1, hidden_ready)):
                    u = dense_group(j) + n
                    unit(u)
                    if j:
                        pe.wait_ge(freed, j)
                    for tt in range(TT):
                        for c in range(KD):
                            last = product(ps[:, n, 256 * tt:256 * tt + 256], acts(c, tt), weights(u, c, 0, 256, 256),
                                           c == 0, c == KD - 1)
                    last.then_inc(unit_used, 1)

            def dense_out(j):
                u = dense_down(j)
                unit(u)
                pe.wait_ge(ht_lo_ready, j + 1)
                for tt in range(TT):
                    for half in range(2):
                        for c in range(2):
                            at = c * SEQ + tt * P
                            last = product(ps[:, 4 + 2 * tt + half, :], (h_t_hi[:, at:at + P], h_t_lo[:, at:at + P]),
                                           weights(u, c, 512 * half, 512, D), j == 0 and c == 0, j == JF - 1 and c == 1)
                last.then_inc(unit_used, 1)

            transpose_norm(1)
            pe.wait_ge(xt_lo_ready, 2 * KD)
            for j in range(JF):
                dense_in(j)
                if j:
                    dense_out(j - 1)
                transpose_hidden(j)
            dense_out(JF - 1)

            transpose_norm(2)
            per_layer(0, U_PLE0)

            transpose_norm(3)
            pe.wait_ge(pool_lo, 4)
            unit(U_POOL)
            for tt in range(TT):
                for g in range(4):
                    at = 256 * (g % 2)
                    for c in range(2):
                        last = product(ps[:, 2 * tt + g // 2, at:at + 256], acts(2 * g + c, tt),
                                       weights(U_POOL, 2 * g + c, 0, 256, 256), c == 0, c == 1)
            last.then_inc(unit_used, 1)

            transpose_norm(4)
            pe.wait_ge(xt_lo_ready, KD * (XT_OF[4] + 1))
            pe.wait_ge(router_lo_ready, 1)
            for tt in range(TT):
                for c in range(KD):
                    cols = slice(NE * c, NE * (c + 1))
                    last = product(ps[:, 0, NE * tt:NE * (tt + 1)], acts(c, tt),
                                   (router_hi[:, cols], router_lo[:, cols]), c == 0, c == KD - 1)
            last.then_inc(logits_ready, 1)
            pe.wait_ge(mask_ready, 1)
            nc.tensor.matmul(ps[:, 1, 0:8], before[:, :], mask[:, 0, :], start=True, stop=True)
            nc.tensor.matmul(ps[:, 1, 8:16], before[:, :], mask[:, 1, :], start=True, stop=False)
            nc.tensor.matmul(ps[:, 1, 8:16], ones[:, :], mask[:, 0, :], start=False, stop=True)
            nc.tensor.matmul(ps[:, 1, 16:24], ones[:, :], mask[:, 2, :], start=True, stop=True).then_inc(counted, 1)

            def gather(t0, k=0):
                pe.wait_ge(pick_ready, t0 + 1 + k)
                if t0 == 0:
                    pe.wait_ge(rows_lo, TT)
                if t0 >= 2:
                    pe.wait_ge(added, 4 * (t0 - 1 + k))
                for c in range(KD):
                    n = 0
                    for a in (a_hi, a_lo):
                        for tt in range(TT):
                            last = nc.tensor.matmul(ps[:, 5 + c // 4, (c % 4) * P:(c % 4 + 1) * P],
                                                    a[:, tt * D + c * P:tt * D + (c + 1) * P],
                                                    pick[:, tt * SLOTS:(tt + 1) * SLOTS], start=n == 0, stop=n == 3)
                            n += 1
                last.then_inc(gathered, 1)

            def scatter(q, t, k=0):
                pe.wait_ge(y_lo_ready, t + 1 + k)
                pe.wait_ge(pick_t_copied, t + 1 + k)
                if q < 2:
                    pe.wait_ge(xe_lo_ready, t + 2 + k)
                else:
                    pe.wait_ge(added, 4 * (t + k) + q - 1)
                tt, half = q // 2, q % 2
                for y, stop in ((y_hi, False), (y_lo, True)):
                    last = nc.tensor.matmul(ps[:, 5 + q % 2, :], pick_t[:, tt * P:(tt + 1) * P],
                                            y[:, 512 * half:512 * half + 512], start=not stop, stop=stop)
                last.then_inc(scattered, 1)

            def down(u, f, half, g, k=0):
                unit(u, k)
                pe.wait_ge(ht_lo_ready, g + 1 + FB * k)
                for n in range(2):
                    for c in range(2):
                        at = (2 * half + c) * P
                        last = product(ps[:, 3 + n, :], (h_t_hi[:, at:at + P], h_t_lo[:, at:at + P]),
                                       weights(u, c, 512 * n, 512, D), f == 0 and half == 0 and c == 0,
                                       f == FB - 1 and half == 1 and c == 1)
                last.then_inc(unit_used, 1)

            def turn(t0, k=0):
                pe.wait_ge(xe_lo_ready, t0 + 1 + k)
                for f in range(FB):
                    u, g = turn_unit(t0, f), JF + FB * t0 + f
                    for n, freed in ((0, silu_ready), (1, hidden_ready)):
                        for half in range(2):
                            unit(u, k)
                            if half == 0:
                                pe.wait_ge(freed, g + FB * k)
                            for c in range(4):
                                at = (4 * half + c) * P
                                last = product(ps[:, n, :], (xe_hi[:, at:at + P], xe_lo[:, at:at + P]),
                                               weights(u, c, 0, 512, 512), half == 0 and c == 0, half == 1 and c == 3)
                            last.then_inc(unit_used, 1)
                            u += 1
                    if f == 1 and t0:
                        scatter(0, t0 - 1, k)
                        scatter(1, t0 - 1, k)
                    if f == 2:
                        if t0:
                            pe.wait_ge(pick_t_copied, t0 + k)
                        for tt in range(TT):
                            last = nc.tensor.transpose(ps[:, 7, tt * P:(tt + 1) * P],
                                                       pick[:, tt * SLOTS:(tt + 1) * SLOTS].bitcast(F32), ident[:, :])
                        last.then_inc(pick_transposed, 1)
                    if f == FB - 1:
                        gather(t0 + 1, k)
                    if f or t0:
                        if f == 1 and t0:
                            pe.wait_ge(y_lo_ready, t0 + k)
                        for half in range(2):
                            down(u, (f - 1) % FB, half, g - 1, k)
                            u += 1
                    if f == 1 and t0:
                        scatter(2, t0 - 1, k)
                        scatter(3, t0 - 1, k)
                    transpose_hidden(g, k)

            gather(0)
            turn(0)
            pe.wait_ge(more_ready, 1)
            extra = pe.value_load(more[0:1, 0:1], min_val=0, max_val=NE)
            turns = extra + (NE - 1)
            with pe.Fori(1, turns + 1) as it:
                turn(1, it - 1)
            for half in range(2):
                down(U_TURN + half, FB - 1, half, JF + FB - 1, turns)
            for q in range(4):
                scatter(q, 0, turns)

            transpose_norm(5)
            per_layer(1, U_TURN + 2, turns)

        @block.scalar
        def _(act):
            def used(u, k=0):
                act.wait_ge(unit_used, u + 1 + PER_EXPERT * k)

            def square_norm(n):
                for tt in range(TT):
                    last = nc.scalar.activation(xs[:, tt, :], resid[:, tt, :], ACT.Square, accum_out=mean_sq[:, tt:tt + 1])
                last.then_inc(squares_ready, 1)

            def norm_hi(n):
                for c in range(KD):
                    if c % 2 == 0:
                        act.wait_ge(xs_transposed, 4 * n + c // 2 + 1)
                    nc.scalar.activation(a_hi[:, c * SEQ:(c + 1) * SEQ],
                                         ps[:, 4 + c // 2, (c % 2) * SEQ:(c % 2 + 1) * SEQ], ACT.Copy,
                                         scale=norm_gain(n, c)).then_inc(xt_hi_ready, 1)

            def sigmoids(layer, n, u, k=0):
                used(u, k)
                for tt in range(TT):
                    q = 2 * n + tt
                    if q >= 2:
                        act.wait_ge(resid_ready, 8 * (layer + 1) + q - 1)
                    nc.scalar.activation(sig[tt], ps[:, q, :], ACT.Sigmoid).then_inc(sig_ready, 1)

            for layer in range(2):
                act.dma_start(p_sb[:, layer], dram["p"][layer, 0].rearrange("(t p) n -> p t n", p=P)).then_inc(p_landed, 16)
            for n, name in enumerate(("norm_mix", "norm_ffn", "norm_ple")):
                act.dma_start(gain_rows[2 * KD * n:2 * KD * (n + 1), :],
                              dram[name].rearrange("l (c p) -> (l c) p", p=P)).then_inc(rows_landed, 16)
            act.dma_start(gain_rows[6 * KD:6 * KD + 1, :], dram["attn_subln"]).then_inc(rows_landed, 16)
            act.dma_start(rope[:, :, :, :], dram["rope"].rearrange("(t p) a n -> p t a n", p=P)).then_inc(small_landed, 16)
            for n, name in enumerate(("attn_q_norm", "attn_k_norm")):
                act.dma_start(qk_gain[:, n, :], dram[name][0].partition_broadcast(P)).then_inc(small_landed, 16)
            for n, name in enumerate(("attn_lambda_q1", "attn_lambda_k1", "attn_lambda_q2", "attn_lambda_k2")):
                act.dma_start(lam_in[:, n, :], dram[name][0].partition_broadcast(P)).then_inc(small_landed, 16)
            act.dma_start(router[:, :].rearrange("p (c e) -> p c e", c=KD),
                          dram["moe_router"][0].rearrange("(c p) e -> p c e", p=P)).then_inc(small_landed, 16)

            act.wait_ge(x_landed, 16)
            square_norm(0)
            act.wait_ge(gains_transposed, 1)
            nc.scalar.activation(gains[:, :], ps[:, 2, 0:6 * KD + 1], ACT.Copy).then_inc(gains_ready, 1)
            split_hi(0)
            split_hi(1)
            act.wait_ge(gains_ready, 1)
            norm_hi(0)
            for layer in range(2):
                act.wait_ge(p_transposed, layer + 1)
                nc.scalar.activation(p_t_hi[:, layer, :], ps[:, layer, :], ACT.Copy).then_inc(p_hi_ready, 1)
            act.wait_ge(small_landed, 128)
            nc.scalar.activation(router_hi[:, :], router[:, :], ACT.Copy).then_inc(router_hi_ready, 1)
            act.wait_ge(lam_summed, 1)
            nc.scalar.activation(lam_sum[:, :], lam_sum[:, :], ACT.Exp).then_inc(lam_exp, 1)

            for u in range(U_QKV, U_WO):
                split_hi(u + AHEAD)
                if u % 2 == 0:
                    continue
                nb = u // 2
                used(u)
                for tt in range(TT):
                    nc.scalar.activation(qkv[:, tt, 512 * nb:512 * nb + 512], ps[:, 2 * (nb % 4) + tt, :],
                                         ACT.Copy).then_inc(block_copied, 1)
                if nb in (1, 3):
                    s = nb // 2
                    act.wait_ge(block_copied, 4 * (s + 1))
                    for tt in range(TT):
                        m = 2 * s + tt
                        if m:
                            act.wait_ge(qk_mean, m)
                        else:
                            act.wait_ge(p_transposed, 2)
                        nc.scalar.activation(squares, qkv[:, tt, s * D:(s + 1) * D], ACT.Square).then_inc(qk_squares, 1)
                if nb >= 4:
                    s = nb - 4
                    if s == 0:
                        act.wait_ge(xs_transposed, 4)
                    for pair in range(4):
                        act.wait_ge(qk_transposed, 4 * s + pair + 1)
                        if s == 0:
                            dst = q_t[:, 2 * pair:2 * pair + 2, :].rearrange("p h (t s) -> p h t s", t=TT)
                        else:
                            dst = qkv[:, :, 2 * pair * P:(2 * pair + 2) * P].rearrange("p t (h s) -> p h t s", h=2)
                        src = ps[:, 4 + pair, :].rearrange("p (h t s) -> p h t s", h=2, t=TT)
                        nc.scalar.activation(dst, src, ACT.Copy).then_inc(qk_t_copied, 1)

            for i in range(HEAD_TILES + 2):
                if i < HEAD_TILES:
                    b, nk = i % 2, keys_of(i)
                    act.wait_ge(shift_ready, i + 1)
                    if i == 0:
                        act.wait_ge(qk_rotated, 4)
                    if i >= 2:
                        act.wait_ge(probs_transposed, i - 1)
                    for c in range(2):
                        nc.scalar.activation(probs[:, b, 256 * c:256 * c + nk], ps[:, 2 * b + c, 0:nk], ACT.Exp,
                                             bias=smax[:, b, 2 + c:3 + c], scale=SCALE,
                                             accum_out=esum[:, b, c:c + 1]).then_inc(exp_ready, 1)
                if 1 <= i <= HEAD_TILES:
                    j = i - 1
                    act.wait_ge(probs_transposed, j + 1)
                    if j >= 2:
                        act.wait_ge(av_ready, j - 1)
                    nc.scalar.activation(probs_t[:, j % 2, 0:keys_of(j)], ps[:, 4 + j % 2, 0:keys_of(j)],
                                         ACT.Copy).then_inc(probs_t_copied, 1)
                if i >= 2 and (i - 2) % 4 == 3:
                    m = (i - 2) // 4
                    act.wait_ge(av_ready, 4 * (m + 1))
                    at = D + 512 * (m % 2)
                    nc.scalar.activation(qkv[:, m // 2, at:at + 512], ps[:, 6 + m % 2, :], ACT.Copy).then_inc(av_copied, 1)
            act.wait_ge(av_copied, 4)
            for tt in range(TT):
                nc.scalar.activation(tmp[:, tt * D:(tt + 1) * D], qkv[:, tt, D:2 * D], ACT.Square).then_inc(o_squares, 1)
            a_hi_heads = a_hi[:, :].rearrange("p (h s) -> p h s", h=HEADS)
            for n in range(4):
                tt, b = n // 2, n % 2
                act.wait_ge(o_transposed, n + 1)
                nc.scalar.activation(a_hi_heads[:, 4 * b:4 * b + 4, tt * P:(tt + 1) * P],
                                     ps[:, 4 + n, :].rearrange("p (h s) -> p h s", h=4), ACT.Copy,
                                     scale=sub_gain[:, 0:1]).then_inc(o_hi_ready, 1)
            for u in range(U_WO, U_FFN):
                split_hi(u + AHEAD)

            def silus(g, u, k=0):
                used(u, k)
                if g:
                    act.wait_ge(hidden_ready, g + FB * k)
                nc.scalar.activation(silu, ps[:, 0, :], ACT.Silu).then_inc(silu_ready, 1)

            def hidden_hi(g, k=0):
                act.wait_ge(hidden_transposed, g + 1 + FB * k)
                nc.scalar.activation(h_t_hi[:, :], ps[:, 2, :], ACT.Copy).then_inc(ht_hi_ready, 1)

            act.wait_ge(resid_ready, 4)
            square_norm(1)
            norm_hi(1)
            for j in range(JF):
                u = dense_group(j)
                split_hi(u + AHEAD)
                silus(j, u)
                split_hi(u + 1 + AHEAD)
                if j:
                    split_hi(u + 2 + AHEAD)
                hidden_hi(j)
            split_hi(dense_down(JF - 1) + AHEAD)

            act.wait_ge(resid_ready, 8)
            square_norm(2)
            norm_hi(2)
            split_hi(U_PLE0 + AHEAD)
            for n in range(2):
                split_hi(U_PLE0 + 1 + 2 * n + AHEAD)
                split_hi(U_PLE0 + 2 + 2 * n + AHEAD)
                sigmoids(0, n, U_PLE0 + 2 + 2 * n)

            act.wait_ge(resid_ready, 12)
            square_norm(3)
            for c in range(KD):
                act.wait_ge(xs_transposed, 4 * 3 + c // 2 + 1)
                nc.scalar.activation(tmp[:, c * SEQ:(c + 1) * SEQ], ps[:, 4 + c // 2, (c % 2) * SEQ:(c % 2 + 1) * SEQ],
                                     ACT.Copy, scale=norm_gain(3, c)).then_inc(pool_x_ready, 1)
            for g in range(4):
                act.wait_ge(pool_y, g + 1)
                nc.scalar.activation(a_hi[:, 512 * g:512 * g + 512], sums[:, 512 * g:512 * g + 512],
                                     ACT.Copy).then_inc(pool_hi, 1)
            split_hi(U_POOL + AHEAD)

            act.wait_ge(resid_ready, 16)
            square_norm(4)
            norm_hi(4)
            act.wait_ge(gap_ready, 1)
            nc.scalar.activation(top_w[:, :, 1:2], top_w[:, :, 0:1], ACT.Exp).then_inc(gap_exp, 1)
            for tt in range(TT):
                act.wait_ge(rows_ready, tt + 1)
                act.wait_ge(logits_ready, 1)
                nc.scalar.activation(a_hi[:, tt * D:(tt + 1) * D], xs[:, tt, :], ACT.Copy).then_inc(rows_hi, 1)

            def tokens_hi(t, k=0):
                act.wait_ge(gathered, t + 1 + k)
                nc.scalar.activation(xe_hi[:, :].rearrange("p (b n) -> p b n", b=2), ps[:, 5:7, :],
                                     ACT.Copy).then_inc(xe_hi_ready, 1)

            def result_hi(u, k=0):
                used(u, k)
                nc.scalar.activation(y_hi[:, :].rearrange("p (b n) -> p b n", b=2), ps[:, 3:5, :],
                                     ACT.Copy).then_inc(y_hi_ready, 1)

            def turn(t0, k=0):
                for f in range(FB):
                    u, g = turn_unit(t0, f), JF + FB * t0 + f
                    split_hi(u + AHEAD, k)
                    split_hi(u + 1 + AHEAD, k)
                    silus(g, u + 1, k)
                    split_hi(u + 2 + AHEAD, k)
                    split_hi(u + 3 + AHEAD, k)
                    if f == FB - 1:
                        tokens_hi(t0 + 1, k)
                    if f or t0:
                        split_hi(u + 4 + AHEAD, k)
                        split_hi(u + 5 + AHEAD, k)
                    hidden_hi(g, k)
                    if f == 0 and t0:
                        result_hi(u + 5, k)

            tokens_hi(0)
            turn(0)
            act.wait_ge(more_ready, 1)
            extra = act.value_load(more[0:1, 0:1], min_val=0, max_val=NE)
            turns = extra + (NE - 1)
            with act.Fori(1, turns + 1) as it:
                turn(1, it - 1)
            split_hi(U_TURN + AHEAD, turns)
            split_hi(U_TURN + 1 + AHEAD, turns)
            result_hi(U_TURN + 1, turns)

            act.wait_ge(added, 4 * turns + 4)
            square_norm(5)
            norm_hi(5)
            split_hi(U_TURN + 2 + AHEAD, turns)
            for n in range(2):
                if n == 0:
                    split_hi(U_TURN + 3 + AHEAD, turns)
                    split_hi(U_TURN + 4 + AHEAD, turns)
                sigmoids(1, n, U_TURN + 4 + 2 * n, turns)

        @block.vector
        def _(dve):
            chain = [0]

            def then(ins):
                chain[0] += 1
                ins.then_inc(dve_chain, 1)
                dve.wait_ge(dve_chain, chain[0])

            def used(u, k=0):
                dve.wait_ge(unit_used, u + 1 + PER_EXPERT * k)

            def norm_rows(n):
                dve.wait_ge(squares_ready, n + 1)
                nc.vector.tensor_scalar(mean_sq[:, 0:TT], mean_sq[:, 0:TT], 1.0 / D, EPS, ALU.mult,
                                        ALU.add).then_inc(mean_ready, 1)
                dve.wait_ge(rstd_ready, n + 1)
                for tt in range(TT):
                    nc.vector.tensor_scalar(xs[:, tt, :], resid[:, tt, :], rstd[:, tt:tt + 1], None,
                                            ALU.mult).then_inc(xs_ready, 1)

            def norm_lo(n):
                for c in range(KD):
                    if c % 2 == 0:
                        dve.wait_ge(xt_hi_ready, KD * XT_OF[n] + c + 2)
                    cols = slice(c * SEQ, (c + 1) * SEQ)
                    nc.vector.scalar_tensor_tensor(out=a_lo[:, cols],
                                                   in0=ps[:, 4 + c // 2, (c % 2) * SEQ:(c % 2 + 1) * SEQ],
                                                   scalar=norm_gain(n, c), in1=a_hi[:, cols].bitcast(F32),
                                                   op0=ALU.mult, op1=ALU.subtract).then_inc(xt_lo_ready, 1)

            def mean_of(at, n, width):
                return nc.vector.tensor_scalar(mean_sq[:, at:at + n], mean_sq[:, at:at + n], 1.0 / width, EPS,
                                               ALU.mult, ALU.add)

            dve.wait_ge(x_landed, 16)
            norm_rows(0)
            split_lo(0)
            split_lo(1)
            dve.wait_ge(gains_ready, 1)
            norm_lo(0)
            for layer in range(2):
                dve.wait_ge(p_hi_ready, layer + 1)
                nc.vector.tensor_tensor(p_t_lo[:, layer, :], ps[:, layer, :], p_t_hi[:, layer, :].bitcast(F32),
                                        ALU.subtract).then_inc(p_lo_ready, 1)
            dve.wait_ge(small_landed, 128)
            dve.wait_ge(router_hi_ready, 1)
            nc.vector.tensor_tensor(router_lo[:, :], router[:, :], router_hi[:, :].bitcast(F32),
                                    ALU.subtract).then_inc(router_lo_ready, 1)
            nc.vector.tensor_tensor(lam_prod[:, 0, :], lam_in[:, 0, :], lam_in[:, 1, :], ALU.mult)
            then(nc.vector.tensor_tensor(lam_prod[:, 1, :], lam_in[:, 2, :], lam_in[:, 3, :], ALU.mult))
            nc.vector.tensor_reduce(lam_sum[:, :], lam_prod[:, :, :], AX_X, ALU.add).then_inc(lam_summed, 1)
            for s in range(2):
                for n, (angle, half) in enumerate(((0, 0), (1, 1), (0, 1), (1, 0))):
                    gain = qk_gain[:, s, half * 32:half * 32 + 32].unsqueeze(1).to_broadcast([P, TT, 32])
                    last = nc.vector.tensor_tensor(rope_g[:, s, :, n, :], rope[:, :, angle, :], gain, ALU.mult)
            last.then_inc(rope_g_ready, 1)
            nc.vector.tensor_scalar(sub_gain[:, :], gains[:, 6 * KD:6 * KD + 1], 1.0 - LAM_INIT, None, ALU.mult)
            then(nc.vector.reciprocal(inv_count[:, :], inv_count[:, :]))
            dve.wait_ge(lam_exp, 1)
            then(nc.vector.tensor_tensor(neg_lam[:, :], lam_sum[:, 1:2], lam_sum[:, 0:1], ALU.subtract))
            then(nc.vector.tensor_scalar(neg_lam[:, :], neg_lam[:, :], LAM_INIT, None, ALU.subtract))

            def rotate(m):
                s, tt = m // 2, m % 2
                x = qkv[:, tt, s * D:(s + 1) * D].rearrange("p (g d) -> p g d", g=SUB)
                x1, x2 = x[:, :, 0:32], x[:, :, 32:64]

                def factor(n):
                    return rope_g[:, s, tt, n, :].unsqueeze(1).to_broadcast([P, SUB, 32])

                at = 16 + SUB * m
                dve.wait_ge(qk_squares, m + 1)
                then(nc.vector.tensor_reduce(mean_sq[:, at:at + SUB], squares.rearrange("p (g d) -> p g d", g=SUB),
                                             AX_X, ALU.add))
                mean_of(at, SUB, DH).then_inc(qk_mean, 1)
                dve.wait_ge(qk_rstd, m + 1)
                nc.vector.tensor_tensor(x, x, rstd[:, at:at + SUB].unsqueeze(2).to_broadcast([P, SUB, DH]),
                                        ALU.mult).then_inc(qk_normed, 1)
                dve.wait_ge(qk_normed, m + 1)
                t = turned[0].rearrange("p (g d) -> p g d", g=SUB)
                t2 = turned[1].rearrange("p (g d) -> p g d", g=SUB)
                then(nc.vector.tensor_tensor(t, x2, factor(1), ALU.mult))
                dve.wait_ge(qk_half, m + 1)
                nc.vector.tensor_tensor(x1, x1, factor(0), ALU.mult)
                then(nc.vector.tensor_tensor(x2, x2, factor(2), ALU.mult))
                nc.vector.tensor_tensor(x1, x1, t, ALU.subtract)
                nc.vector.tensor_tensor(x2, x2, t2, ALU.add).then_inc(qk_rotated, 1)

            for u in range(U_QKV, U_WO):
                split_lo(u + AHEAD)
                if u in (3, 7):
                    for tt in range(TT):
                        rotate(2 * (u // 4) + tt)

            def softmax_end(j):
                b, nk = j % 2, keys_of(j)
                dve.wait_ge(exp_ready, 2 * (j + 1))
                then(nc.vector.reciprocal(esum[:, b, 2:4], esum[:, b, 0:2]))
                then(nc.vector.tensor_tensor(esum[:, b, 3:4], esum[:, b, 3:4], neg_lam[:, :], ALU.mult))
                second = probs[:, b, 256:256 + nk]
                then(nc.vector.tensor_scalar(second, second, esum[:, b, 3:4], None, ALU.mult))
                nc.vector.scalar_tensor_tensor(out=probs[:, b, 0:nk], in0=probs[:, b, 0:nk], scalar=esum[:, b, 2:3],
                                               in1=second, op0=ALU.mult, op1=ALU.add).then_inc(probs_ready, 1)

            for i in range(HEAD_TILES + 1):
                if i < HEAD_TILES:
                    b, nk = i % 2, keys_of(i)
                    dve.wait_ge(scores_ready, i + 1)
                    then(nc.vector.tensor_reduce(smax[:, b, 0:2], ps[:, 2 * b:2 * b + 2, 0:nk], AX_X, ALU.max))
                    nc.vector.tensor_scalar(smax[:, b, 2:4], smax[:, b, 0:2], -SCALE, None,
                                            ALU.mult).then_inc(shift_ready, 1)
                if i >= 1:
                    softmax_end(i - 1)

            for tt in range(TT):
                at = 80 + HEADS * tt
                dve.wait_ge(o_squares, tt + 1)
                then(nc.vector.tensor_reduce(mean_sq[:, at:at + HEADS],
                                             tmp[:, tt * D:(tt + 1) * D].rearrange("p (h d) -> p h d", h=HEADS),
                                             AX_X, ALU.add))
                mean_of(at, HEADS, 2 * DH).then_inc(o_mean, 1)
            for tt in range(TT):
                at = 80 + HEADS * tt
                dve.wait_ge(o_rstd, tt + 1)
                o = qkv[:, tt, D:2 * D].rearrange("p (h d) -> p h d", h=HEADS)
                nc.vector.tensor_tensor(o, o, rstd[:, at:at + HEADS].unsqueeze(2).to_broadcast([P, HEADS, 2 * DH]),
                                        ALU.mult).then_inc(o_normed, 1)
            for n in range(4):
                tt, b = n // 2, n % 2
                dve.wait_ge(o_hi_ready, n + 1)
                hi, lo = (a[:, :].rearrange("p (h s) -> p h s", h=HEADS)[:, 4 * b:4 * b + 4, tt * P:(tt + 1) * P]
                          for a in (a_hi, a_lo))
                nc.vector.scalar_tensor_tensor(out=lo, in0=ps[:, 4 + n, :].rearrange("p (h s) -> p h s", h=4),
                                               scalar=sub_gain[:, 0:1], in1=hi.bitcast(F32), op0=ALU.mult,
                                               op1=ALU.subtract).then_inc(o_lo_ready, 1)
            for u in range(U_WO, U_FFN):
                split_lo(u + AHEAD)
                if u % 2:
                    nb = (u - U_WO) // 2
                    used(u)
                    for tt in range(TT):
                        r = resid[:, tt, 512 * nb:512 * nb + 512]
                        nc.vector.tensor_tensor(r, r, ps[:, 2 * nb + tt, :], ALU.add).then_inc(resid_ready, 1)

            def hiddens(g, u, k=0):
                used(u, k)
                dve.wait_ge(silu_ready, g + 1 + FB * k)
                if g:
                    dve.wait_ge(hidden_transposed, g + FB * k)
                nc.vector.tensor_tensor(hidden, silu, ps[:, 1, :], ALU.mult).then_inc(hidden_ready, 1)

            def hidden_lo(g, k=0):
                dve.wait_ge(ht_hi_ready, g + 1 + FB * k)
                nc.vector.tensor_tensor(h_t_lo[:, :], ps[:, 2, :], h_t_hi[:, :].bitcast(F32),
                                        ALU.subtract).then_inc(ht_lo_ready, 1)

            norm_rows(1)
            norm_lo(1)
            for j in range(JF):
                u = dense_group(j)
                split_lo(u + AHEAD)
                split_lo(u + 1 + AHEAD)
                hiddens(j, u + 1)
                if j:
                    split_lo(u + 2 + AHEAD)
                hidden_lo(j)
            split_lo(dense_down(JF - 1) + AHEAD)
            used(dense_down(JF - 1))
            for tt in range(TT):
                for half in range(2):
                    r = resid[:, tt, 512 * half:512 * half + 512]
                    nc.vector.tensor_tensor(r, r, ps[:, 4 + 2 * tt + half, :], ALU.add).then_inc(resid_ready, 1)

            def gate_projection(layer, n):
                for tt in range(TT):
                    q = 4 * layer + 2 * n + tt
                    dve.wait_ge(sig_ready, q + 1)
                    nc.vector.tensor_tensor(sig[tt], sig[tt], ps[:, 4 + 2 * tt + n, :], ALU.mult).then_inc(gated, 1)

            norm_rows(2)
            norm_lo(2)
            split_lo(U_PLE0 + AHEAD)
            for n in range(2):
                split_lo(U_PLE0 + 1 + 2 * n + AHEAD)
                split_lo(U_PLE0 + 2 + 2 * n + AHEAD)
                gate_projection(0, n)

            norm_rows(3)
            for g in range(4):
                dve.wait_ge(pool_x_ready, 2 * (g + 1))
                x = tmp[:, 512 * g:512 * g + 512].rearrange("p (c s) -> p c s", c=2)
                total = sums[:, 512 * g:512 * g + 512].rearrange("p (c s) -> p c s", c=2)
                now = x
                for s in range(g + 1):
                    by = 1 << s
                    to = total if s == g else part[s % 2].rearrange("p (c s) -> p c s", c=2)
                    nc.vector.tensor_copy(to[:, :, 0:by], now[:, :, 0:by])
                    then(nc.vector.tensor_tensor(to[:, :, by:SEQ], now[:, :, by:SEQ], now[:, :, 0:SEQ - by], ALU.add))
                    now = to
                w = 2 << g
                counts = inv_count[:, 0:w].unsqueeze(1).to_broadcast([P, 2, w])
                nc.vector.scalar_tensor_tensor(out=total[:, :, w:SEQ], in0=total[:, :, w:SEQ], scalar=1.0 / w,
                                               in1=x[:, :, w:SEQ], op0=ALU.mult, op1=ALU.subtract)
                then(nc.vector.tensor_tensor(total[:, :, 0:w], total[:, :, 0:w], counts, ALU.mult))
                nc.vector.tensor_tensor(total[:, :, 0:w], total[:, :, 0:w], x[:, :, 0:w],
                                        ALU.subtract).then_inc(pool_y, 1)
            for g in range(4):
                cols = slice(512 * g, 512 * g + 512)
                dve.wait_ge(pool_hi, g + 1)
                nc.vector.tensor_tensor(a_lo[:, cols], sums[:, cols], a_hi[:, cols].bitcast(F32),
                                        ALU.subtract).then_inc(pool_lo, 1)
            split_lo(U_POOL + AHEAD)
            used(U_POOL)
            dve.wait_ge(bc_landed, 48)
            for q in range(4):
                half = slice(512 * (q % 2), 512 * (q % 2) + 512)
                nc.vector.tensor_tensor(sums[:, 512 * q:512 * q + 512], ps[:, q, :], bias_bc[:, half],
                                        ALU.add).then_inc(pool_biased, 1)

            norm_rows(4)
            norm_lo(4)
            for tt in range(TT):
                nc.vector.tensor_tensor(xs[:, tt, :], xs[:, tt, :], gain_bc, ALU.mult).then_inc(rows_ready, 1)

            dve.wait_ge(logits_ready, 1)
            then(nc.vector.tensor_copy(logits[:, :, :].rearrange("p t e -> p (t e)"), ps[:, 0, 0:TT * NE]))
            for tt in range(TT):
                then(nc.vector.max(top_v[:, tt, :], logits[:, tt, :]))
                then(nc.vector.max_index(top_i[:, tt, :], top_v[:, tt, :], logits[:, tt, :]))
            nc.vector.tensor_tensor(top_w[:, :, 0:1], top_v[:, :, 1:2], top_v[:, :, 0:1],
                                    ALU.subtract).then_inc(gap_ready, 1)
            then(nc.vector.tensor_copy(top_f[:, :, :], top_i[:, :, :]))
            for tt in range(TT):
                for n in range(2):
                    last = nc.vector.tensor_scalar(chose[:, tt, n, :], iota_expert[:, :], top_f[:, tt, n:n + 1], None,
                                                   ALU.is_equal)
            then(last)
            then(nc.vector.tensor_tensor(mask[:, 0:TT, :], chose[:, :, 0, :], chose[:, :, 1, :], ALU.add))
            nc.vector.tensor_tensor(mask[:, 2, :], mask[:, 0, :], mask[:, 1, :], ALU.add).then_inc(mask_ready, 1)
            dve.wait_ge(gap_exp, 1)
            then(nc.vector.tensor_scalar(top_w[:, :, 2:3], top_w[:, :, 1:2], 1.0, None, ALU.add))
            then(nc.vector.reciprocal(top_w[:, :, 2:3], top_w[:, :, 2:3]))
            then(nc.vector.tensor_tensor(top_w[:, :, 3:4], top_w[:, :, 1:2], top_w[:, :, 2:3], ALU.mult))
            for tt in range(TT):
                for at in (0, NE):
                    last = nc.vector.tensor_scalar(gate[:, tt, at:at + NE], chose[:, tt, 0, :], top_w[:, tt, 2:3], None,
                                                   ALU.mult)
            then(last)
            for tt in range(TT):
                for at in (0, NE):
                    last = nc.vector.scalar_tensor_tensor(out=gate[:, tt, at:at + NE], in0=chose[:, tt, 1, :],
                                                          scalar=top_w[:, tt, 3:4], in1=gate[:, tt, at:at + NE],
                                                          op0=ALU.mult, op1=ALU.add)
            then(last)
            dve.wait_ge(counted, 1)
            nc.vector.memset(place[:, :, 2 * NE:2 * NE + 1], -1.0)
            then(nc.vector.scalar_tensor_tensor(out=place[:, :, 0:NE],
                                                in0=ps[:, 1, 0:TT * NE].rearrange("p (t e) -> p t e", t=TT), scalar=1.0,
                                                in1=mask[:, 0:TT, :], op0=ALU.add, op1=ALU.mult))
            then(nc.vector.tensor_scalar(place[:, :, 0:NE], place[:, :, 0:NE], 1.0, None, ALU.subtract))
            then(nc.vector.tensor_scalar(place[:, :, NE:2 * NE], place[:, :, 0:NE], float(SLOTS), None, ALU.subtract))
            then(nc.vector.tensor_reduce(tokens[:, 0:1], ps[:, 1, 2 * NE:3 * NE], AX_X, ALU.max))
            nc.vector.tensor_scalar(more[:, :], tokens[:, 0:1], float(SLOTS), float(NE), ALU.is_gt,
                                    ALU.mult).then_inc(more_ready, 1)

            def picks(t, k=0):
                if t:
                    dve.wait_ge(pick_transposed, t + k)
                for tt in range(TT):
                    last = nc.vector.tensor_scalar(pick[:, tt * SLOTS:(tt + 1) * SLOTS], iota_slot[:, :],
                                                   place[:, tt, bass.ds(t + k, 1)], None, ALU.is_equal)
                last.then_inc(pick_ready, 1)

            def tokens_lo(t, k=0):
                dve.wait_ge(xe_hi_ready, t + 1 + k)
                nc.vector.tensor_tensor(xe_lo[:, :].rearrange("p (b n) -> p b n", b=2), ps[:, 5:7, :],
                                        xe_hi[:, :].bitcast(F32).rearrange("p (b n) -> p b n", b=2),
                                        ALU.subtract).then_inc(xe_lo_ready, 1)

            def result_lo(t, k=0):
                dve.wait_ge(y_hi_ready, t + 1 + k)
                nc.vector.tensor_tensor(y_lo[:, :].rearrange("p (b n) -> p b n", b=2), ps[:, 3:5, :],
                                        y_hi[:, :].bitcast(F32).rearrange("p (b n) -> p b n", b=2),
                                        ALU.subtract).then_inc(y_lo_ready, 1)

            def add_result(q, t, k=0):
                tt, half = q // 2, q % 2
                dve.wait_ge(scattered, 4 * (t + k) + q + 1)
                r = resid[:, tt, 512 * half:512 * half + 512]
                nc.vector.scalar_tensor_tensor(out=r, in0=ps[:, 5 + q % 2, :], scalar=gate[:, tt, bass.ds(t + k, 1)],
                                               in1=r, op0=ALU.mult, op1=ALU.add).then_inc(added, 1)

            picks(0)
            for tt in range(TT):
                dve.wait_ge(rows_hi, tt + 1)
                nc.vector.tensor_tensor(a_lo[:, tt * D:(tt + 1) * D], xs[:, tt, :],
                                        a_hi[:, tt * D:(tt + 1) * D].bitcast(F32), ALU.subtract).then_inc(rows_lo, 1)
            tokens_lo(0)

            def turn(t0, k=0):
                for f in range(FB):
                    u, g = turn_unit(t0, f), JF + FB * t0 + f
                    for n in range(4):
                        split_lo(u + n + AHEAD, k)
                    hiddens(g, u + 3, k)
                    if f == 1 and t0:
                        add_result(0, t0 - 1, k)
                        add_result(1, t0 - 1, k)
                    if f == 2:
                        dve.wait_ge(pick_transposed, t0 + 1 + k)
                        nc.vector.tensor_copy(pick_t[:, :], ps[:, 7, 0:TT * P]).then_inc(pick_t_copied, 1)
                    if f == 3:
                        picks(t0 + 1, k)
                    if f == FB - 1:
                        tokens_lo(t0 + 1, k)
                    if f or t0:
                        split_lo(u + 4 + AHEAD, k)
                        split_lo(u + 5 + AHEAD, k)
                    if f == 1 and t0:
                        add_result(2, t0 - 1, k)
                        add_result(3, t0 - 1, k)
                    hidden_lo(g, k)
                    if f == 0 and t0:
                        result_lo(t0 - 1, k)

            turn(0)
            extra = dve.value_load(more[0:1, 0:1], min_val=0, max_val=NE)
            turns = extra + (NE - 1)
            with dve.Fori(1, turns + 1) as it:
                turn(1, it - 1)
            split_lo(U_TURN + AHEAD, turns)
            split_lo(U_TURN + 1 + AHEAD, turns)
            result_lo(0, turns)
            for q in range(4):
                add_result(q, 0, turns)

            norm_rows(5)
            norm_lo(5)
            split_lo(U_TURN + 2 + AHEAD, turns)
            for n in range(2):
                if n == 0:
                    split_lo(U_TURN + 3 + AHEAD, turns)
                    split_lo(U_TURN + 4 + AHEAD, turns)
                gate_projection(1, n)

        @block.gpsimd
        def _(pool):
            chain = [0]

            def then(ins):
                chain[0] += 1
                ins.then_inc(pool_chain, 1)
                pool.wait_ge(pool_chain, chain[0])

            nc.gpsimd.memset(minus_half[:, :], -0.5)
            nc.gpsimd.memset(ones[:, :], 1.0)
            nc.gpsimd.memset(causal[:, :], 0.0)
            then(nc.gpsimd.memset(ident[:, :], 0.0))
            nc.gpsimd.affine_select(out=ident[:, :], in_=ident[:, :], compare_op=ALU.not_equal, fill=1.0, base=0,
                                    pattern=[[-1, P]], channel_multiplier=1)
            nc.gpsimd.affine_select(out=causal[:, :], in_=causal[:, :], compare_op=ALU.is_ge, fill=MASKED, base=0,
                                    pattern=[[-1, P]], channel_multiplier=1)
            nc.gpsimd.affine_select(out=before[:, :], in_=ones[:, :], compare_op=ALU.is_gt, fill=0.0, base=0,
                                    pattern=[[1, P]], channel_multiplier=-1)
            nc.gpsimd.iota(iota_slot[:, :], pattern=[[1, SLOTS]], base=0, channel_multiplier=0,
                           allow_small_or_imprecise_dtypes=True)
            nc.gpsimd.iota(inv_count[:, :], pattern=[[1, 16]], base=1, channel_multiplier=0,
                           allow_small_or_imprecise_dtypes=True)
            nc.gpsimd.iota(iota_expert[:, :], pattern=[[1, NE]], base=0, channel_multiplier=0,
                           allow_small_or_imprecise_dtypes=True).then_inc(consts_ready, 1)
            pool.wait_ge(consts_ready, 1)

            def root(at, n):
                return nc.gpsimd.tensor_tensor(rstd[:, at:at + n], mean_sq[:, at:at + n], minus_half[:, 0:n], ALU.pow)

            def norm_root(n):
                pool.wait_ge(mean_ready, n + 1)
                root(0, TT).then_inc(rstd_ready, 1)

            def add_gated(layer, k=0):
                for q in range(4):
                    n, tt = q // 2, q % 2
                    pool.wait_ge(gated, 4 * layer + q + 1)
                    r = resid[:, tt, 512 * n:512 * n + 512]
                    nc.gpsimd.tensor_tensor(r, r, sig[tt], ALU.add).then_inc(resid_ready, 1)

            norm_root(0)
            for m in range(4):
                s, tt = m // 2, m % 2
                pool.wait_ge(qk_mean, m + 1)
                root(16 + SUB * m, SUB).then_inc(qk_rstd, 1)
                pool.wait_ge(qk_normed, m + 1)
                if m == 0:
                    pool.wait_ge(rope_g_ready, 1)
                else:
                    pool.wait_ge(qk_rotated, m)
                x1 = qkv[:, tt, s * D:(s + 1) * D].rearrange("p (g d) -> p g d", g=SUB)[:, :, 0:32]
                nc.gpsimd.tensor_tensor(turned[1].rearrange("p (g d) -> p g d", g=SUB), x1,
                                        rope_g[:, s, tt, 3, :].unsqueeze(1).to_broadcast([P, SUB, 32]),
                                        ALU.mult).then_inc(qk_half, 1)
            for tt in range(TT):
                pool.wait_ge(o_mean, tt + 1)
                root(80 + HEADS * tt, HEADS).then_inc(o_rstd, 1)
            pool.wait_ge(o_transposed, 4)
            pool.dma_start(gain_bc, dram["norm_ffn"][1].partition_broadcast(P)).then_inc(bc_landed, 16)
            pool.dma_start(bias_bc, dram["pool_b"][0].rearrange("g e -> (g e)").partition_broadcast(P)).then_inc(bc_landed, 16)
            pool.dma_start(scale_bc, dram["pool_scale"][0].partition_broadcast(P)).then_inc(bc_landed, 16)
            norm_root(1)
            norm_root(2)
            add_gated(0)
            norm_root(3)
            pool.wait_ge(bc_landed, 48)
            for q in range(4):
                tt, half = q // 2, q % 2
                pool.wait_ge(pool_biased, q + 1)
                t = sums[:, 512 * q:512 * q + 512]
                then(nc.gpsimd.tensor_tensor(t, t, scale_bc[:, 512 * half:512 * half + 512], ALU.mult))
                r = resid[:, tt, 512 * half:512 * half + 512]
                nc.gpsimd.tensor_tensor(r, r, t, ALU.add).then_inc(resid_ready, 1)
            norm_root(4)
            norm_root(5)
            add_gated(1)


_INS = ["x", "p", "norm_mix", "norm_ffn", "norm_ple", "attn_w_qkv", "attn_w_o", "attn_q_norm", "attn_k_norm",
        "attn_lambda_q1", "attn_lambda_k1", "attn_lambda_q2", "attn_lambda_k2", "attn_subln", "pool_w", "pool_b",
        "pool_scale", "ffn_w_gate", "ffn_w_up", "ffn_w_down", "moe_router", "moe_w_gate", "moe_w_up", "moe_w_down",
        "ple_w_proj", "ple_w_gate"]


def kernel(**inputs):
    import numpy as np
    import concourse.bacc as bacc
    from concourse.bass_utils import run_bass_kernel_spmd

    nc = bacc.Bacc("TRN2", target_bir_lowering=False, num_devices=1)
    inv = (1.0 / (np.float32(10000.0) ** (np.arange(0, DH, 2, dtype=np.float32) / np.float32(DH)))).astype(np.float32)
    angle = np.arange(SEQ, dtype=np.float32)[:, None] * inv[None, :]
    arrays = {"in_rope_dram": np.stack([np.cos(angle), np.sin(angle)], axis=1).astype(np.float32)}
    for name in _INS:
        arrays[f"in_{name}_dram"] = np.ascontiguousarray(inputs[name])
    dram = {}
    for key, a in arrays.items():
        dram[key[3:-5]] = nc.dram_tensor(key, a.shape, mybir.dt.from_np(a.dtype), kind="ExternalInput").ap()
    dram["out"] = nc.dram_tensor("out_0_dram", (1, SEQ, D), F32, kind="ExternalOutput").ap()
    trunk(nc, dram)
    r = run_bass_kernel_spmd(nc, [arrays], core_ids=[0])
    return r.results[0]["out_0_dram"]
```

```python
from contextlib import ExitStack

import concourse.bass as bass
from concourse import mybir

F32 = mybir.dt.float32
F32R = mybir.dt.float32r
I32 = mybir.dt.int32
U32 = mybir.dt.uint32
ALU = mybir.AluOpType
ACT = mybir.ActivationFunctionType
AX_X = mybir.AxisListType.X

P = 128
SEQ = 256
TT = SEQ // P
D = 1024
KD = D // P
DH = 64
HEADS = D // (2 * DH)
SUB = 2 * HEADS
NE = 8
FF = 2816
FE = 3584
PLE = 256
EPS = 1e-6
LAM_INIT = 0.2
SCALE = DH ** -0.5
MASKED = -1e30

UNIT = 2048
RAW = 7
SPLIT = 3
AHEAD = 2

U_QKV = 0
U_WO = 12
U_FFN = 16
JF = FF // 256
U_PLE0 = U_FFN + 3 * JF
U_POOL = U_PLE0 + 5
U_MOE = U_POOL + 1
FB = FE // 512
PER_EXPERT = 6 * FB
U_TURN = U_MOE + PER_EXPERT - 2
SLOTS = P


def trunk(nc, dram):
    ctx = ExitStack()
    with ctx:
        def sb(name, shape, dt=F32):
            return ctx.enter_context(nc.sbuf_tensor(name, shape, dt))

        def sem(name):
            return ctx.enter_context(nc.semaphore(name))

        raw = sb("raw", [P, RAW, UNIT])
        w_hi = sb("w_hi", [P, SPLIT, UNIT], F32R)
        w_lo = sb("w_lo", [P, SPLIT, UNIT], F32R)
        resid = sb("resid", [P, TT, D])
        xs = sb("xs", [P, TT, D])
        a_hi = sb("a_hi", [P, UNIT], F32R)
        a_lo = sb("a_lo", [P, UNIT], F32R)
        wide = sb("wide", [P, 6144])
        h_t_hi = sb("h_t_hi", [P, 512], F32R)
        h_t_lo = sb("h_t_lo", [P, 512], F32R)
        xe_hi = sb("xe_hi", [P, D], F32R)
        xe_lo = sb("xe_lo", [P, D], F32R)
        y_hi = sb("y_hi", [P, D], F32R)
        y_lo = sb("y_lo", [P, D], F32R)
        tmp = sb("tmp", [P, UNIT])
        p_t_hi = sb("p_t_hi", [P, 2, 512], F32R)
        p_t_lo = sb("p_t_lo", [P, 2, 512], F32R)
        ident = sb("ident", [P, P])
        ones = sb("ones", [P, P])
        before = sb("before", [P, P])
        causal = sb("causal", [P, P])
        iota_slot = sb("iota_slot", [P, SLOTS])
        iota_expert = sb("iota_expert", [P, NE])
        rope = sb("rope", [P, TT, 2, DH // 2])
        qk_gain = sb("qk_gain", [P, 2, DH])
        rope_g = sb("rope_g", [P, 2, TT, 4, DH // 2])
        lam_sum = sb("lam_sum", [P, 2])
        neg_lam = sb("neg_lam", [P, 1])
        sub_gain = sb("sub_gain", [P, 1])
        minus_half = sb("minus_half", [P, 16])
        mean_sq = sb("mean_sq", [P, 96])
        rstd = sb("rstd", [P, 96])
        smax = sb("smax", [P, 3, 4])
        esum = sb("esum", [P, 3, 4])
        inv_count = sb("inv_count", [P, 16])
        router = sb("router", [P, KD * NE])
        router_hi = sb("router_hi", [P, KD * NE + P - NE], F32R)
        router_lo = sb("router_lo", [P, KD * NE + P - NE], F32R)
        logits = sb("logits", [P, TT, NE])
        top_v = sb("top_v", [P, TT, 8])
        top_i = sb("top_i", [P, TT, 8], U32)
        top_f = sb("top_f", [P, TT, 8])
        top_w = sb("top_w", [P, TT, 4])
        chose = sb("chose", [P, TT, 2, NE])
        mask = sb("mask", [P, 3, NE])
        gate = sb("gate", [P, TT, 2 * NE])
        place = sb("place", [P, TT, 2 * NE + 1])
        tokens = sb("tokens", [P, NE])
        more = sb("more", [P, 1], I32)
        pick = sb("pick", [P, TT * SLOTS], F32R)
        pick_t = sb("pick_t", [P, TT * P], F32R)
        ps = ctx.enter_context(nc.psum_tensor("ps", [P, 8, 512], F32))

        qkv = wide[:, :].rearrange("p (t n) -> p t n", t=TT)
        q_t = xs[:, :, :].rearrange("p t n -> p (t n)").rearrange("p (h s) -> p h s", h=HEADS)
        gain_bc = [wide[:, 0:D], wide[:, D:2 * D]]
        scale_bc = wide[:, 2 * D:3 * D]
        bias_row = wide[0:1, 3 * D:4 * D]
        scaled = wide[:, 4 * D:6 * D]
        band_hi = xe_hi[:, :].rearrange("p (g s) -> p g s", g=4)
        band_own = xe_lo[:, 0:512].rearrange("p (g s) -> p g s", g=4)
        band_lo = xe_lo[:, 512:576].rearrange("p (g s) -> p g s", g=4)
        p_sb = tmp[:, 0:D].rearrange("p (l t n) -> p l t n", l=2, t=TT)
        lam_in = tmp[:, D + P:D + P + 4 * DH].rearrange("p (a d) -> p a d", a=4)
        lam_prod = tmp[:, D + P + 4 * DH:D + P + 6 * DH].rearrange("p (a d) -> p a d", a=2)
        band = tmp[:, 3 * 512:3 * 512 + SEQ]
        squares = tmp[:, 0:D]
        turned = [tmp[:, D:D + 512], tmp[:, D + 512:2 * D]]
        probs = tmp[:, 0:3 * 512].rearrange("p (b n) -> p b n", b=3)
        probs_t = tmp[:, 3 * 512:4 * 512].rearrange("p (b n) -> p b n", b=2)
        logits_t = tmp[0:NE, 0:SEQ]
        hidden = tmp[:, 0:512]
        silu = tmp[:, 512:1024]
        sig = [tmp[:, 1024:1536], tmp[:, 1536:2048]]

        landed = [sem(f"landed{i}") for i in range(RAW)]
        (hi_ready, lo_ready, unit_used,
         x_landed, p_landed, gain_landed0, gain_landed1, small_landed, scale_landed, bias_landed, consts_ready,
         dve_chain, pool_chain, tile0_used, counts_inverted, bands_ready,
         p_transposed, p_hi_ready, p_lo_ready,
         squares_ready, mean_ready, rstd_ready, xs_ready, xs_transposed, xt_hi_ready, xt_lo_ready,
         resid_ready, block_copied,
         rope_g_ready, qk_squares, qk_mean, qk_rstd, qk_normed, qk_half, qk_rotated, qk_transposed, qk_t_copied,
         lam_summed, lam_exp, lam_ready,
         first_scores, scores_ready, shift_ready, exp_ready, probs_ready, probs_transposed, probs_t_copied,
         av_ready, av_copied,
         o_squares, o_mean, o_rstd, o_normed, o_transposed, o_hi_ready, o_lo_ready,
         silu_ready, hidden_ready, hidden_transposed, ht_hi_ready, ht_lo_ready, sig_ready, projected,
         pooled, pool_hi, pool_lo,
         router_hi_ready, router_lo_ready, routed, logits_t_ready, logits_ready, gap_ready, gap_exp, mask_ready, counted, more_ready,
         rows_hi, rows_lo,
         pick_ready, gathered, xe_hi_ready, xe_lo_ready, pick_transposed, pick_t_copied,
         y_hi_ready, y_lo_ready, scattered, added, stored) = (sem(n) for n in """
         hi_ready lo_ready unit_used
         x_landed p_landed gain_landed0 gain_landed1 small_landed scale_landed bias_landed consts_ready
         dve_chain pool_chain tile0_used counts_inverted bands_ready
         p_transposed p_hi_ready p_lo_ready
         squares_ready mean_ready rstd_ready xs_ready xs_transposed xt_hi_ready xt_lo_ready
         resid_ready block_copied
         rope_g_ready qk_squares qk_mean qk_rstd qk_normed qk_half qk_rotated qk_transposed qk_t_copied
         lam_summed lam_exp lam_ready
         first_scores scores_ready shift_ready exp_ready probs_ready probs_transposed probs_t_copied
         av_ready av_copied
         o_squares o_mean o_rstd o_normed o_transposed o_hi_ready o_lo_ready
         silu_ready hidden_ready hidden_transposed ht_hi_ready ht_lo_ready sig_ready projected
         pooled pool_hi pool_lo
         router_hi_ready router_lo_ready routed logits_t_ready logits_ready gap_ready gap_exp mask_ready counted more_ready
         rows_hi rows_lo
         pick_ready gathered xe_hi_ready xe_lo_ready pick_transposed pick_t_copied
         y_hi_ready y_lo_ready scattered added stored""".split())

        gain_landed = [gain_landed0, gain_landed1]

        def raw_slot(u):
            return raw[:, u % RAW, :]

        def load_wait(eng, u, k=0):
            eng.wait_ge(landed[u % RAW], 16 * (u // RAW + 1) + 16 * (PER_EXPERT // RAW) * k)

        def split_hi(u, k=0):
            load_wait(nc.scalar, u, k)
            if u >= SPLIT:
                nc.scalar.wait_ge(unit_used, u - SPLIT + 1 + PER_EXPERT * k)
            nc.scalar.activation(w_hi[:, u % SPLIT, :], raw_slot(u), ACT.Copy).then_inc(hi_ready, 1)

        def split_lo(u, k=0):
            nc.vector.wait_ge(hi_ready, u + 1 + PER_EXPERT * k)
            nc.vector.tensor_tensor(w_lo[:, u % SPLIT, :], raw_slot(u), w_hi[:, u % SPLIT, :].bitcast(F32),
                                    ALU.subtract).then_inc(lo_ready, 1)

        def load(eng, u, view, k=0):
            if u >= RAW:
                eng.wait_ge(lo_ready, u - RAW + 1 + PER_EXPERT * k)
            dst = raw_slot(u).rearrange("p (c n) -> p c n", c=view.shape[1])
            eng.dma_start(dst, view).then_inc(landed[u % RAW], 16)

        def product(out, x, w, first, last):
            nc.tensor.matmul(out, x[0], w[0], start=first, stop=False)
            nc.tensor.matmul(out, x[0], w[1], start=False, stop=False)
            return nc.tensor.matmul(out, x[1], w[0], start=False, stop=last)

        def weights(u, c, n0, n, width):
            at = c * width + n0
            return w_hi[:, u % SPLIT, at:at + n], w_lo[:, u % SPLIT, at:at + n]

        def acts(c, tt):
            at = c * SEQ + tt * P
            return a_hi[:, at:at + P], a_lo[:, at:at + P]

        block = ctx.enter_context(nc.Block())

        @block.sync
        def _(sp):
            def chunks(w, c0, c, n0, n):
                return w.rearrange("(c p) n -> p c n", p=P)[:, c0:c0 + c, n0:n0 + n]

            sp.dma_start(resid[:, :, :], dram["x"][0].rearrange("(t p) d -> p t d", p=P)).then_inc(x_landed, 16)
            sp.dma_start(gain_bc[0], dram["norm_mix"][0].partition_broadcast(P)).then_inc(gain_landed0, 16)
            u = U_QKV
            for nb in range(6):
                for half in range(2):
                    load(sp, u, chunks(dram["attn_w_qkv"][0], 4 * half, 4, 512 * nb, 512))
                    u += 1

            def load_gain(n):
                if n >= 3:
                    sp.wait_ge(xs_ready, 4 * (n - 1))
                name = ("norm_mix", "norm_ffn", "norm_ple")[n % 3]
                sp.dma_start(gain_bc[n % 2], dram[name][n // 3].partition_broadcast(P)).then_inc(gain_landed[n % 2], 16)

            for nb in range(2):
                for half in range(2):
                    load(sp, u, chunks(dram["attn_w_o"][0], 4 * half, 4, 512 * nb, 512))
                    u += 1
            wg, wu, wd = (dram[n][0] for n in ("ffn_w_gate", "ffn_w_up", "ffn_w_down"))
            for j in range(JF):
                if j == 2:
                    sp.wait_ge(o_transposed, 4)
                    load_gain(1)
                    load_gain(2)
                    sp.dma_start(scale_bc, dram["pool_scale"][0].partition_broadcast(P)).then_inc(scale_landed, 16)
                    sp.dma_start(bias_row, dram["pool_b"][0].rearrange("g e -> (g e)").unsqueeze(0)).then_inc(bias_landed, 16)
                if j == 5:
                    load_gain(3)
                for w in (wg, wu):
                    load(sp, u, chunks(w, 0, KD, 256 * j, 256))
                    u += 1
                if j:
                    load(sp, u, chunks(wd, 2 * (j - 1), 2, 0, D))
                    u += 1
            load(sp, u, chunks(wd, 2 * (JF - 1), 2, 0, D))
            u += 1

            def load_ple(layer, u, k=0):
                load(sp, u, chunks(dram["ple_w_proj"][layer], 0, 2, 0, D), k)
                for n in range(4):
                    load(sp, u + 1 + n, chunks(dram["ple_w_gate"][layer], 4 * (n % 2), 4, 512 * (n // 2), 512), k)

            load_ple(0, u)
            load(sp, U_POOL, dram["pool_w"][0].rearrange("g (c p) e -> p (g c) e", p=P))

            ge, ue, de = (dram[n][0] for n in ("moe_w_gate", "moe_w_up", "moe_w_down"))

            def expert_rows(w, e, c0, c, n0, n):
                m = w.rearrange("e (c p) n -> e p c n", p=P)[bass.ds(e, 1), :, c0:c0 + c, n0:n0 + n]
                return m.rearrange("a p c n -> (a p) c n")

            def load_expert(e, e_before, u, k, first=False):
                for f in range(FB):
                    if first and f in (1, 2):
                        load_gain(3 + f)
                    for w in (ge, ue):
                        for half in range(2):
                            load(sp, u, expert_rows(w, e, 4 * half, 4, 512 * f, 512), k)
                            u += 1
                    if f or not first:
                        for half in range(2):
                            load(sp, u, expert_rows(de, e if f else e_before, 4 * ((f - 1) % FB) + 2 * half, 2, 0, D), k)
                            u += 1

            load_expert(0, None, U_MOE, 0, first=True)
            with sp.Fori(1, NE) as it:
                load_expert(it, it - 1, U_TURN, it - 1)
            sp.wait_ge(more_ready, 1)
            extra = sp.value_load(more[0:1, 0:1], min_val=0, max_val=NE)
            with sp.If(extra > 0):
                load_expert(0, NE - 1, U_TURN, NE - 1)
                with sp.Fori(1, NE) as it:
                    load_expert(it, it - 1, U_TURN, it + (NE - 1))
            turns = extra + (NE - 1)
            for half in range(2):
                load(sp, U_TURN + half, expert_rows(de, NE - 1, 4 * (FB - 1) + 2 * half, 2, 0, D), turns)
            load_ple(1, U_TURN + 2, turns)
            out = dram["out"][0].rearrange("(t p) d -> p t d", p=P)
            for n in range(4):
                half, tt = n // 2, n % 2
                sp.wait_ge(resid_ready, 4 * 4 + n + 1)
                cols = slice(512 * half, 512 * half + 512)
                sp.dma_start(out[:, tt, cols], resid[:, tt, cols]).then_inc(stored, 16)
            sp.wait_ge(stored, 64)

        def dense_group(j):
            return U_FFN if j == 0 else U_FFN - 1 + 3 * j

        def dense_down(j):
            return U_PLE0 - 1 if j == JF - 1 else dense_group(j + 1) + 2

        def turn_unit(t0, f):
            return U_TURN + PER_EXPERT * (t0 - 1) + 6 * f + (2 if t0 == 0 and f == 0 else 0)

        XT_OF = {0: 0, 1: 1, 2: 2, 4: 3, 5: 4}
        NORM_BANKS = {n: (3, 4, 5, 6) if n == 5 else (4, 5, 6, 7) for n in XT_OF}
        PROJ_BANKS = ((0, 1, 2, 3), (0, 1, 2, 7))
        GATE_BANKS = ((4, 5, 6, 7), (3, 4, 5, 6))
        BUFS = 3

        RESID_TILE = {1: (3, 4), 2: (2, 4), 3: (3, 4), 4: (2, 4)}
        xs_flat = xs[:, :, :].rearrange("p t n -> p (t n)")

        def quarter(a, tt, b):
            return a[:, :].rearrange("p (c s) -> p c s", c=KD)[:, 4 * b:4 * b + 4, tt * P:(tt + 1) * P]

        def bank4(bank):
            return ps[:, bank, :].rearrange("p (c s) -> p c s", c=4)

        def pool_half(y, a, g):
            return (y if g < 2 else a)[:, 512 * (g % 2):512 * (g % 2) + 512]

        HEAD_TILES = TT * HEADS

        def keys_of(i):
            return P * (i // HEADS + 1)

        @block.tensor
        def _(pe):
            def unit(u, k=0):
                pe.wait_ge(lo_ready, u + 1 + PER_EXPERT * k)

            def transpose_norm(n):
                k = XT_OF[n]
                for q in range(4):
                    tt, b = q // 2, q % 2
                    pe.wait_ge(xs_ready, 4 * n + q + 1)
                    for c in range(4):
                        last = nc.tensor.transpose(ps[:, NORM_BANKS[n][q], c * P:(c + 1) * P],
                                                   xs[:, tt, (4 * b + c) * P:(4 * b + c + 1) * P], ident[:, :])
                    last.then_inc(xs_transposed, 1)

            def block512(u, half, banks, k=0, norm=None, early=False):
                unit(u, k)
                for tt in range(TT):
                    if norm is not None:
                        pe.wait_ge(xt_lo_ready, 4 * XT_OF[norm] + 2 * tt + half + 1)
                    for c in range(4):
                        last = product(ps[:, banks[tt], :], acts(4 * half + c, tt), weights(u, c, 0, 512, 512),
                                       half == 0 and c == 0, half == 1 and c == 3)
                    if early and tt == 0:
                        last.then_inc(tile0_used, 1)
                last.then_inc(unit_used, 1)

            def project(layer, tt, u):
                for half in range(2):
                    for c in range(2):
                        at = c * SEQ + tt * P
                        last = product(ps[:, PROJ_BANKS[layer][2 * tt + half], :],
                                       (p_t_hi[:, layer, at:at + P], p_t_lo[:, layer, at:at + P]),
                                       weights(u, c, 512 * half, 512, D), c == 0, c == 1)
                return last

            def gates(layer, u, k=0):
                for n in range(4):
                    half = n // 2
                    block512(u + n, n % 2, GATE_BANKS[layer][2 * half:2 * half + 2], k,
                             norm=3 * layer + 2 if n < 2 else None, early=n == 3)

            pe.wait_ge(consts_ready, 1)
            transpose_norm(0)
            for nb in range(6):
                if nb == 2:
                    pe.wait_ge(xt_lo_ready, 4)
                if nb >= 4:
                    pe.wait_ge(block_copied, 2 * (nb - 3))
                for half in range(2):
                    block512(U_QKV + 2 * nb + half, half, (2 * (nb % 4), 2 * (nb % 4) + 1), norm=0 if nb == 0 else None)
                if nb == 2:
                    pe.wait_ge(p_landed, 32)
                    for layer in range(2):
                        for c in range(2):
                            for tt in range(TT):
                                at = c * SEQ + tt * P
                                last = nc.tensor.transpose(ps[:, 6 + layer, at:at + P],
                                                           p_sb[:, layer, tt, c * P:(c + 1) * P], ident[:, :])
                        last.then_inc(p_transposed, 1)
                    pe.wait_ge(p_lo_ready, 2)
            for s in range(2):
                pe.wait_ge(qk_rotated, 2 * (s + 1))
                pe.wait_ge(block_copied, 8)
                for pair in range(4):
                    if s == 1:
                        pe.wait_ge(qk_t_copied, pair + 1)
                    for h in (2 * pair, 2 * pair + 1):
                        for tt in range(TT):
                            at = (h % 2) * SEQ + tt * P
                            last = nc.tensor.transpose(ps[:, 4 + pair, at:at + P],
                                                       qkv[:, tt, s * D + h * P:s * D + (h + 1) * P], ident[:, :])
                    last.then_inc(qk_transposed, 1)

            def score(i, c):
                qt, h, nk = i // HEADS, i % HEADS, keys_of(i)
                at, rows = 256 * c, slice(DH * c, DH * c + DH)
                nc.tensor.matmul(ps[:, i % BUFS, at:at + nk], q_t[rows, h, qt * P:(qt + 1) * P],
                                 qkv[rows, 0:qt + 1, h * P:(h + 1) * P], start=True, stop=False)
                return nc.tensor.matmul(ps[:, i % BUFS, at + nk - P:at + nk], ident[:, :], causal[:, :],
                                        start=False, stop=True)

            pe.wait_ge(block_copied, 12)
            pe.wait_ge(qk_t_copied, 8)
            for i in range(HEAD_TILES + 6):
                if i < HEAD_TILES:
                    if i >= BUFS:
                        pe.wait_ge(exp_ready, 2 * (i - BUFS + 1))
                    score(i, 0).then_inc(first_scores, 1)
                if 2 <= i < HEAD_TILES + 2:
                    j = i - 2
                    pe.wait_ge(probs_ready, j + 1)
                    if j >= 2:
                        pe.wait_ge(probs_t_copied, j - 1)
                    for kc in range(keys_of(j) // P):
                        last = nc.tensor.transpose(ps[:, 4 + j % 2, kc * P:(kc + 1) * P],
                                                   probs[:, j % BUFS, kc * P:(kc + 1) * P], ident[:, :])
                    last.then_inc(probs_transposed, 1)
                if i < HEAD_TILES:
                    pe.wait_ge(first_scores, i + 1)
                    score(i, 1).then_inc(scores_ready, 1)
                if 3 <= i < HEAD_TILES + 3:
                    j = i - 3
                    h, nt = j % HEADS, keys_of(j) // P
                    pe.wait_ge(probs_t_copied, j + 1)
                    if j % 4 == 0 and j >= 8:
                        pe.wait_ge(o_squares, 4 * (j // 4 - 1))
                    at = (j % 4) * P
                    for kc in range(nt):
                        last = nc.tensor.matmul(ps[:, 6 + (j // 4) % 2, at:at + P],
                                                probs_t[:, j % 2, kc * P:(kc + 1) * P],
                                                qkv[:, kc, 2 * D + h * P:2 * D + (h + 1) * P],
                                                start=kc == 0, stop=kc == nt - 1)
                    last.then_inc(av_ready, 1)
                if i >= 9 and (i - 9) % 4 == 0:
                    m = (i - 9) // 4
                    pe.wait_ge(o_normed, m + 1)
                    if m:
                        pe.wait_ge(o_lo_ready, m)
                    tt = m // 2
                    for h in range(4 * (m % 2), 4 * (m % 2) + 4):
                        last = nc.tensor.transpose(ps[:, 3, (h % 4) * P:(h % 4 + 1) * P],
                                                   qkv[:, tt, D + h * P:D + (h + 1) * P], ident[:, :])
                    last.then_inc(o_transposed, 1)
            pe.wait_ge(o_lo_ready, 4)
            for n in range(4):
                half = n // 2
                block512(U_WO + n, n % 2, (4 + 2 * half, 5 + 2 * half), early=n == 3)

            def transpose_hidden(g, k=0):
                pe.wait_ge(hidden_ready, g + 1 + FB * k)
                if g:
                    pe.wait_ge(ht_lo_ready, g + FB * k)
                for n in range(4):
                    src = (n % 2) * 256 + (n // 2) * P if g < JF else n * P
                    last = nc.tensor.transpose(ps[:, 2, n * P:(n + 1) * P], hidden[:, src:src + P], ident[:, :])
                last.then_inc(hidden_transposed, 1)

            def dense_in(j):
                for n, freed in ((0, silu_ready), (1, hidden_ready)):
                    u = dense_group(j) + n
                    unit(u)
                    if j:
                        pe.wait_ge(freed, j)
                    for tt in range(TT):
                        for c in range(KD):
                            if j == 0 and n == 0 and c % 4 == 0:
                                pe.wait_ge(xt_lo_ready, 4 * XT_OF[1] + 2 * tt + c // 4 + 1)
                            last = product(ps[:, n, 256 * tt:256 * tt + 256], acts(c, tt), weights(u, c, 0, 256, 256),
                                           c == 0, c == KD - 1)
                    last.then_inc(unit_used, 1)

            def dense_out(j):
                u = dense_down(j)
                unit(u)
                pe.wait_ge(ht_lo_ready, j + 1)
                for tt in range(TT):
                    for half in range(2):
                        for c in range(2):
                            at = c * SEQ + tt * P
                            last = product(ps[:, 4 + 2 * tt + half, :], (h_t_hi[:, at:at + P], h_t_lo[:, at:at + P]),
                                           weights(u, c, 512 * half, 512, D), j == 0 and c == 0, j == JF - 1 and c == 1)
                    if j == JF - 1 and tt == 0:
                        last.then_inc(tile0_used, 1)
                last.then_inc(unit_used, 1)

            transpose_norm(1)
            for j in range(JF):
                dense_in(j)
                if j:
                    dense_out(j - 1)
                transpose_hidden(j)
            dense_out(JF - 1)

            pe.wait_ge(p_lo_ready, 2)
            unit(U_PLE0)
            project(0, 0, U_PLE0)
            project(0, 1, U_PLE0).then_inc(unit_used, 1)
            transpose_norm(2)
            gates(0, U_PLE0 + 1)

            pe.wait_ge(bias_landed, 16)
            pe.wait_ge(resid_ready, 12)
            for q in range(4):
                cols = slice(512 * (q % 2), 512 * (q % 2) + 512)
                nc.tensor.matmul(ps[:, q, :], ones[0:1, :], bias_row[:, cols], start=True, stop=False)
            pe.wait_ge(bands_ready, 1)
            pe.wait_ge(rows_lo, 4)
            for g in range(4):
                for c in (2 * g, 2 * g + 1):
                    at = SEQ * (c % 2)
                    first, own = slice(c * P, (c + 1) * P), slice(D + c * P, D + (c + 1) * P)
                    nc.tensor.matmul(ps[:, 4 + g, at:at + SEQ], a_hi[:, first], band_hi[:, g, :], start=True, stop=False)
                    nc.tensor.matmul(ps[:, 4 + g, at:at + SEQ], a_lo[:, first], band_hi[:, g, :], start=False, stop=False)
                    nc.tensor.matmul(ps[:, 4 + g, at:at + 16], a_hi[:, first], band_lo[:, g, :], start=False, stop=False)
                    nc.tensor.matmul(ps[:, 4 + g, at + P:at + SEQ], a_hi[:, own], band_own[:, g, :], start=False, stop=False)
                    last = nc.tensor.matmul(ps[:, 4 + g, at + P:at + SEQ], a_lo[:, own], band_own[:, g, :],
                                            start=False, stop=True)
                last.then_inc(pooled, 1)
            unit(U_POOL)
            for tt in range(TT):
                for g in range(4):
                    if tt == 0:
                        pe.wait_ge(pool_lo, g + 1)
                    at = 256 * (g % 2)
                    x = (y_hi, y_lo) if g < 2 else (a_hi, a_lo)
                    for c in range(2):
                        xc = slice((2 * (g % 2) + c) * SEQ + tt * P, (2 * (g % 2) + c) * SEQ + (tt + 1) * P)
                        last = product(ps[:, 2 * tt + g // 2, at:at + 256], (x[0][:, xc], x[1][:, xc]),
                                       weights(U_POOL, 2 * g + c, 0, 256, 256), False, g % 2 == 1 and c == 1)
                if tt == 0:
                    last.then_inc(tile0_used, 1)
            last.then_inc(unit_used, 1)

            transpose_norm(4)
            pe.wait_ge(router_lo_ready, 1)
            for b in range(2):
                for tt in range(TT):
                    pe.wait_ge(xt_lo_ready, 4 * XT_OF[4] + 2 * tt + b + 1)
                for c in range(4 * b, 4 * b + 4):
                    x = a_hi[:, c * SEQ:(c + 1) * SEQ], a_lo[:, c * SEQ:(c + 1) * SEQ]
                    r = slice(NE * c, NE * c + P)
                    nc.tensor.matmul(ps[:, 0, 0:SEQ], router_hi[:, r], x[0], start=c == 0, stop=False)
                    nc.tensor.matmul(ps[:, 0, 0:SEQ], router_hi[:, r], x[1], start=False, stop=False)
                    last = nc.tensor.matmul(ps[:, 0, 0:SEQ], router_lo[:, r], x[0], start=False, stop=c == KD - 1)
            last.then_inc(routed, 1)
            pe.wait_ge(logits_t_ready, 1)
            for tt in range(TT):
                last = nc.tensor.transpose(ps[:, 2, NE * tt:NE * (tt + 1)], logits_t[:, tt * P:(tt + 1) * P],
                                           ident[0:NE, 0:NE])
            last.then_inc(logits_ready, 1)
            pe.wait_ge(mask_ready, 1)
            nc.tensor.matmul(ps[:, 1, 0:8], before[:, :], mask[:, 0, :], start=True, stop=True)
            nc.tensor.matmul(ps[:, 1, 8:16], before[:, :], mask[:, 1, :], start=True, stop=False)
            nc.tensor.matmul(ps[:, 1, 8:16], ones[:, :], mask[:, 0, :], start=False, stop=True)
            nc.tensor.matmul(ps[:, 1, 16:24], ones[:, :], mask[:, 2, :], start=True, stop=True).then_inc(counted, 1)

            def gather(t0, k=0):
                pe.wait_ge(pick_ready, t0 + 1 + k)
                if t0 == 0:
                    pe.wait_ge(rows_lo, 8)
                if t0 >= 2:
                    pe.wait_ge(added, 4 * (t0 - 1 + k))
                for c in range(KD):
                    n = 0
                    for a in (a_hi, a_lo):
                        for tt in range(TT):
                            last = nc.tensor.matmul(ps[:, 5 + c // 4, (c % 4) * P:(c % 4 + 1) * P],
                                                    a[:, tt * D + c * P:tt * D + (c + 1) * P],
                                                    pick[:, tt * SLOTS:(tt + 1) * SLOTS], start=n == 0, stop=n == 3)
                            n += 1
                last.then_inc(gathered, 1)

            def scatter(q, t, k=0):
                pe.wait_ge(y_lo_ready, t + 1 + k)
                pe.wait_ge(pick_t_copied, t + 1 + k)
                if q < 2:
                    pe.wait_ge(xe_lo_ready, t + 2 + k)
                else:
                    pe.wait_ge(added, 4 * (t + k) + q - 1)
                tt, half = q // 2, q % 2
                for y, stop in ((y_hi, False), (y_lo, True)):
                    last = nc.tensor.matmul(ps[:, 5 + q % 2, :], pick_t[:, tt * P:(tt + 1) * P],
                                            y[:, 512 * half:512 * half + 512], start=not stop, stop=stop)
                last.then_inc(scattered, 1)

            def down(u, f, half, g, k=0):
                unit(u, k)
                pe.wait_ge(ht_lo_ready, g + 1 + FB * k)
                for n in range(2):
                    for c in range(2):
                        at = (2 * half + c) * P
                        last = product(ps[:, 3 + n, :], (h_t_hi[:, at:at + P], h_t_lo[:, at:at + P]),
                                       weights(u, c, 512 * n, 512, D), f == 0 and half == 0 and c == 0,
                                       f == FB - 1 and half == 1 and c == 1)
                last.then_inc(unit_used, 1)

            def turn(t0, k=0):
                pe.wait_ge(xe_lo_ready, t0 + 1 + k)
                for f in range(FB):
                    u, g = turn_unit(t0, f), JF + FB * t0 + f
                    for n, freed in ((0, silu_ready), (1, hidden_ready)):
                        for half in range(2):
                            unit(u, k)
                            if half == 0:
                                pe.wait_ge(freed, g + FB * k)
                            for c in range(4):
                                at = (4 * half + c) * P
                                last = product(ps[:, n, :], (xe_hi[:, at:at + P], xe_lo[:, at:at + P]),
                                               weights(u, c, 0, 512, 512), half == 0 and c == 0, half == 1 and c == 3)
                            last.then_inc(unit_used, 1)
                            u += 1
                    if f == 1 and t0:
                        scatter(0, t0 - 1, k)
                        scatter(1, t0 - 1, k)
                    if f == 2:
                        if t0:
                            pe.wait_ge(pick_t_copied, t0 + k)
                        for tt in range(TT):
                            last = nc.tensor.transpose(ps[:, 7, tt * P:(tt + 1) * P],
                                                       pick[:, tt * SLOTS:(tt + 1) * SLOTS].bitcast(F32), ident[:, :])
                        last.then_inc(pick_transposed, 1)
                    if f == FB - 1:
                        gather(t0 + 1, k)
                    if f or t0:
                        if f == 1 and t0:
                            pe.wait_ge(y_lo_ready, t0 + k)
                        for half in range(2):
                            down(u, (f - 1) % FB, half, g - 1, k)
                            u += 1
                    if f == 1 and t0:
                        scatter(2, t0 - 1, k)
                        scatter(3, t0 - 1, k)
                    transpose_hidden(g, k)

            gather(0)
            turn(0)
            pe.wait_ge(more_ready, 1)
            extra = pe.value_load(more[0:1, 0:1], min_val=0, max_val=NE)
            turns = extra + (NE - 1)
            with pe.Fori(1, turns + 1) as it:
                turn(1, it - 1)
            for half in range(2):
                down(U_TURN + half, FB - 1, half, JF + FB - 1, turns)
            unit(U_TURN + 2, turns)
            pe.wait_ge(pick_t_copied, turns + 1)
            project(1, 0, U_TURN + 2)
            for q in range(4):
                scatter(q, 0, turns)
            project(1, 1, U_TURN + 2).then_inc(unit_used, 1)
            transpose_norm(5)
            gates(1, U_TURN + 3, turns)

        @block.scalar
        def _(act):
            def used(u, k=0):
                act.wait_ge(unit_used, u + 1 + PER_EXPERT * k)

            def square_norm(n, tiles=range(TT)):
                for tt in tiles:
                    if 1 <= n <= 4:
                        act.wait_ge(resid_ready, 4 * (n - 1) + RESID_TILE[n][tt])
                    nc.scalar.activation(xs[:, tt, :], resid[:, tt, :], ACT.Square,
                                         accum_out=mean_sq[:, tt:tt + 1]).then_inc(squares_ready, 1)

            def transposed_hi(n):
                for q in range(4):
                    tt, b = q // 2, q % 2
                    act.wait_ge(xs_transposed, 4 * XT_OF[n] + q + 1)
                    nc.scalar.activation(quarter(a_hi, tt, b), bank4(NORM_BANKS[n][q]), ACT.Copy).then_inc(xt_hi_ready, 1)

            def sigmoids(layer, n, u, k=0):
                for tt in range(TT):
                    q = 2 * n + tt
                    if n == 1 and tt == 0:
                        act.wait_ge(tile0_used, 3 if layer == 0 else 5)
                    else:
                        used(u, k)
                    if q >= 2:
                        act.wait_ge(resid_ready, 8 * (layer + 1) + q - 1)
                    nc.scalar.activation(sig[tt], ps[:, GATE_BANKS[layer][q], :], ACT.Sigmoid).then_inc(sig_ready, 1)

            act.wait_ge(x_landed, 16)
            square_norm(0)
            split_hi(0)
            transposed_hi(0)
            split_hi(1)

            for u in range(U_QKV, U_WO):
                split_hi(u + AHEAD)
                if u % 2 == 0:
                    continue
                nb = u // 2
                used(u)
                for tt in range(TT):
                    nc.scalar.activation(qkv[:, tt, 512 * nb:512 * nb + 512], ps[:, 2 * (nb % 4) + tt, :],
                                         ACT.Copy).then_inc(block_copied, 1)
                if nb == 2:
                    for layer in range(2):
                        act.wait_ge(p_transposed, layer + 1)
                        nc.scalar.activation(p_t_hi[:, layer, :], ps[:, 6 + layer, :], ACT.Copy).then_inc(p_hi_ready, 1)
                    act.wait_ge(small_landed, 144)
                    nc.scalar.activation(router_hi[:, 0:KD * NE], router[:, :], ACT.Copy).then_inc(router_hi_ready, 1)
                    act.wait_ge(lam_summed, 1)
                    nc.scalar.activation(lam_sum[:, :], lam_sum[:, :], ACT.Exp).then_inc(lam_exp, 1)
                for m in ((0, 1) if nb == 2 else (2, 3) if nb == 3 else ()):
                    s, tt = m // 2, m % 2
                    act.wait_ge(block_copied, 4 * (s + 1))
                    if m:
                        act.wait_ge(qk_mean, m)
                    nc.scalar.activation(squares, qkv[:, tt, s * D:(s + 1) * D], ACT.Square).then_inc(qk_squares, 1)
            for n in range(8):
                s, pair = n // 4, n % 4
                act.wait_ge(qk_transposed, n + 1)
                if s == 0:
                    dst = q_t[:, 2 * pair:2 * pair + 2, :].rearrange("p h (t s) -> p h t s", t=TT)
                else:
                    dst = qkv[:, :, 2 * pair * P:(2 * pair + 2) * P].rearrange("p t (h s) -> p h t s", h=2)
                src = ps[:, 4 + pair, :].rearrange("p (h t s) -> p h t s", h=2, t=TT)
                nc.scalar.activation(dst, src, ACT.Copy).then_inc(qk_t_copied, 1)

            for i in range(HEAD_TILES + 7):
                if i < HEAD_TILES:
                    b, nk = i % BUFS, keys_of(i)
                    act.wait_ge(shift_ready, i + 1)
                    if i == 0:
                        act.wait_ge(qk_rotated, 4)
                    if i >= BUFS:
                        act.wait_ge(probs_transposed, i - BUFS + 1)
                    for c in range(2):
                        nc.scalar.activation(probs[:, b, 256 * c:256 * c + nk], ps[:, b, 256 * c:256 * c + nk], ACT.Exp,
                                             bias=smax[:, b, 2 + c:3 + c], scale=SCALE,
                                             accum_out=esum[:, b, c:c + 1]).then_inc(exp_ready, 1)
                if 2 <= i < HEAD_TILES + 2:
                    j = i - 2
                    act.wait_ge(probs_transposed, j + 1)
                    if j >= 2:
                        act.wait_ge(av_ready, j - 1)
                    nc.scalar.activation(probs_t[:, j % 2, 0:keys_of(j)], ps[:, 4 + j % 2, 0:keys_of(j)],
                                         ACT.Copy).then_inc(probs_t_copied, 1)
                if 6 <= i < HEAD_TILES + 3 and (i - 3) % 4 == 3:
                    m = (i - 3) // 4
                    act.wait_ge(av_ready, 4 * (m + 1))
                    at = D + 512 * (m % 2)
                    nc.scalar.activation(qkv[:, m // 2, at:at + 512], ps[:, 6 + m % 2, :], ACT.Copy).then_inc(av_copied, 1)
                    for h in range(4):
                        nc.scalar.activation(y_hi[:, h * P:(h + 1) * P], ps[:, 6 + m % 2, h * P:(h + 1) * P], ACT.Square,
                                             accum_out=mean_sq[:, 80 + 4 * m + h:81 + 4 * m + h]).then_inc(o_squares, 1)
                if i >= 10 and (i - 10) % 4 == 0:
                    m = (i - 10) // 4
                    act.wait_ge(o_transposed, m + 1)
                    nc.scalar.activation(quarter(a_hi, m // 2, m % 2), bank4(3), ACT.Copy,
                                         scale=sub_gain[:, 0:1]).then_inc(o_hi_ready, 1)
            for u in range(U_WO, U_FFN):
                split_hi(u + AHEAD)

            def silus(g, u, k=0):
                used(u, k)
                if g:
                    act.wait_ge(hidden_ready, g + FB * k)
                nc.scalar.activation(silu, ps[:, 0, :], ACT.Silu).then_inc(silu_ready, 1)

            def hidden_hi(g, k=0):
                act.wait_ge(hidden_transposed, g + 1 + FB * k)
                nc.scalar.activation(h_t_hi[:, :], ps[:, 2, :], ACT.Copy).then_inc(ht_hi_ready, 1)

            square_norm(1)
            transposed_hi(1)
            for j in range(JF):
                u = dense_group(j)
                split_hi(u + AHEAD)
                silus(j, u)
                split_hi(u + 1 + AHEAD)
                if j:
                    split_hi(u + 2 + AHEAD)
                hidden_hi(j)
            split_hi(dense_down(JF - 1) + AHEAD)

            square_norm(2)
            split_hi(U_PLE0 + AHEAD)
            transposed_hi(2)
            for n in range(2):
                split_hi(U_PLE0 + 1 + 2 * n + AHEAD)
                split_hi(U_PLE0 + 2 + 2 * n + AHEAD)
                sigmoids(0, n, U_PLE0 + 2 + 2 * n)

            square_norm(3)
            for q in range(4):
                act.wait_ge(xs_ready, 4 * 3 + q + 1)
                nc.scalar.activation(a_hi[:, 512 * q:512 * q + 512], xs_flat[:, 512 * q:512 * q + 512],
                                     ACT.Copy).then_inc(rows_hi, 1)
            for g in range(4):
                act.wait_ge(pooled, g + 1 if g < 2 else 4)
                nc.scalar.activation(pool_half(y_hi, a_hi, g), ps[:, 4 + g, :], ACT.Copy).then_inc(pool_hi, 1)
            split_hi(U_POOL + AHEAD)

            square_norm(4)
            transposed_hi(4)
            act.wait_ge(routed, 1)
            nc.scalar.activation(logits_t, ps[0:NE, 0, 0:SEQ], ACT.Copy).then_inc(logits_t_ready, 1)
            for q in range(4):
                nc.scalar.activation(a_hi[:, 512 * q:512 * q + 512], xs_flat[:, 512 * q:512 * q + 512],
                                     ACT.Copy).then_inc(rows_hi, 1)
            act.wait_ge(gap_ready, 1)
            nc.scalar.activation(top_w[:, :, 1:2], top_w[:, :, 0:1], ACT.Exp).then_inc(gap_exp, 1)

            def tokens_hi(t, k=0):
                act.wait_ge(gathered, t + 1 + k)
                nc.scalar.activation(xe_hi[:, :].rearrange("p (b n) -> p b n", b=2), ps[:, 5:7, :],
                                     ACT.Copy).then_inc(xe_hi_ready, 1)

            def result_hi(u, k=0):
                used(u, k)
                nc.scalar.activation(y_hi[:, :].rearrange("p (b n) -> p b n", b=2), ps[:, 3:5, :],
                                     ACT.Copy).then_inc(y_hi_ready, 1)

            def turn(t0, k=0):
                for f in range(FB):
                    u, g = turn_unit(t0, f), JF + FB * t0 + f
                    split_hi(u + AHEAD, k)
                    split_hi(u + 1 + AHEAD, k)
                    silus(g, u + 1, k)
                    split_hi(u + 2 + AHEAD, k)
                    split_hi(u + 3 + AHEAD, k)
                    if f == FB - 1:
                        tokens_hi(t0 + 1, k)
                    if f or t0:
                        split_hi(u + 4 + AHEAD, k)
                        split_hi(u + 5 + AHEAD, k)
                    hidden_hi(g, k)
                    if f == 0 and t0:
                        result_hi(u + 5, k)

            tokens_hi(0)
            turn(0)
            act.wait_ge(more_ready, 1)
            extra = act.value_load(more[0:1, 0:1], min_val=0, max_val=NE)
            turns = extra + (NE - 1)
            with act.Fori(1, turns + 1) as it:
                turn(1, it - 1)
            split_hi(U_TURN + AHEAD, turns)
            split_hi(U_TURN + 1 + AHEAD, turns)
            result_hi(U_TURN + 1, turns)

            split_hi(U_TURN + 2 + AHEAD, turns)
            for tt in range(TT):
                act.wait_ge(added, 4 * turns + 2 * tt + 2)
                square_norm(5, (tt,))
            transposed_hi(5)
            for n in range(2):
                if n == 0:
                    split_hi(U_TURN + 3 + AHEAD, turns)
                    split_hi(U_TURN + 4 + AHEAD, turns)
                sigmoids(1, n, U_TURN + 4 + 2 * n, turns)

        @block.vector
        def _(dve):
            chain = [0]

            def then(ins):
                chain[0] += 1
                ins.then_inc(dve_chain, 1)
                dve.wait_ge(dve_chain, chain[0])

            def used(u, k=0):
                dve.wait_ge(unit_used, u + 1 + PER_EXPERT * k)

            def norm_rows(n):
                for tt in range(TT):
                    dve.wait_ge(squares_ready, 2 * n + tt + 1)
                    mean_of(tt, 1, D).then_inc(mean_ready, 1)
                dve.wait_ge(gain_landed[n % 2], 16 * (n // 2 + 1))
                for q in range(4):
                    tt, b = q // 2, q % 2
                    if b == 0:
                        dve.wait_ge(rstd_ready, 2 * n + tt + 1)
                    cols = slice(512 * b, 512 * b + 512)
                    nc.vector.scalar_tensor_tensor(out=xs[:, tt, cols], in0=resid[:, tt, cols], scalar=rstd[:, tt:tt + 1],
                                                   in1=gain_bc[n % 2][:, cols], op0=ALU.mult,
                                                   op1=ALU.mult).then_inc(xs_ready, 1)

            def transposed_lo(n):
                for q in range(4):
                    tt, b = q // 2, q % 2
                    dve.wait_ge(xt_hi_ready, 4 * XT_OF[n] + q + 1)
                    nc.vector.tensor_tensor(quarter(a_lo, tt, b), bank4(NORM_BANKS[n][q]),
                                            quarter(a_hi, tt, b).bitcast(F32), ALU.subtract).then_inc(xt_lo_ready, 1)

            def mean_of(at, n, width):
                return nc.vector.tensor_scalar(mean_sq[:, at:at + n], mean_sq[:, at:at + n], 1.0 / width, EPS,
                                               ALU.mult, ALU.add)

            dve.wait_ge(x_landed, 16)
            norm_rows(0)
            split_lo(0)
            transposed_lo(0)
            split_lo(1)

            def small_inputs():
                dve.wait_ge(small_landed, 144)
                nc.vector.tensor_tensor(lam_prod[:, 0, :], lam_in[:, 0, :], lam_in[:, 1, :], ALU.mult)
                then(nc.vector.tensor_tensor(lam_prod[:, 1, :], lam_in[:, 2, :], lam_in[:, 3, :], ALU.mult))
                nc.vector.tensor_reduce(lam_sum[:, :], lam_prod[:, :, :], AX_X, ALU.add).then_inc(lam_summed, 1)
                for s in range(2):
                    for n, (angle, half) in enumerate(((0, 0), (1, 1), (0, 1), (1, 0))):
                        gain = qk_gain[:, s, half * 32:half * 32 + 32].unsqueeze(1).to_broadcast([P, TT, 32])
                        last = nc.vector.tensor_tensor(rope_g[:, s, :, n, :], rope[:, :, angle, :], gain, ALU.mult)
                last.then_inc(rope_g_ready, 1)
                dve.wait_ge(consts_ready, 1)
                nc.vector.reciprocal(inv_count[:, :], inv_count[:, :]).then_inc(counts_inverted, 1)
                nc.vector.tensor_scalar(sub_gain[:, :], sub_gain[:, :], 1.0 - LAM_INIT, None, ALU.mult)

            def embeddings_lo():
                for layer in range(2):
                    dve.wait_ge(p_hi_ready, layer + 1)
                    nc.vector.tensor_tensor(p_t_lo[:, layer, :], ps[:, 6 + layer, :], p_t_hi[:, layer, :].bitcast(F32),
                                            ALU.subtract).then_inc(p_lo_ready, 1)
                dve.wait_ge(router_hi_ready, 1)
                nc.vector.tensor_tensor(router_lo[:, 0:KD * NE], router[:, :], router_hi[:, 0:KD * NE].bitcast(F32),
                                        ALU.subtract).then_inc(router_lo_ready, 1)
                dve.wait_ge(lam_exp, 1)
                then(nc.vector.tensor_tensor(neg_lam[:, :], lam_sum[:, 1:2], lam_sum[:, 0:1], ALU.subtract))
                then(nc.vector.tensor_scalar(neg_lam[:, :], neg_lam[:, :], LAM_INIT, None, ALU.subtract))

            def rotate(m):
                s, tt = m // 2, m % 2
                x = qkv[:, tt, s * D:(s + 1) * D].rearrange("p (g d) -> p g d", g=SUB)
                x1, x2 = x[:, :, 0:32], x[:, :, 32:64]

                def factor(n):
                    return rope_g[:, s, tt, n, :].unsqueeze(1).to_broadcast([P, SUB, 32])

                at = 16 + SUB * m
                dve.wait_ge(qk_squares, m + 1)
                then(nc.vector.tensor_reduce(mean_sq[:, at:at + SUB], squares.rearrange("p (g d) -> p g d", g=SUB),
                                             AX_X, ALU.add))
                mean_of(at, SUB, DH).then_inc(qk_mean, 1)
                dve.wait_ge(qk_rstd, m + 1)
                nc.vector.tensor_tensor(x, x, rstd[:, at:at + SUB].unsqueeze(2).to_broadcast([P, SUB, DH]),
                                        ALU.mult).then_inc(qk_normed, 1)
                dve.wait_ge(qk_normed, m + 1)
                t = turned[0].rearrange("p (g d) -> p g d", g=SUB)
                t2 = turned[1].rearrange("p (g d) -> p g d", g=SUB)
                then(nc.vector.tensor_tensor(t, x2, factor(1), ALU.mult))
                dve.wait_ge(qk_half, m + 1)
                nc.vector.tensor_tensor(x1, x1, factor(0), ALU.mult)
                then(nc.vector.tensor_tensor(x2, x2, factor(2), ALU.mult))
                nc.vector.tensor_tensor(x1, x1, t, ALU.subtract)
                nc.vector.tensor_tensor(x2, x2, t2, ALU.add).then_inc(qk_rotated, 1)

            for u in range(U_QKV, U_WO):
                split_lo(u + AHEAD)
                if u == 1:
                    small_inputs()
                if u == 5:
                    embeddings_lo()
                    rotate(0)
                if u == 6:
                    rotate(1)
                if u in (7, 9):
                    rotate(2 + (u - 7) // 2)

            def softmax_end(j):
                b, nk = j % BUFS, keys_of(j)
                dve.wait_ge(exp_ready, 2 * (j + 1))
                then(nc.vector.reciprocal(esum[:, b, 2:4], esum[:, b, 0:2]))
                then(nc.vector.tensor_tensor(esum[:, b, 3:4], esum[:, b, 3:4], neg_lam[:, :], ALU.mult))
                second = probs[:, b, 256:256 + nk]
                then(nc.vector.tensor_scalar(second, second, esum[:, b, 3:4], None, ALU.mult))
                nc.vector.scalar_tensor_tensor(out=probs[:, b, 0:nk], in0=probs[:, b, 0:nk], scalar=esum[:, b, 2:3],
                                               in1=second, op0=ALU.mult, op1=ALU.add).then_inc(probs_ready, 1)

            for i in range(HEAD_TILES + 7):
                if i < HEAD_TILES:
                    b, nk = i % BUFS, keys_of(i)
                    dve.wait_ge(scores_ready, i + 1)
                    then(nc.vector.tensor_reduce(smax[:, b, 0:2],
                                                 ps[:, b, :].rearrange("p (c n) -> p c n", c=2)[:, :, 0:nk],
                                                 AX_X, ALU.max))
                    nc.vector.tensor_scalar(smax[:, b, 2:4], smax[:, b, 0:2], -SCALE, None,
                                            ALU.mult).then_inc(shift_ready, 1)
                if 1 <= i < HEAD_TILES + 1:
                    softmax_end(i - 1)
                if i >= 7 and (i - 7) % 4 == 0 and (i - 7) // 4 < 4:
                    m = (i - 7) // 4
                    dve.wait_ge(o_squares, 4 * (m + 1))
                    mean_of(80 + 4 * m, 4, 2 * DH).then_inc(o_mean, 1)
                if i >= 8 and (i - 8) % 4 == 0 and (i - 8) // 4 < 4:
                    m = (i - 8) // 4
                    dve.wait_ge(o_rstd, m + 1)
                    at = D + 512 * (m % 2)
                    o = qkv[:, m // 2, at:at + 512].rearrange("p (h d) -> p h d", h=4)
                    scale = rstd[:, 80 + 4 * m:84 + 4 * m].unsqueeze(2).to_broadcast([P, 4, 2 * DH])
                    nc.vector.tensor_tensor(o, o, scale, ALU.mult).then_inc(o_normed, 1)
                if i >= 10 and (i - 10) % 4 == 0:
                    m = (i - 10) // 4
                    dve.wait_ge(o_hi_ready, m + 1)
                    nc.vector.scalar_tensor_tensor(out=quarter(a_lo, m // 2, m % 2), in0=bank4(3), scalar=sub_gain[:, 0:1],
                                                   in1=quarter(a_hi, m // 2, m % 2).bitcast(F32), op0=ALU.mult,
                                                   op1=ALU.subtract).then_inc(o_lo_ready, 1)
            for u in range(U_WO, U_FFN):
                split_lo(u + AHEAD)
                if u % 2:
                    nb = (u - U_WO) // 2
                    for tt in range(TT):
                        if nb == 1 and tt == 0:
                            dve.wait_ge(tile0_used, 1)
                        else:
                            used(u)
                        r = resid[:, tt, 512 * nb:512 * nb + 512]
                        nc.vector.tensor_tensor(r, r, ps[:, 4 + 2 * nb + tt, :], ALU.add).then_inc(resid_ready, 1)

            def hiddens(g, u, k=0):
                used(u, k)
                dve.wait_ge(silu_ready, g + 1 + FB * k)
                if g:
                    dve.wait_ge(hidden_transposed, g + FB * k)
                nc.vector.tensor_tensor(hidden, silu, ps[:, 1, :], ALU.mult).then_inc(hidden_ready, 1)

            def hidden_lo(g, k=0):
                dve.wait_ge(ht_hi_ready, g + 1 + FB * k)
                nc.vector.tensor_tensor(h_t_lo[:, :], ps[:, 2, :], h_t_hi[:, :].bitcast(F32),
                                        ALU.subtract).then_inc(ht_lo_ready, 1)

            norm_rows(1)
            transposed_lo(1)
            for j in range(JF):
                u = dense_group(j)
                split_lo(u + AHEAD)
                split_lo(u + 1 + AHEAD)
                hiddens(j, u + 1)
                if j:
                    split_lo(u + 2 + AHEAD)
                hidden_lo(j)
            split_lo(dense_down(JF - 1) + AHEAD)
            for tt in range(TT):
                if tt == 0:
                    dve.wait_ge(tile0_used, 2)
                else:
                    used(dense_down(JF - 1))
                for half in range(2):
                    r = resid[:, tt, 512 * half:512 * half + 512]
                    nc.vector.tensor_tensor(r, r, ps[:, 4 + 2 * tt + half, :], ALU.add).then_inc(resid_ready, 1)

            def add_gated(layer, n):
                for tt in range(TT):
                    q = 2 * n + tt
                    dve.wait_ge(sig_ready, 4 * layer + q + 1)
                    nc.vector.tensor_tensor(sig[tt], sig[tt], ps[:, PROJ_BANKS[layer][2 * tt + n], :],
                                            ALU.mult).then_inc(projected, 1)
                    dve.wait_ge(projected, 4 * layer + q + 1)
                    r = resid[:, tt, 512 * n:512 * n + 512]
                    nc.vector.tensor_tensor(r, r, sig[tt], ALU.add).then_inc(resid_ready, 1)

            norm_rows(2)
            split_lo(U_PLE0 + AHEAD)
            transposed_lo(2)
            for n in range(2):
                split_lo(U_PLE0 + 1 + 2 * n + AHEAD)
                split_lo(U_PLE0 + 2 + 2 * n + AHEAD)
                add_gated(0, n)

            norm_rows(3)
            for q in range(4):
                cols = slice(512 * q, 512 * q + 512)
                dve.wait_ge(rows_hi, q + 1)
                nc.vector.tensor_tensor(a_lo[:, cols], xs_flat[:, cols], a_hi[:, cols].bitcast(F32),
                                        ALU.subtract).then_inc(rows_lo, 1)
            for g in range(4):
                dve.wait_ge(pool_hi, g + 1)
                nc.vector.tensor_tensor(pool_half(y_lo, a_lo, g), ps[:, 4 + g, :], pool_half(y_hi, a_hi, g).bitcast(F32),
                                        ALU.subtract).then_inc(pool_lo, 1)
            split_lo(U_POOL + AHEAD)
            dve.wait_ge(scale_landed, 16)
            for q in range(4):
                tt, half = q // 2, slice(512 * (q % 2), 512 * (q % 2) + 512)
                if tt == 0:
                    dve.wait_ge(tile0_used, 4)
                else:
                    used(U_POOL)
                t = scaled[:, 512 * q:512 * q + 512]
                then(nc.vector.tensor_tensor(t, ps[:, q, :], scale_bc[:, half], ALU.mult))
                nc.vector.tensor_tensor(resid[:, tt, half], resid[:, tt, half], t, ALU.add).then_inc(resid_ready, 1)

            norm_rows(4)
            transposed_lo(4)

            dve.wait_ge(logits_ready, 1)
            then(nc.vector.tensor_copy(logits[:, :, :].rearrange("p t e -> p (t e)"), ps[:, 2, 0:TT * NE]))
            for tt in range(TT):
                then(nc.vector.max(top_v[:, tt, :], logits[:, tt, :]))
                then(nc.vector.max_index(top_i[:, tt, :], top_v[:, tt, :], logits[:, tt, :]))
            nc.vector.tensor_tensor(top_w[:, :, 0:1], top_v[:, :, 1:2], top_v[:, :, 0:1],
                                    ALU.subtract).then_inc(gap_ready, 1)
            then(nc.vector.tensor_copy(top_f[:, :, :], top_i[:, :, :]))
            for tt in range(TT):
                for n in range(2):
                    last = nc.vector.tensor_scalar(chose[:, tt, n, :], iota_expert[:, :], top_f[:, tt, n:n + 1], None,
                                                   ALU.is_equal)
            then(last)
            then(nc.vector.tensor_tensor(mask[:, 0:TT, :], chose[:, :, 0, :], chose[:, :, 1, :], ALU.add))
            nc.vector.tensor_tensor(mask[:, 2, :], mask[:, 0, :], mask[:, 1, :], ALU.add).then_inc(mask_ready, 1)
            dve.wait_ge(counted, 1)
            nc.vector.memset(place[:, :, 2 * NE:2 * NE + 1], -1.0)
            then(nc.vector.scalar_tensor_tensor(out=place[:, :, 0:NE],
                                                in0=ps[:, 1, 0:TT * NE].rearrange("p (t e) -> p t e", t=TT), scalar=1.0,
                                                in1=mask[:, 0:TT, :], op0=ALU.add, op1=ALU.mult))
            then(nc.vector.tensor_scalar(place[:, :, 0:NE], place[:, :, 0:NE], 1.0, None, ALU.subtract))
            then(nc.vector.tensor_scalar(place[:, :, NE:2 * NE], place[:, :, 0:NE], float(SLOTS), None, ALU.subtract))
            then(nc.vector.tensor_reduce(tokens[:, 0:1], ps[:, 1, 2 * NE:3 * NE], AX_X, ALU.max))
            nc.vector.tensor_scalar(more[:, :], tokens[:, 0:1], float(SLOTS), float(NE), ALU.is_gt,
                                    ALU.mult).then_inc(more_ready, 1)

            def picks(t, k=0):
                if t:
                    dve.wait_ge(pick_transposed, t + k)
                for tt in range(TT):
                    last = nc.vector.tensor_scalar(pick[:, tt * SLOTS:(tt + 1) * SLOTS], iota_slot[:, :],
                                                   place[:, tt, bass.ds(t + k, 1)], None, ALU.is_equal)
                last.then_inc(pick_ready, 1)

            def tokens_lo(t, k=0):
                dve.wait_ge(xe_hi_ready, t + 1 + k)
                nc.vector.tensor_tensor(xe_lo[:, :].rearrange("p (b n) -> p b n", b=2), ps[:, 5:7, :],
                                        xe_hi[:, :].bitcast(F32).rearrange("p (b n) -> p b n", b=2),
                                        ALU.subtract).then_inc(xe_lo_ready, 1)

            def result_lo(t, k=0):
                dve.wait_ge(y_hi_ready, t + 1 + k)
                nc.vector.tensor_tensor(y_lo[:, :].rearrange("p (b n) -> p b n", b=2), ps[:, 3:5, :],
                                        y_hi[:, :].bitcast(F32).rearrange("p (b n) -> p b n", b=2),
                                        ALU.subtract).then_inc(y_lo_ready, 1)

            def add_result(q, t, k=0):
                tt, half = q // 2, q % 2
                dve.wait_ge(scattered, 4 * (t + k) + q + 1)
                r = resid[:, tt, 512 * half:512 * half + 512]
                nc.vector.scalar_tensor_tensor(out=r, in0=ps[:, 5 + q % 2, :], scalar=gate[:, tt, bass.ds(t + k, 1)],
                                               in1=r, op0=ALU.mult, op1=ALU.add).then_inc(added, 1)

            picks(0)
            dve.wait_ge(gap_exp, 1)
            then(nc.vector.tensor_scalar(top_w[:, :, 2:3], top_w[:, :, 1:2], 1.0, None, ALU.add))
            then(nc.vector.reciprocal(top_w[:, :, 2:3], top_w[:, :, 2:3]))
            then(nc.vector.tensor_tensor(top_w[:, :, 3:4], top_w[:, :, 1:2], top_w[:, :, 2:3], ALU.mult))
            for tt in range(TT):
                for at in (0, NE):
                    last = nc.vector.tensor_scalar(gate[:, tt, at:at + NE], chose[:, tt, 0, :], top_w[:, tt, 2:3], None,
                                                   ALU.mult)
            then(last)
            for tt in range(TT):
                for at in (0, NE):
                    last = nc.vector.scalar_tensor_tensor(out=gate[:, tt, at:at + NE], in0=chose[:, tt, 1, :],
                                                          scalar=top_w[:, tt, 3:4], in1=gate[:, tt, at:at + NE],
                                                          op0=ALU.mult, op1=ALU.add)
            then(last)
            tokens_lo(0)

            def turn(t0, k=0):
                for f in range(FB):
                    u, g = turn_unit(t0, f), JF + FB * t0 + f
                    for n in range(4):
                        split_lo(u + n + AHEAD, k)
                    hiddens(g, u + 3, k)
                    if f == 1 and t0:
                        add_result(0, t0 - 1, k)
                        add_result(1, t0 - 1, k)
                    if f == 2:
                        dve.wait_ge(pick_transposed, t0 + 1 + k)
                        nc.vector.tensor_copy(pick_t[:, :], ps[:, 7, 0:TT * P]).then_inc(pick_t_copied, 1)
                    if f == 3:
                        picks(t0 + 1, k)
                    if f == FB - 1:
                        tokens_lo(t0 + 1, k)
                    if f or t0:
                        split_lo(u + 4 + AHEAD, k)
                        split_lo(u + 5 + AHEAD, k)
                    if f == 1 and t0:
                        add_result(2, t0 - 1, k)
                        add_result(3, t0 - 1, k)
                    hidden_lo(g, k)
                    if f == 0 and t0:
                        result_lo(t0 - 1, k)

            turn(0)
            extra = dve.value_load(more[0:1, 0:1], min_val=0, max_val=NE)
            turns = extra + (NE - 1)
            with dve.Fori(1, turns + 1) as it:
                turn(1, it - 1)
            split_lo(U_TURN + AHEAD, turns)
            split_lo(U_TURN + 1 + AHEAD, turns)
            result_lo(0, turns)
            for q in range(4):
                add_result(q, 0, turns)

            norm_rows(5)
            split_lo(U_TURN + 2 + AHEAD, turns)
            transposed_lo(5)
            for n in range(2):
                if n == 0:
                    split_lo(U_TURN + 3 + AHEAD, turns)
                    split_lo(U_TURN + 4 + AHEAD, turns)
                add_gated(1, n)

        @block.gpsimd
        def _(pool):
            chain = [0]

            def then(ins):
                chain[0] += 1
                ins.then_inc(pool_chain, 1)
                pool.wait_ge(pool_chain, chain[0])

            nc.gpsimd.memset(minus_half[:, :], -0.5)
            nc.gpsimd.memset(ones[:, :], 1.0)
            nc.gpsimd.memset(causal[:, :], 0.0)
            then(nc.gpsimd.memset(ident[:, :], 0.0))
            nc.gpsimd.affine_select(out=ident[:, :], in_=ident[:, :], compare_op=ALU.not_equal, fill=1.0, base=0,
                                    pattern=[[-1, P]], channel_multiplier=1)
            nc.gpsimd.affine_select(out=causal[:, :], in_=causal[:, :], compare_op=ALU.is_ge, fill=MASKED, base=0,
                                    pattern=[[-1, P]], channel_multiplier=1)
            nc.gpsimd.affine_select(out=before[:, :], in_=ones[:, :], compare_op=ALU.is_gt, fill=0.0, base=0,
                                    pattern=[[1, P]], channel_multiplier=-1)
            nc.gpsimd.iota(iota_slot[:, :], pattern=[[1, SLOTS]], base=0, channel_multiplier=0,
                           allow_small_or_imprecise_dtypes=True)
            nc.gpsimd.iota(inv_count[:, :], pattern=[[1, 16]], base=1, channel_multiplier=0,
                           allow_small_or_imprecise_dtypes=True)
            nc.gpsimd.iota(iota_expert[:, :], pattern=[[1, NE]], base=0, channel_multiplier=0,
                           allow_small_or_imprecise_dtypes=True).then_inc(consts_ready, 1)
            pool.wait_ge(consts_ready, 1)

            def root(at, n):
                return nc.gpsimd.tensor_tensor(rstd[:, at:at + n], mean_sq[:, at:at + n], minus_half[:, 0:n], ALU.pow)

            def norm_root(n):
                for tt in range(TT):
                    pool.wait_ge(mean_ready, 2 * n + tt + 1)
                    root(tt, 1).then_inc(rstd_ready, 1)

            pool.dma_start(rope[:, :, :, :], dram["rope"].rearrange("(t p) a n -> p t a n", p=P)).then_inc(small_landed, 16)
            for n, name in enumerate(("attn_q_norm", "attn_k_norm")):
                pool.dma_start(qk_gain[:, n, :], dram[name][0].partition_broadcast(P)).then_inc(small_landed, 16)
            for n, name in enumerate(("attn_lambda_q1", "attn_lambda_k1", "attn_lambda_q2", "attn_lambda_k2")):
                pool.dma_start(lam_in[:, n, :], dram[name][0].partition_broadcast(P)).then_inc(small_landed, 16)
            pool.dma_start(router[:, :].rearrange("p (c e) -> p c e", c=KD),
                           dram["moe_router"][0].rearrange("(c p) e -> p c e", p=P)).then_inc(small_landed, 16)
            pool.dma_start(sub_gain[:, :], dram["attn_subln"].rearrange("a p -> p a"),
                           allow_slow_non_contiguous=True).then_inc(small_landed, 16)
            norm_root(0)
            for layer in range(2):
                pool.dma_start(p_sb[:, layer], dram["p"][layer, 0].rearrange("(t p) n -> p t n", p=P)).then_inc(p_landed, 16)
            nc.gpsimd.memset(router_hi[:, KD * NE:].bitcast(F32), 0.0)
            nc.gpsimd.memset(router_lo[:, KD * NE:].bitcast(F32), 0.0)

            pool.wait_ge(counts_inverted, 1)
            for g in range(4):
                w = 2 << g
                then(nc.gpsimd.memset(band, 1.0))
                then(nc.gpsimd.affine_select(out=band, in_=band, compare_op=ALU.is_ge, fill=0.0, base=0,
                                             pattern=[[1, SEQ]], channel_multiplier=-1))
                then(nc.gpsimd.affine_select(out=band, in_=band, compare_op=ALU.is_ge, fill=0.0, base=w - 1,
                                             pattern=[[-1, SEQ]], channel_multiplier=1))
                nc.gpsimd.tensor_tensor(band[:, 0:w], band[:, 0:w], inv_count[:, 0:w], ALU.mult)
                then(nc.gpsimd.tensor_scalar(band[:, w:SEQ], band[:, w:SEQ], 1.0 / w, None, ALU.mult))
                then(nc.gpsimd.tensor_tensor(band[:, 0:P], band[:, 0:P], ident[:, :], ALU.subtract))
                then(nc.gpsimd.tensor_copy(band_hi[:, g, :], band))
                nc.gpsimd.tensor_tensor(band_lo[:, g, :], band[:, 0:16], band_hi[:, g, 0:16].bitcast(F32), ALU.subtract)
                then(nc.gpsimd.tensor_copy(band_own[:, g, w:P], band[:, w:P]))
                then(nc.gpsimd.memset(band[:, 0:w], 1.0 / w))
                then(nc.gpsimd.affine_select(out=band[:, 0:w], in_=band[:, 0:w], compare_op=ALU.is_ge, fill=0.0, base=0,
                                             pattern=[[1, w]], channel_multiplier=-1))
                then(nc.gpsimd.tensor_tensor(band[:, 0:w], band[:, 0:w], ident[:, 0:w], ALU.subtract))
                then(nc.gpsimd.tensor_copy(band_own[:, g, 0:w], band[:, 0:w]))
            nc.gpsimd.nop().then_inc(bands_ready, 1)

            for m in range(4):
                s, tt = m // 2, m % 2
                pool.wait_ge(qk_mean, m + 1)
                root(16 + SUB * m, SUB).then_inc(qk_rstd, 1)
                pool.wait_ge(qk_normed, m + 1)
                if m == 0:
                    pool.wait_ge(rope_g_ready, 1)
                else:
                    pool.wait_ge(qk_rotated, m)
                x1 = qkv[:, tt, s * D:(s + 1) * D].rearrange("p (g d) -> p g d", g=SUB)[:, :, 0:32]
                nc.gpsimd.tensor_tensor(turned[1].rearrange("p (g d) -> p g d", g=SUB), x1,
                                        rope_g[:, s, tt, 3, :].unsqueeze(1).to_broadcast([P, SUB, 32]),
                                        ALU.mult).then_inc(qk_half, 1)
            for m in range(4):
                pool.wait_ge(o_mean, m + 1)
                root(80 + 4 * m, 4).then_inc(o_rstd, 1)
            norm_root(1)
            norm_root(2)
            norm_root(3)
            norm_root(4)
            for q in range(4):
                cols = slice(512 * q, 512 * q + 512)
                pool.wait_ge(rows_hi, 4 + q + 1)
                nc.gpsimd.tensor_tensor(a_lo[:, cols], xs_flat[:, cols], a_hi[:, cols].bitcast(F32),
                                        ALU.subtract).then_inc(rows_lo, 1)
            norm_root(5)


_INS = ["x", "p", "norm_mix", "norm_ffn", "norm_ple", "attn_w_qkv", "attn_w_o", "attn_q_norm", "attn_k_norm",
        "attn_lambda_q1", "attn_lambda_k1", "attn_lambda_q2", "attn_lambda_k2", "attn_subln", "pool_w", "pool_b",
        "pool_scale", "ffn_w_gate", "ffn_w_up", "ffn_w_down", "moe_router", "moe_w_gate", "moe_w_up", "moe_w_down",
        "ple_w_proj", "ple_w_gate"]


def kernel(**inputs):
    import numpy as np
    import concourse.bacc as bacc
    from concourse.bass_utils import run_bass_kernel_spmd

    nc = bacc.Bacc("TRN2", target_bir_lowering=False, num_devices=1)
    inv = (1.0 / (np.float32(10000.0) ** (np.arange(0, DH, 2, dtype=np.float32) / np.float32(DH)))).astype(np.float32)
    angle = np.arange(SEQ, dtype=np.float32)[:, None] * inv[None, :]
    arrays = {"in_rope_dram": np.stack([np.cos(angle), np.sin(angle)], axis=1).astype(np.float32)}
    for name in _INS:
        arrays[f"in_{name}_dram"] = np.ascontiguousarray(inputs[name])
    dram = {}
    for key, a in arrays.items():
        dram[key[3:-5]] = nc.dram_tensor(key, a.shape, mybir.dt.from_np(a.dtype), kind="ExternalInput").ap()
    dram["out"] = nc.dram_tensor("out_0_dram", (1, SEQ, D), F32, kind="ExternalOutput").ap()
    trunk(nc, dram)
    r = run_bass_kernel_spmd(nc, [arrays], core_ids=[0])
    return r.results[0]["out_0_dram"]
```

```python
from contextlib import ExitStack

import concourse.bass as bass
from concourse import mybir

F32 = mybir.dt.float32
BF16 = mybir.dt.bfloat16
F32R = mybir.dt.float32r
I32 = mybir.dt.int32
U32 = mybir.dt.uint32
ALU = mybir.AluOpType
ACT = mybir.ActivationFunctionType
AX_X = mybir.AxisListType.X

P = 128
SEQ = 256
TT = SEQ // P
D = 1024
KD = D // P
DH = 64
HEADS = D // (2 * DH)
SUB = 2 * HEADS
NE = 8
FF = 2816
FE = 3584
PLE = 256
EPS = 1e-6
LAM_INIT = 0.2
SCALE = DH ** -0.5
MASKED = -1e30

UNIT = 2048
RAW = 7
SPLIT = 3
AHEAD = 2

U_QKV = 0
U_WO = 12
SHARED = (0, *range(2, 16), 56)
U_FFN = 16
JF = FF // 256
U_PLE0 = U_FFN + 3 * JF
U_POOL = U_PLE0 + 5
U_MOE = U_POOL + 1
FB = FE // 512
PER_EXPERT = 6 * FB
U_TURN = U_MOE + PER_EXPERT - 2
EXTRA = 3
U_WIDE = U_TURN - RAW - EXTRA
SLOTS = P


def trunk(nc, dram):
    ctx = ExitStack()
    with ctx:
        def sb(name, shape, dt=F32):
            return ctx.enter_context(nc.sbuf_tensor(name, shape, dt))

        def sem(name):
            return ctx.enter_context(nc.semaphore(name))

        raw = sb("raw", [P, RAW, UNIT])
        w_hi = sb("w_hi", [P, SPLIT, UNIT], F32R)
        w_lo = sb("w_lo", [P, SPLIT, UNIT], F32R)
        resid = sb("resid", [P, TT, D])
        xs = sb("xs", [P, TT, D])
        a_hi = sb("a_hi", [P, UNIT], F32R)
        a_lo = sb("a_lo", [P, UNIT], F32R)
        wide = sb("wide", [P, 6144])
        h_t_hi = sb("h_t_hi", [P, 512], F32R)
        h_t_lo = sb("h_t_lo", [P, 512], F32R)
        xe_hi = sb("xe_hi", [P, D], F32R)
        xe_lo = sb("xe_lo", [P, D], F32R)
        y_hi = sb("y_hi", [P, D], F32R)
        y_lo = sb("y_lo", [P, D], F32R)
        tmp = sb("tmp", [P, UNIT])
        p_t_hi = sb("p_t_hi", [P, 2, 512], F32R)
        p_t_lo = sb("p_t_lo", [P, 2, 512], F32R)
        ident = sb("ident", [P, P])
        ones = sb("ones", [P, P])
        ones16 = sb("ones16", [P, P], BF16)
        before = sb("before", [P, P], BF16)
        causal = sb("causal", [P, P])
        iota_slot = sb("iota_slot", [P, SLOTS])
        iota_expert = sb("iota_expert", [P, NE])
        rope = sb("rope", [P, TT, 2, DH // 2])
        qk_gain = sb("qk_gain", [P, 2, DH])
        rope_g = sb("rope_g", [P, 2, TT, 4, DH // 2])
        lam_sum = sb("lam_sum", [P, 2])
        neg_lam = sb("neg_lam", [P, 1])
        sub_gain = sb("sub_gain", [P, 1])
        minus_half = sb("minus_half", [P, 16])
        mean_sq = sb("mean_sq", [P, 96])
        rstd = sb("rstd", [P, 96])
        smax = sb("smax", [P, 3, 4])
        esum = sb("esum", [P, 3, 4])
        inv_count = sb("inv_count", [P, 16])
        router = sb("router", [P, KD * NE])
        router_hi = sb("router_hi", [P, KD * NE + P - NE], F32R)
        router_lo = sb("router_lo", [P, KD * NE + P - NE], F32R)
        logits = sb("logits", [P, TT, NE])
        top_v = sb("top_v", [P, TT, 8])
        top_i = sb("top_i", [P, TT, 8], U32)
        top_f = sb("top_f", [P, TT, 8])
        top_w = sb("top_w", [P, TT, 4])
        chose = sb("chose", [P, TT, 2, NE])
        mask = sb("mask", [P, 3, NE], BF16)
        gate = sb("gate", [P, TT, 2 * NE])
        place = sb("place", [P, TT, 2 * NE + 1])
        tokens = sb("tokens", [P, NE])
        more = sb("more", [P, 1], I32)
        pick = sb("pick", [P, TT * SLOTS])
        pick_t = sb("pick_t", [P, TT * P], F32R)
        ps = ctx.enter_context(nc.psum_tensor("ps", [P, 8, 512], F32))

        qkv = wide[:, :].rearrange("p (t n) -> p t n", t=TT)
        q_t = xs[:, :, :].rearrange("p t n -> p (t n)").rearrange("p (h s) -> p h s", h=HEADS)
        gain_bc = [wide[:, 0:D], wide[:, D:2 * D]]
        scale_bc = wide[:, 2 * D:3 * D]
        bias_bc = wide[:, 3 * D:4 * D]
        band_hi = xe_hi[:, :].rearrange("p (g s) -> p g s", g=4)
        band_own = xe_lo[:, :].rearrange("p (g s) -> p g s", g=4)
        band_lo = pick_t[:, 0:64].rearrange("p (g s) -> p g s", g=4)
        p_sb = qkv[:, :, 2 * D:2 * D + 512].rearrange("p l (t n) -> p l t n", t=TT)
        lam_in = tmp[:, D + P:D + P + 4 * DH].rearrange("p (a d) -> p a d", a=4)
        lam_prod = tmp[:, D + P + 4 * DH:D + P + 6 * DH].rearrange("p (a d) -> p a d", a=2)
        band = tmp[:, 3 * 512:3 * 512 + SEQ]
        squares = tmp[:, 0:D]
        turned = [tmp[:, D:D + 512], tmp[:, D + 512:2 * D]]
        probs = tmp[:, 0:3 * 512].rearrange("p (b n) -> p b n", b=3)
        probs_t = tmp[:, 3 * 512:4 * 512].rearrange("p (b n) -> p b n", b=2)
        logits_t = tmp[0:NE, 0:SEQ]
        hidden = tmp[:, 0:512]
        silu = tmp[:, 512:1024]
        sig = [tmp[:, 1024:1536], tmp[:, 1536:2048]]

        landed = [sem(f"landed{i}") for i in range(RAW)]
        extra_landed = [sem(f"extra_landed{i}") for i in range(EXTRA)]
        (hi_ready, lo_ready, shared_ready, unit_used,
         x_landed0, x_landed1, p_landed, gain_landed0, gain_landed1, small_landed, scale_landed, bias_landed, consts_ready,
         dve_chain, pool_chain, tile0_used, counts_inverted, bands_ready, mixer_scaled,
         p_transposed, p_hi_ready, p_lo_ready,
         squares_ready, mean_ready, rstd_ready, xs_ready, xs_transposed, xt_hi_ready, xt_lo_ready,
         resid_ready, block_copied,
         rope_g_ready, qk_squares, qk_mean, qk_rstd, qk_normed, qk_half, qk_rotated, qk_transposed, qk_t_copied,
         lam_summed, lam_exp, lam_ready,
         first_scores, scores_ready, shift_ready, exp_ready, probs_ready, probs_transposed, probs_t_copied,
         av_ready, av_copied,
         o_squares, o_mean, o_rstd, o_normed, o_transposed, o_hi_ready, o_lo_ready,
         silu_ready, hidden_ready, hidden_transposed, ht_hi_ready, ht_lo_ready, sig_ready, projected,
         biased, pooled, pool_hi, pool_lo,
         router_hi_ready, router_lo_ready, routed, logits_t_ready, logits_ready, gap_ready, gap_exp, mask_ready, counted, more_ready,
         rows_hi, rows_lo, rows_lo0,
         pick_ready, gathered, xe_hi_ready, xe_lo_ready, pick_transposed, pick_t_copied,
         y_hi_ready, y_lo_ready, scattered, added, stored) = (sem(n) for n in """
         hi_ready lo_ready shared_ready unit_used
         x_landed0 x_landed1 p_landed gain_landed0 gain_landed1 small_landed scale_landed bias_landed consts_ready
         dve_chain pool_chain tile0_used counts_inverted bands_ready mixer_scaled
         p_transposed p_hi_ready p_lo_ready
         squares_ready mean_ready rstd_ready xs_ready xs_transposed xt_hi_ready xt_lo_ready
         resid_ready block_copied
         rope_g_ready qk_squares qk_mean qk_rstd qk_normed qk_half qk_rotated qk_transposed qk_t_copied
         lam_summed lam_exp lam_ready
         first_scores scores_ready shift_ready exp_ready probs_ready probs_transposed probs_t_copied
         av_ready av_copied
         o_squares o_mean o_rstd o_normed o_transposed o_hi_ready o_lo_ready
         silu_ready hidden_ready hidden_transposed ht_hi_ready ht_lo_ready sig_ready projected
         biased pooled pool_hi pool_lo
         router_hi_ready router_lo_ready routed logits_t_ready logits_ready gap_ready gap_exp mask_ready counted more_ready
         rows_hi rows_lo rows_lo0
         pick_ready gathered xe_hi_ready xe_lo_ready pick_transposed pick_t_copied
         y_hi_ready y_lo_ready scattered added stored""".split())

        gain_landed = [gain_landed0, gain_landed1]
        x_landed = [x_landed0, x_landed1]

        def in_wide(u):
            return U_WIDE <= u < U_WIDE + EXTRA

        def ring(u):
            return u if u < U_WIDE else u - EXTRA

        def raw_slot(u):
            if in_wide(u):
                at = (2 * D, 4 * D, 0)[u - U_WIDE]
                return wide[:, at:at + UNIT]
            return raw[:, ring(u) % RAW, :]

        def load_wait(eng, u, k=0):
            if in_wide(u):
                eng.wait_ge(extra_landed[u - U_WIDE], 16)
            else:
                eng.wait_ge(landed[ring(u) % RAW], 16 * (ring(u) // RAW + 1) + 16 * (PER_EXPERT // RAW) * k)

        def split_hi(u, k=0):
            load_wait(nc.scalar, u, k)
            if u == U_POOL:
                nc.scalar.wait_ge(mixer_scaled, 2)
            if u >= SPLIT:
                nc.scalar.wait_ge(unit_used, u - SPLIT + 1 + PER_EXPERT * k)
            nc.scalar.activation(w_hi[:, u % SPLIT, :], raw_slot(u), ACT.Copy).then_inc(hi_ready, 1)

        def split_lo(u, k=0):
            nc.vector.wait_ge(hi_ready, u + 1 + PER_EXPERT * k)
            n = UNIT // 2 if u in SHARED else UNIT
            nc.vector.tensor_tensor(w_lo[:, u % SPLIT, 0:n], raw_slot(u)[:, 0:n], w_hi[:, u % SPLIT, 0:n].bitcast(F32),
                                    ALU.subtract).then_inc(lo_ready, 1)

        def share_lo(u):
            nc.gpsimd.wait_ge(hi_ready, u + 1)
            n = UNIT // 2
            nc.gpsimd.tensor_tensor(w_lo[:, u % SPLIT, n:], raw_slot(u)[:, n:], w_hi[:, u % SPLIT, n:].bitcast(F32),
                                    ALU.subtract).then_inc(shared_ready, 1)

        def split_wait(eng, u, k=0):
            eng.wait_ge(lo_ready, u + 1 + PER_EXPERT * k)
            if u in SHARED:
                eng.wait_ge(shared_ready, SHARED.index(u) + 1)

        def load(eng, u, view, k=0):
            dst = raw_slot(u).rearrange("p (c n) -> p c n", c=view.shape[1])
            if in_wide(u):
                eng.dma_start(dst, view).then_inc(extra_landed[u - U_WIDE], 16)
                return
            if u >= RAW:
                before_it = ring(u) - RAW
                split_wait(eng, before_it if before_it < U_WIDE else before_it + EXTRA, k)
            eng.dma_start(dst, view).then_inc(landed[ring(u) % RAW], 16)

        def product(out, x, w, first, last):
            nc.tensor.matmul(out, x[0], w[0], start=first, stop=False)
            nc.tensor.matmul(out, x[0], w[1], start=False, stop=False)
            return nc.tensor.matmul(out, x[1], w[0], start=False, stop=last)

        def weights(u, c, n0, n, width):
            at = c * width + n0
            return w_hi[:, u % SPLIT, at:at + n], w_lo[:, u % SPLIT, at:at + n]

        def acts(c, tt):
            at = c * SEQ + tt * P
            return a_hi[:, at:at + P], a_lo[:, at:at + P]

        block = ctx.enter_context(nc.Block())

        @block.sync
        def _(sp):
            def chunks(w, c0, c, n0, n):
                return w.rearrange("(c p) n -> p c n", p=P)[:, c0:c0 + c, n0:n0 + n]

            for tt in range(TT):
                sp.dma_start(resid[:, tt, :], dram["x"][0, tt * P:(tt + 1) * P, :]).then_inc(x_landed[tt], 16)
            sp.dma_start(gain_bc[0], dram["norm_mix"][0].partition_broadcast(P)).then_inc(gain_landed0, 16)
            u = U_QKV
            for nb in range(6):
                for half in range(2):
                    load(sp, u, chunks(dram["attn_w_qkv"][0], 4 * half, 4, 512 * nb, 512))
                    u += 1

            def load_gain(n):
                if n >= 3:
                    sp.wait_ge(xs_ready, 4 * (n - 1))
                name = ("norm_mix", "norm_ffn", "norm_ple")[n % 3]
                sp.dma_start(gain_bc[n % 2], dram[name][n // 3].partition_broadcast(P)).then_inc(gain_landed[n % 2], 16)

            for nb in range(2):
                for half in range(2):
                    load(sp, u, chunks(dram["attn_w_o"][0], 4 * half, 4, 512 * nb, 512))
                    u += 1
            wg, wu, wd = (dram[n][0] for n in ("ffn_w_gate", "ffn_w_up", "ffn_w_down"))
            for j in range(JF):
                if j == 2:
                    sp.wait_ge(o_transposed, 4)
                    load_gain(1)
                    load_gain(2)
                    sp.dma_start(scale_bc, dram["pool_scale"][0].partition_broadcast(P)).then_inc(scale_landed, 16)
                    sp.dma_start(bias_bc, dram["pool_b"][0].rearrange("g e -> (g e)").partition_broadcast(P)).then_inc(bias_landed, 16)
                if j == 5:
                    load_gain(3)
                for w in (wg, wu):
                    load(sp, u, chunks(w, 0, KD, 256 * j, 256))
                    u += 1
                if j:
                    load(sp, u, chunks(wd, 2 * (j - 1), 2, 0, D))
                    u += 1
            load(sp, u, chunks(wd, 2 * (JF - 1), 2, 0, D))
            u += 1

            def load_ple(layer, u, k=0):
                load(sp, u, chunks(dram["ple_w_proj"][layer], 0, 2, 0, D), k)
                for n in range(4):
                    load(sp, u + 1 + n, chunks(dram["ple_w_gate"][layer], 4 * (n % 2), 4, 512 * (n // 2), 512), k)

            load_ple(0, u)
            load(sp, U_POOL, dram["pool_w"][0].rearrange("g (c p) e -> p (g c) e", p=P))

            ge, ue, de = (dram[n][0] for n in ("moe_w_gate", "moe_w_up", "moe_w_down"))

            def expert_rows(w, e, c0, c, n0, n):
                m = w.rearrange("e (c p) n -> e p c n", p=P)[bass.ds(e, 1), :, c0:c0 + c, n0:n0 + n]
                return m.rearrange("a p c n -> (a p) c n")

            def expert_units(e, e_before, u, first=False):
                units = []
                for f in range(FB):
                    views = [expert_rows(w, e, 4 * half, 4, 512 * f, 512) for w in (ge, ue) for half in range(2)]
                    if f or not first:
                        views += [expert_rows(de, e if f else e_before, 4 * ((f - 1) % FB) + 2 * half, 2, 0, D)
                                  for half in range(2)]
                    units += [(u + n, view) for n, view in enumerate(views)]
                    u += len(views)
                return units

            def load_expert(e, e_before, k):
                for u, view in expert_units(e, e_before, U_TURN):
                    load(sp, u, view, k)

            first_expert = expert_units(0, None, U_MOE, first=True)
            extras = [item for item in first_expert if in_wide(item[0])]
            for u, view in first_expert:
                if u == U_MOE + RAW - 3:
                    load_gain(4)
                if u == U_MOE + RAW + 1:
                    sp.wait_ge(biased, 4)
                    load(sp, *extras[0])
                    load(sp, *extras[1])
                if u == U_MOE + RAW + 2:
                    sp.wait_ge(xs_ready, 20)
                    load(sp, *extras[2])
                if not in_wide(u):
                    load(sp, u, view)
            with sp.Fori(1, NE) as it:
                load_expert(it, it - 1, it - 1)
            sp.wait_ge(more_ready, 1)
            extra = sp.value_load(more[0:1, 0:1], min_val=0, max_val=NE)
            with sp.If(extra > 0):
                load_expert(0, NE - 1, NE - 1)
                with sp.Fori(1, NE) as it:
                    load_expert(it, it - 1, it + (NE - 1))
            turns = extra + (NE - 1)
            load_gain(5)
            for half in range(2):
                load(sp, U_TURN + half, expert_rows(de, NE - 1, 4 * (FB - 1) + 2 * half, 2, 0, D), turns)
            load_ple(1, U_TURN + 2, turns)
            out = dram["out"][0].rearrange("(t p) d -> p t d", p=P)
            for n in range(4):
                half, tt = n // 2, n % 2
                sp.wait_ge(resid_ready, 4 * 4 + n + 1)
                cols = slice(512 * half, 512 * half + 512)
                sp.dma_start(out[:, tt, cols], resid[:, tt, cols]).then_inc(stored, 16)
            sp.wait_ge(stored, 64)

        def dense_group(j):
            return U_FFN if j == 0 else U_FFN - 1 + 3 * j

        def dense_down(j):
            return U_PLE0 - 1 if j == JF - 1 else dense_group(j + 1) + 2

        def turn_unit(t0, f):
            return U_TURN + PER_EXPERT * (t0 - 1) + 6 * f + (2 if t0 == 0 and f == 0 else 0)

        XT_OF = {0: 0, 1: 1, 2: 2, 4: 3, 5: 4}
        NORM_BANKS = {n: (3, 4, 5, 6) if n == 5 else (4, 5, 6, 7) for n in XT_OF}
        PROJ_BANKS = ((0, 1, 2, 3), (0, 1, 2, 7))
        GATE_BANKS = ((4, 5, 6, 7), (3, 4, 5, 6))
        MEANS_AT = (3, 4, 7, 8)
        ROTATE_AT = (4, 5, 8, 9)
        WO_BANKS = ((1, 4), (2, 5))
        BUFS = 3

        BY_TILE, BY_HALF = ((0, 0), (0, 1), (1, 0), (1, 1)), ((0, 0), (1, 0), (0, 1), (1, 1))
        QUARTERS = {0: BY_TILE, 1: BY_HALF, 2: BY_TILE, 3: BY_HALF, 4: BY_TILE, 5: BY_TILE}
        xs_flat = xs[:, :, :].rearrange("p t n -> p (t n)")

        def quarter(a, tt, b):
            return a[:, :].rearrange("p (c s) -> p c s", c=KD)[:, 4 * b:4 * b + 4, tt * P:(tt + 1) * P]

        def bank4(bank):
            return ps[:, bank, :].rearrange("p (c s) -> p c s", c=4)

        def pool_half(y, a, g):
            return (y if g < 2 else a)[:, 512 * (g % 2):512 * (g % 2) + 512]

        HEAD_TILES = TT * HEADS

        def keys_of(i):
            return P * (i // HEADS + 1)

        @block.tensor
        def _(pe):
            def unit(u, k=0):
                split_wait(pe, u, k)

            def transpose_norm(n):
                k = XT_OF[n]
                for q in range(4):
                    tt, b = q // 2, q % 2
                    pe.wait_ge(xs_ready, 4 * n + q + 1)
                    for c in range(4):
                        last = nc.tensor.transpose(ps[:, NORM_BANKS[n][q], c * P:(c + 1) * P],
                                                   xs[:, tt, (4 * b + c) * P:(4 * b + c + 1) * P], ident[:, :])
                    last.then_inc(xs_transposed, 1)

            def tile512(u, half, bank, tt):
                for c in range(4):
                    last = product(ps[:, bank, :], acts(4 * half + c, tt), weights(u, c, 0, 512, 512),
                                   half == 0 and c == 0, half == 1 and c == 3)
                return last

            def block512(u, half, banks, k=0, norm=None, early=False):
                unit(u, k)
                for tt in range(TT):
                    if norm is not None:
                        pe.wait_ge(xt_lo_ready, 4 * XT_OF[norm] + 2 * tt + half + 1)
                    last = tile512(u, half, banks[tt], tt)
                    if early and tt == 0:
                        last.then_inc(tile0_used, 1)
                last.then_inc(unit_used, 1)

            def project(layer, tt, u):
                for half in range(2):
                    for c in range(2):
                        at = c * SEQ + tt * P
                        last = product(ps[:, PROJ_BANKS[layer][2 * tt + half], :],
                                       (p_t_hi[:, layer, at:at + P], p_t_lo[:, layer, at:at + P]),
                                       weights(u, c, 512 * half, 512, D), c == 0, c == 1)
                return last

            def gates(layer, u, k=0):
                for n in range(4):
                    half = n // 2
                    block512(u + n, n % 2, GATE_BANKS[layer][2 * half:2 * half + 2], k,
                             norm=3 * layer + 2 if n < 2 else None, early=n == 3)

            def transpose_qk(s):
                pe.wait_ge(qk_rotated, 2 * (s + 1))
                pe.wait_ge(block_copied, 8)
                for pair in range(4):
                    if s == 1:
                        pe.wait_ge(qk_t_copied, pair + 1)
                    for h in (2 * pair, 2 * pair + 1):
                        for tt in range(TT):
                            at = (h % 2) * SEQ + tt * P
                            last = nc.tensor.transpose(ps[:, 4 + pair, at:at + P],
                                                       qkv[:, tt, s * D + h * P:s * D + (h + 1) * P], ident[:, :])
                    last.then_inc(qk_transposed, 1)

            pe.wait_ge(consts_ready, 1)
            transpose_norm(0)
            for nb in range(6):
                if nb == 2:
                    pe.wait_ge(xt_lo_ready, 4)
                if nb == 3:
                    pe.wait_ge(p_lo_ready, 2)
                if nb >= 4:
                    pe.wait_ge(block_copied, 2 * (nb - 3))
                for half in range(2):
                    block512(U_QKV + 2 * nb + half, half, (2 * (nb % 4), 2 * (nb % 4) + 1), norm=0 if nb == 0 else None)
                if nb == 1:
                    pe.wait_ge(xt_lo_ready, 4)
                    pe.wait_ge(p_landed, 32)
                    for layer in range(2):
                        for c in range(2):
                            for tt in range(TT):
                                at = c * SEQ + tt * P
                                last = nc.tensor.transpose(ps[:, 6 + layer, at:at + P],
                                                           p_sb[:, layer, tt, c * P:(c + 1) * P], ident[:, :])
                        last.then_inc(p_transposed, 1)
                if nb >= 4:
                    transpose_qk(nb - 4)
            def score(i, c):
                qt, h, nk = i // HEADS, i % HEADS, keys_of(i)
                at, rows = 256 * c, slice(DH * c, DH * c + DH)
                nc.tensor.matmul(ps[:, i % BUFS, at:at + nk], q_t[rows, h, qt * P:(qt + 1) * P],
                                 qkv[rows, 0:qt + 1, h * P:(h + 1) * P], start=True, stop=False)
                return nc.tensor.matmul(ps[:, i % BUFS, at + nk - P:at + nk], ident[:, :], causal[:, :],
                                        start=False, stop=True)

            pe.wait_ge(block_copied, 12)
            for i in range(HEAD_TILES + 8):
                if i < HEAD_TILES:
                    if i < HEADS:
                        pe.wait_ge(qk_t_copied, 4 + i // 2 + 1)
                    if i >= BUFS:
                        pe.wait_ge(exp_ready, 2 * (i - BUFS + 1))
                    score(i, 0).then_inc(first_scores, 1)
                if 4 <= i < HEAD_TILES + 4:
                    j = i - 4
                    h, nt = j % HEADS, keys_of(j) // P
                    pe.wait_ge(probs_t_copied, j + 1)
                    if j % 4 == 0 and j >= 8:
                        pe.wait_ge(o_squares, 4 * (j // 4 - 1))
                    at = (j % 4) * P
                    for kc in range(nt):
                        last = nc.tensor.matmul(ps[:, 6 + (j // 4) % 2, at:at + P],
                                                probs_t[:, j % 2, kc * P:(kc + 1) * P],
                                                qkv[:, kc, 2 * D + h * P:2 * D + (h + 1) * P],
                                                start=kc == 0, stop=kc == nt - 1)
                    last.then_inc(av_ready, 1)
                if i < HEAD_TILES:
                    pe.wait_ge(first_scores, i + 1)
                    score(i, 1).then_inc(scores_ready, 1)
                if 2 <= i < HEAD_TILES + 2:
                    j = i - 2
                    pe.wait_ge(probs_ready, j + 1)
                    if j == 0:
                        pe.wait_ge(qk_t_copied, 8)
                    if j >= 2:
                        pe.wait_ge(probs_t_copied, j - 1)
                    for kc in range(keys_of(j) // P):
                        last = nc.tensor.transpose(ps[:, 4 + j % 2, kc * P:(kc + 1) * P],
                                                   probs[:, j % BUFS, kc * P:(kc + 1) * P], ident[:, :])
                    last.then_inc(probs_transposed, 1)
                if i >= 11 and (i - 11) % 4 == 0:
                    m = (i - 11) // 4
                    pe.wait_ge(o_normed, m + 1)
                    if m:
                        pe.wait_ge(o_lo_ready, m)
                    tt = m // 2
                    for h in range(4 * (m % 2), 4 * (m % 2) + 4):
                        last = nc.tensor.transpose(ps[:, 3, (h % 4) * P:(h % 4 + 1) * P],
                                                   qkv[:, tt, D + h * P:D + (h + 1) * P], ident[:, :])
                    last.then_inc(o_transposed, 1)
                if i in (HEAD_TILES, HEAD_TILES + 3, HEAD_TILES + 4):
                    n = (HEAD_TILES, HEAD_TILES + 3, HEAD_TILES + 4).index(i)
                    if n == 0:
                        pe.wait_ge(o_lo_ready, 2)
                    pe.wait_ge(exp_ready, 2 * (HEAD_TILES - 1))
                    unit(U_WO + n)
                    tile512(U_WO + n, n % 2, WO_BANKS[n // 2][0], 0)
            pe.wait_ge(o_lo_ready, 4)
            for n in range(3):
                tile512(U_WO + n, n % 2, WO_BANKS[n // 2][1], 1).then_inc(unit_used, 1)
            block512(U_WO + 3, 1, WO_BANKS[1], early=True)

            def transpose_hidden(g, k=0):
                pe.wait_ge(hidden_ready, g + 1 + FB * k)
                if g:
                    pe.wait_ge(ht_lo_ready, g + FB * k)
                for n in range(4):
                    src = (n % 2) * 256 + (n // 2) * P if g < JF else n * P
                    last = nc.tensor.transpose(ps[:, 2, n * P:(n + 1) * P], hidden[:, src:src + P], ident[:, :])
                last.then_inc(hidden_transposed, 1)

            def dense_in(j):
                for n, freed in ((0, silu_ready), (1, hidden_ready)):
                    u = dense_group(j) + n
                    unit(u)
                    if j:
                        pe.wait_ge(freed, j)
                    for tt in range(TT):
                        for c in range(KD):
                            if j == 0 and n == 0 and c % 4 == 0:
                                pe.wait_ge(xt_lo_ready, 4 * XT_OF[1] + 2 * tt + c // 4 + 1)
                            last = product(ps[:, n, 256 * tt:256 * tt + 256], acts(c, tt), weights(u, c, 0, 256, 256),
                                           c == 0, c == KD - 1)
                    last.then_inc(unit_used, 1)

            def dense_out(j):
                u = dense_down(j)
                unit(u)
                pe.wait_ge(ht_lo_ready, j + 1)
                for tt in range(TT):
                    for half in range(2):
                        for c in range(2):
                            at = c * SEQ + tt * P
                            last = product(ps[:, 4 + 2 * tt + half, :], (h_t_hi[:, at:at + P], h_t_lo[:, at:at + P]),
                                           weights(u, c, 512 * half, 512, D), j == 0 and c == 0, j == JF - 1 and c == 1)
                    if j == JF - 1 and tt == 0:
                        last.then_inc(tile0_used, 1)
                last.then_inc(unit_used, 1)

            transpose_norm(1)
            for j in range(JF):
                dense_in(j)
                if j:
                    dense_out(j - 1)
                transpose_hidden(j)
            dense_out(JF - 1)

            pe.wait_ge(p_lo_ready, 2)
            unit(U_PLE0)
            project(0, 0, U_PLE0)
            project(0, 1, U_PLE0).then_inc(unit_used, 1)
            transpose_norm(2)
            gates(0, U_PLE0 + 1)

            pe.wait_ge(bands_ready, 1)
            for g in range(4):
                if g % 2 == 0:
                    pe.wait_ge(rows_lo0, g // 2 + 1)
                    pe.wait_ge(rows_lo, g // 2 + 1)
                for c in (2 * g, 2 * g + 1):
                    at = SEQ * (c % 2)
                    first, own = slice(c * P, (c + 1) * P), slice(D + c * P, D + (c + 1) * P)
                    nc.tensor.matmul(ps[:, 4 + g, at:at + SEQ], a_hi[:, first], band_hi[:, g, :], start=True, stop=False)
                    nc.tensor.matmul(ps[:, 4 + g, at:at + SEQ], a_lo[:, first], band_hi[:, g, :], start=False, stop=False)
                    nc.tensor.matmul(ps[:, 4 + g, at:at + 16], a_hi[:, first], band_lo[:, g, :], start=False, stop=False)
                    nc.tensor.matmul(ps[:, 4 + g, at:at + SEQ], a_hi[:, own], band_own[:, g, :], start=False, stop=False)
                    last = nc.tensor.matmul(ps[:, 4 + g, at:at + SEQ], a_lo[:, own], band_own[:, g, :],
                                            start=False, stop=True)
                last.then_inc(pooled, 1)
            unit(U_POOL)
            pe.wait_ge(resid_ready, 12)
            for tt in range(TT):
                for g in range(4):
                    if tt == 0:
                        pe.wait_ge(pool_lo, g + 1)
                    at = 256 * (g % 2)
                    x = (y_hi, y_lo) if g < 2 else (a_hi, a_lo)
                    for c in range(2):
                        xc = slice((2 * (g % 2) + c) * SEQ + tt * P, (2 * (g % 2) + c) * SEQ + (tt + 1) * P)
                        last = product(ps[:, 2 * tt + g // 2, at:at + 256], (x[0][:, xc], x[1][:, xc]),
                                       weights(U_POOL, 2 * g + c, 0, 256, 256), c == 0, c == 1)
                if tt == 0:
                    last.then_inc(tile0_used, 1)
            last.then_inc(unit_used, 1)

            transpose_norm(4)
            pe.wait_ge(router_lo_ready, 1)
            for b in range(2):
                for tt in range(TT):
                    pe.wait_ge(xt_lo_ready, 4 * XT_OF[4] + 2 * tt + b + 1)
                for c in range(4 * b, 4 * b + 4):
                    x = a_hi[:, c * SEQ:(c + 1) * SEQ], a_lo[:, c * SEQ:(c + 1) * SEQ]
                    r = slice(NE * c, NE * c + P)
                    nc.tensor.matmul(ps[:, 0, 0:SEQ], router_hi[:, r], x[0], start=c == 0, stop=False)
                    nc.tensor.matmul(ps[:, 0, 0:SEQ], router_hi[:, r], x[1], start=False, stop=False)
                    last = nc.tensor.matmul(ps[:, 0, 0:SEQ], router_lo[:, r], x[0], start=False, stop=c == KD - 1)
            last.then_inc(routed, 1)
            pe.wait_ge(logits_t_ready, 1)
            for tt in range(TT):
                last = nc.tensor.transpose(ps[:, 2, NE * tt:NE * (tt + 1)], logits_t[:, tt * P:(tt + 1) * P],
                                           ident[0:NE, 0:NE])
            last.then_inc(logits_ready, 1)
            pe.wait_ge(mask_ready, 1)
            nc.tensor.matmul(ps[:, 1, 0:8], before[:, :], mask[:, 0, :], start=True, stop=True)
            nc.tensor.matmul(ps[:, 1, 8:16], before[:, :], mask[:, 1, :], start=True, stop=False)
            nc.tensor.matmul(ps[:, 1, 8:16], ones16[:, :], mask[:, 0, :], start=False, stop=True)
            nc.tensor.matmul(ps[:, 1, 16:24], ones16[:, :], mask[:, 2, :], start=True, stop=True).then_inc(counted, 1)

            def gather(t0, k=0):
                pe.wait_ge(pick_ready, t0 + 1 + k)
                if t0 >= 2:
                    pe.wait_ge(added, 4 * (t0 - 1 + k))
                for c in range(KD):
                    for tt in range(TT):
                        last = nc.tensor.matmul(ps[:, 5 + c // 4, (c % 4) * P:(c % 4 + 1) * P],
                                                xs[:, tt, c * P:(c + 1) * P],
                                                pick[:, tt * SLOTS:(tt + 1) * SLOTS], start=tt == 0, stop=tt == TT - 1)
                    if c % 4 == 3:
                        last.then_inc(gathered, 1)

            def scatter(q, t, k=0):
                pe.wait_ge(y_lo_ready, t + 1 + k)
                pe.wait_ge(pick_t_copied, t + 1 + k)
                if q < 2:
                    pe.wait_ge(xe_lo_ready, 2 * (t + 2 + k))
                else:
                    pe.wait_ge(added, 4 * (t + k) + q - 1)
                tt, half = q // 2, q % 2
                for y, stop in ((y_hi, False), (y_lo, True)):
                    last = nc.tensor.matmul(ps[:, 5 + q % 2, :], pick_t[:, tt * P:(tt + 1) * P],
                                            y[:, 512 * half:512 * half + 512], start=not stop, stop=stop)
                last.then_inc(scattered, 1)

            def down(u, f, half, g, k=0):
                unit(u, k)
                pe.wait_ge(ht_lo_ready, g + 1 + FB * k)
                for n in range(2):
                    for c in range(2):
                        at = (2 * half + c) * P
                        last = product(ps[:, 3 + n, :], (h_t_hi[:, at:at + P], h_t_lo[:, at:at + P]),
                                       weights(u, c, 512 * n, 512, D), f == 0 and half == 0 and c == 0,
                                       f == FB - 1 and half == 1 and c == 1)
                last.then_inc(unit_used, 1)

            def turn(t0, k=0):
                for f in range(FB):
                    u, g = turn_unit(t0, f), JF + FB * t0 + f
                    for n, freed in ((0, silu_ready), (1, hidden_ready)):
                        for half in range(2):
                            unit(u, k)
                            if f == 0 and n == 0:
                                pe.wait_ge(xe_lo_ready, 2 * (t0 + k) + half + 1)
                            if half == 0:
                                pe.wait_ge(freed, g + FB * k)
                            for c in range(4):
                                at = (4 * half + c) * P
                                last = product(ps[:, n, :], (xe_hi[:, at:at + P], xe_lo[:, at:at + P]),
                                               weights(u, c, 0, 512, 512), half == 0 and c == 0, half == 1 and c == 3)
                            last.then_inc(unit_used, 1)
                            u += 1
                    if f == 1 and t0:
                        scatter(0, t0 - 1, k)
                        scatter(1, t0 - 1, k)
                    if f == 2:
                        if t0:
                            pe.wait_ge(pick_t_copied, t0 + k)
                        for tt in range(TT):
                            last = nc.tensor.transpose(ps[:, 7, tt * P:(tt + 1) * P],
                                                       pick[:, tt * SLOTS:(tt + 1) * SLOTS], ident[:, :])
                        last.then_inc(pick_transposed, 1)
                    if f == FB - 1:
                        gather(t0 + 1, k)
                    if f or t0:
                        if f == 1 and t0:
                            pe.wait_ge(y_lo_ready, t0 + k)
                        for half in range(2):
                            down(u, (f - 1) % FB, half, g - 1, k)
                            u += 1
                    if f == 1 and t0:
                        scatter(2, t0 - 1, k)
                        scatter(3, t0 - 1, k)
                    transpose_hidden(g, k)

            gather(0)
            turn(0)
            pe.wait_ge(more_ready, 1)
            extra = pe.value_load(more[0:1, 0:1], min_val=0, max_val=NE)
            turns = extra + (NE - 1)
            with pe.Fori(1, turns + 1) as it:
                turn(1, it - 1)
            for half in range(2):
                down(U_TURN + half, FB - 1, half, JF + FB - 1, turns)
            unit(U_TURN + 2, turns)
            pe.wait_ge(pick_t_copied, turns + 1)
            project(1, 0, U_TURN + 2)
            for q in range(4):
                scatter(q, 0, turns)
            project(1, 1, U_TURN + 2).then_inc(unit_used, 1)
            transpose_norm(5)
            gates(1, U_TURN + 3, turns)

        @block.scalar
        def _(act):
            def used(u, k=0):
                act.wait_ge(unit_used, u + 1 + PER_EXPERT * k)

            def square_norm(n, k=0):
                for q, (tt, b) in enumerate(QUARTERS[n]):
                    if n == 0:
                        act.wait_ge(x_landed[tt], 16)
                    elif n < 5:
                        act.wait_ge(resid_ready, 4 * (n - 1) + q + 1)
                    else:
                        act.wait_ge(added, 4 * k + q + 1)
                    cols, at = slice(512 * b, 512 * b + 512), 2 * tt + b
                    nc.scalar.activation(xs[:, tt, cols], resid[:, tt, cols], ACT.Square, scale=D ** -0.5,
                                         accum_out=mean_sq[:, at:at + 1]).then_inc(squares_ready, 1)

            def transposed_hi(n, quarters=range(4)):
                for q in quarters:
                    tt, b = q // 2, q % 2
                    act.wait_ge(xs_transposed, 4 * XT_OF[n] + q + 1)
                    nc.scalar.activation(quarter(a_hi, tt, b), bank4(NORM_BANKS[n][q]), ACT.Copy).then_inc(xt_hi_ready, 1)

            def sigmoids(layer, n, u, k=0):
                for tt in range(TT):
                    q = 2 * n + tt
                    if n == 1 and tt == 0:
                        act.wait_ge(tile0_used, 3 if layer == 0 else 5)
                    else:
                        used(u, k)
                    if q >= 2:
                        act.wait_ge(resid_ready, 8 * (layer + 1) + q - 1)
                    if layer == 0 and q == 0:
                        act.wait_ge(bands_ready, 1)
                    nc.scalar.activation(sig[tt], ps[:, GATE_BANKS[layer][q], :], ACT.Sigmoid).then_inc(sig_ready, 1)

            square_norm(0)
            transposed_hi(0, (0, 1))
            split_hi(0)
            transposed_hi(0, (2, 3))
            split_hi(1)

            for u in range(U_QKV, U_WO):
                if u not in (4, 8):
                    split_hi(u + AHEAD)
                if u % 2 == 0:
                    continue
                nb = u // 2
                used(u)
                for tt in range(TT):
                    nc.scalar.activation(qkv[:, tt, 512 * nb:512 * nb + 512], ps[:, 2 * (nb % 4) + tt, :],
                                         ACT.Copy).then_inc(block_copied, 1)
                if nb == 2:
                    act.wait_ge(small_landed, 144)
                    nc.scalar.activation(router_hi[:, 0:KD * NE], router[:, :], ACT.Copy).then_inc(router_hi_ready, 1)
                    act.wait_ge(lam_summed, 1)
                    nc.scalar.activation(lam_sum[:, :], lam_sum[:, :], ACT.Exp).then_inc(lam_exp, 1)
                if nb in (1, 3):
                    for m in (nb - 1, nb):
                        s, tt = m // 2, m % 2
                        act.wait_ge(block_copied, 4 * (s + 1))
                        if m:
                            act.wait_ge(qk_mean, m)
                        nc.scalar.activation(squares, qkv[:, tt, s * D:(s + 1) * D], ACT.Square).then_inc(qk_squares, 1)
                        if m % 2 == 0:
                            split_hi(u + 1 + AHEAD)
                        if m == 0:
                            for layer in range(2):
                                act.wait_ge(p_transposed, layer + 1)
                                nc.scalar.activation(p_t_hi[:, layer, :], ps[:, 6 + layer, :],
                                                     ACT.Copy).then_inc(p_hi_ready, 1)
                if nb >= 4:
                    s = nb - 4
                    for pair in range(4):
                        act.wait_ge(qk_transposed, 4 * s + pair + 1)
                        if s == 0:
                            dst = q_t[:, 2 * pair:2 * pair + 2, :].rearrange("p h (t s) -> p h t s", t=TT)
                        else:
                            dst = qkv[:, :, 2 * pair * P:(2 * pair + 2) * P].rearrange("p t (h s) -> p h t s", h=2)
                        src = ps[:, 4 + pair, :].rearrange("p (h t s) -> p h t s", h=2, t=TT)
                        nc.scalar.activation(dst, src, ACT.Copy).then_inc(qk_t_copied, 1)

            for i in range(HEAD_TILES + 9):
                if 3 <= i < HEAD_TILES + 3:
                    j = i - 3
                    act.wait_ge(probs_transposed, j + 1)
                    if j >= 2:
                        act.wait_ge(av_ready, j - 1)
                    nc.scalar.activation(probs_t[:, j % 2, 0:keys_of(j)], ps[:, 4 + j % 2, 0:keys_of(j)],
                                         ACT.Copy).then_inc(probs_t_copied, 1)
                if i < HEAD_TILES:
                    b, nk = i % BUFS, keys_of(i)
                    act.wait_ge(shift_ready, i + 1)
                    if i == 0:
                        act.wait_ge(qk_rotated, 4)
                    if i >= BUFS:
                        act.wait_ge(probs_transposed, i - BUFS + 1)
                    for c in range(2):
                        nc.scalar.activation(probs[:, b, 256 * c:256 * c + nk], ps[:, b, 256 * c:256 * c + nk], ACT.Exp,
                                             bias=smax[:, b, 2 + c:3 + c], scale=SCALE,
                                             accum_out=esum[:, b, c:c + 1]).then_inc(exp_ready, 1)
                if i >= 7 and (i - 7) % 4 == 0 and i < HEAD_TILES + 4:
                    m = (i - 7) // 4
                    act.wait_ge(av_ready, 4 * (m + 1))
                    at = D + 512 * (m % 2)
                    nc.scalar.activation(qkv[:, m // 2, at:at + 512], ps[:, 6 + m % 2, :], ACT.Copy).then_inc(av_copied, 1)
                if i >= 7 and (i - 7) % 4 < 2 and i < HEAD_TILES + 5:
                    m, part = (i - 7) // 4, (i - 7) % 4
                    for h in (2 * part, 2 * part + 1):
                        nc.scalar.activation(y_hi[:, h * P:(h + 1) * P], ps[:, 6 + m % 2, h * P:(h + 1) * P], ACT.Square,
                                             accum_out=mean_sq[:, 80 + 4 * m + h:81 + 4 * m + h]).then_inc(o_squares, 1)
                if i >= 12 and (i - 12) % 4 == 0:
                    m = (i - 12) // 4
                    act.wait_ge(o_transposed, m + 1)
                    nc.scalar.activation(quarter(a_hi, m // 2, m % 2), bank4(3), ACT.Copy,
                                         scale=sub_gain[:, 0:1]).then_inc(o_hi_ready, 1)
                if i == HEAD_TILES + 1:
                    split_hi(U_WO + AHEAD)
            for u in range(U_WO + 1, U_FFN):
                split_hi(u + AHEAD)

            def silus(g, u, k=0):
                used(u, k)
                if g:
                    act.wait_ge(hidden_ready, g + FB * k)
                nc.scalar.activation(silu, ps[:, 0, :], ACT.Silu).then_inc(silu_ready, 1)

            def hidden_hi(g, k=0):
                act.wait_ge(hidden_transposed, g + 1 + FB * k)
                nc.scalar.activation(h_t_hi[:, :], ps[:, 2, :], ACT.Copy).then_inc(ht_hi_ready, 1)

            square_norm(1)
            transposed_hi(1)
            for j in range(JF):
                u = dense_group(j)
                split_hi(u + AHEAD)
                silus(j, u)
                split_hi(u + 1 + AHEAD)
                if j:
                    split_hi(u + 2 + AHEAD)
                hidden_hi(j)
            split_hi(dense_down(JF - 1) + AHEAD)

            square_norm(2)
            split_hi(U_PLE0 + AHEAD)
            transposed_hi(2)
            for n in range(2):
                split_hi(U_PLE0 + 1 + 2 * n + AHEAD)
                split_hi(U_PLE0 + 2 + 2 * n + AHEAD)
                sigmoids(0, n, U_PLE0 + 2 + 2 * n)

            square_norm(3)
            for q in range(4):
                act.wait_ge(xs_ready, 4 * 3 + q + 1)
                nc.scalar.activation(a_hi[:, 512 * q:512 * q + 512], xs_flat[:, 512 * q:512 * q + 512],
                                     ACT.Copy).then_inc(rows_hi, 1)
            for g in range(4):
                act.wait_ge(pooled, g + 1 if g < 2 else 4)
                nc.scalar.activation(pool_half(y_hi, a_hi, g), ps[:, 4 + g, :], ACT.Copy).then_inc(pool_hi, 1)
            split_hi(U_POOL + AHEAD)

            square_norm(4)
            transposed_hi(4)
            split_hi(U_MOE + AHEAD)
            act.wait_ge(routed, 1)
            nc.scalar.activation(logits_t, ps[0:NE, 0, 0:SEQ], ACT.Copy).then_inc(logits_t_ready, 1)
            act.wait_ge(gap_ready, 1)
            nc.scalar.activation(top_w[:, :, 1:2], top_w[:, :, 0:1], ACT.Exp).then_inc(gap_exp, 1)

            def tokens_hi(t, k=0):
                for b in range(2):
                    act.wait_ge(gathered, 2 * (t + k) + b + 1)
                    nc.scalar.activation(xe_hi[:, 512 * b:512 * b + 512], ps[:, 5 + b, :],
                                         ACT.Copy).then_inc(xe_hi_ready, 1)

            def result_hi(u, k=0):
                used(u, k)
                nc.scalar.activation(y_hi[:, :].rearrange("p (b n) -> p b n", b=2), ps[:, 3:5, :],
                                     ACT.Copy).then_inc(y_hi_ready, 1)

            def turn(t0, k=0):
                for f in range(FB):
                    u, g = turn_unit(t0, f), JF + FB * t0 + f
                    if f or t0:
                        split_hi(u + AHEAD, k)
                    split_hi(u + 1 + AHEAD, k)
                    silus(g, u + 1, k)
                    split_hi(u + 2 + AHEAD, k)
                    split_hi(u + 3 + AHEAD, k)
                    if f == FB - 1:
                        tokens_hi(t0 + 1, k)
                    if f or t0:
                        split_hi(u + 4 + AHEAD, k)
                        split_hi(u + 5 + AHEAD, k)
                    hidden_hi(g, k)
                    if f == 0 and t0:
                        result_hi(u + 5, k)

            tokens_hi(0)
            turn(0)
            act.wait_ge(more_ready, 1)
            extra = act.value_load(more[0:1, 0:1], min_val=0, max_val=NE)
            turns = extra + (NE - 1)
            with act.Fori(1, turns + 1) as it:
                turn(1, it - 1)
            split_hi(U_TURN + AHEAD, turns)
            split_hi(U_TURN + 1 + AHEAD, turns)
            result_hi(U_TURN + 1, turns)

            split_hi(U_TURN + 2 + AHEAD, turns)
            square_norm(5, turns)
            transposed_hi(5)
            for n in range(2):
                if n == 0:
                    split_hi(U_TURN + 3 + AHEAD, turns)
                    split_hi(U_TURN + 4 + AHEAD, turns)
                sigmoids(1, n, U_TURN + 4 + 2 * n, turns)

        @block.vector
        def _(dve):
            chain = [0]

            def then(ins):
                chain[0] += 1
                ins.then_inc(dve_chain, 1)
                dve.wait_ge(dve_chain, chain[0])

            def used(u, k=0):
                dve.wait_ge(unit_used, u + 1 + PER_EXPERT * k)

            def norm_rows(n):
                def mean(tt):
                    dve.wait_ge(squares_ready, 4 * n + QUARTERS[n].index((tt, 1)) + 1)
                    nc.vector.tensor_scalar(mean_sq[:, 8 + tt:9 + tt], mean_sq[:, 2 * tt:2 * tt + 1],
                                            mean_sq[:, 2 * tt + 1:2 * tt + 2], EPS, ALU.add,
                                            ALU.add).then_inc(mean_ready, 1)

                mean(0)
                dve.wait_ge(gain_landed[n % 2], 16 * (n // 2 + 1))
                for q in range(4):
                    tt, b = q // 2, q % 2
                    if b == 0:
                        dve.wait_ge(rstd_ready, 2 * n + tt + 1)
                    cols = slice(512 * b, 512 * b + 512)
                    nc.vector.scalar_tensor_tensor(out=xs[:, tt, cols], in0=resid[:, tt, cols], scalar=rstd[:, 8 + tt:9 + tt],
                                                   in1=gain_bc[n % 2][:, cols], op0=ALU.mult,
                                                   op1=ALU.mult).then_inc(xs_ready, 1)
                    if q == 0:
                        mean(1)

            def transposed_lo(n, quarters=range(4)):
                for q in quarters:
                    tt, b = q // 2, q % 2
                    dve.wait_ge(xt_hi_ready, 4 * XT_OF[n] + q + 1)
                    nc.vector.tensor_tensor(quarter(a_lo, tt, b), bank4(NORM_BANKS[n][q]),
                                            quarter(a_hi, tt, b).bitcast(F32), ALU.subtract).then_inc(xt_lo_ready, 1)

            def mean_of(at, n, width):
                return nc.vector.tensor_scalar(mean_sq[:, at:at + n], mean_sq[:, at:at + n], 1.0 / width, EPS,
                                               ALU.mult, ALU.add)

            norm_rows(0)
            transposed_lo(0, (0, 1))
            split_lo(0)
            transposed_lo(0, (2, 3))
            split_lo(1)

            def small_inputs():
                dve.wait_ge(small_landed, 144)
                nc.vector.tensor_tensor(lam_prod[:, 0, :], lam_in[:, 0, :], lam_in[:, 1, :], ALU.mult)
                then(nc.vector.tensor_tensor(lam_prod[:, 1, :], lam_in[:, 2, :], lam_in[:, 3, :], ALU.mult))
                nc.vector.tensor_reduce(lam_sum[:, :], lam_prod[:, :, :], AX_X, ALU.add).then_inc(lam_summed, 1)
                for s in range(2):
                    for n, (angle, half) in enumerate(((0, 0), (1, 1), (0, 1), (1, 0))):
                        gain = qk_gain[:, s, half * 32:half * 32 + 32].unsqueeze(1).to_broadcast([P, TT, 32])
                        last = nc.vector.tensor_tensor(rope_g[:, s, :, n, :], rope[:, :, angle, :], gain, ALU.mult)
                last.then_inc(rope_g_ready, 1)
                dve.wait_ge(consts_ready, 1)
                nc.vector.reciprocal(inv_count[:, :], inv_count[:, :]).then_inc(counts_inverted, 1)
                nc.vector.tensor_scalar(sub_gain[:, :], sub_gain[:, :], 1.0 - LAM_INIT, None, ALU.mult)

            def embeddings_lo():
                for layer in range(2):
                    dve.wait_ge(p_hi_ready, layer + 1)
                    nc.vector.tensor_tensor(p_t_lo[:, layer, :], ps[:, 6 + layer, :], p_t_hi[:, layer, :].bitcast(F32),
                                            ALU.subtract).then_inc(p_lo_ready, 1)

            def router_and_lambda():
                dve.wait_ge(router_hi_ready, 1)
                nc.vector.tensor_tensor(router_lo[:, 0:KD * NE], router[:, :], router_hi[:, 0:KD * NE].bitcast(F32),
                                        ALU.subtract).then_inc(router_lo_ready, 1)
                dve.wait_ge(lam_exp, 1)
                then(nc.vector.tensor_tensor(neg_lam[:, :], lam_sum[:, 1:2], lam_sum[:, 0:1], ALU.subtract))
                then(nc.vector.tensor_scalar(neg_lam[:, :], neg_lam[:, :], LAM_INIT, None, ALU.subtract))

            def qk_mean_squares(m):
                at = 16 + SUB * m
                dve.wait_ge(qk_squares, m + 1)
                then(nc.vector.tensor_reduce(mean_sq[:, at:at + SUB], squares.rearrange("p (g d) -> p g d", g=SUB),
                                             AX_X, ALU.add))
                mean_of(at, SUB, DH).then_inc(qk_mean, 1)

            def rotate(m):
                s, tt = m // 2, m % 2
                x = qkv[:, tt, s * D:(s + 1) * D].rearrange("p (g d) -> p g d", g=SUB)
                x1, x2 = x[:, :, 0:32], x[:, :, 32:64]

                def factor(n):
                    return rope_g[:, s, tt, n, :].unsqueeze(1).to_broadcast([P, SUB, 32])

                at = 16 + SUB * m
                dve.wait_ge(qk_rstd, m + 1)
                nc.vector.tensor_tensor(x, x, rstd[:, at:at + SUB].unsqueeze(2).to_broadcast([P, SUB, DH]),
                                        ALU.mult).then_inc(qk_normed, 1)
                dve.wait_ge(qk_normed, m + 1)
                t = turned[0].rearrange("p (g d) -> p g d", g=SUB)
                t2 = turned[1].rearrange("p (g d) -> p g d", g=SUB)
                then(nc.vector.tensor_tensor(t, x2, factor(1), ALU.mult))
                dve.wait_ge(qk_half, m + 1)
                nc.vector.tensor_tensor(x1, x1, factor(0), ALU.mult)
                then(nc.vector.tensor_tensor(x2, x2, factor(2), ALU.mult))
                nc.vector.tensor_tensor(x1, x1, t, ALU.subtract)
                nc.vector.tensor_tensor(x2, x2, t2, ALU.add).then_inc(qk_rotated, 1)

            for u in range(U_QKV, U_WO):
                split_lo(u + AHEAD)
                if u == 1:
                    small_inputs()
                if u == 4:
                    embeddings_lo()
                if u in MEANS_AT:
                    qk_mean_squares(MEANS_AT.index(u))
                if u in ROTATE_AT:
                    rotate(ROTATE_AT.index(u))
                if u == 5:
                    router_and_lambda()

            def softmax_end(j):
                b, nk = j % BUFS, keys_of(j)
                dve.wait_ge(exp_ready, 2 * (j + 1))
                then(nc.vector.reciprocal(esum[:, b, 2:4], esum[:, b, 0:2]))
                then(nc.vector.tensor_tensor(esum[:, b, 3:4], esum[:, b, 3:4], neg_lam[:, :], ALU.mult))
                second = probs[:, b, 256:256 + nk]
                then(nc.vector.tensor_scalar(second, second, esum[:, b, 3:4], None, ALU.mult))
                nc.vector.scalar_tensor_tensor(out=probs[:, b, 0:nk], in0=probs[:, b, 0:nk], scalar=esum[:, b, 2:3],
                                               in1=second, op0=ALU.mult, op1=ALU.add).then_inc(probs_ready, 1)

            for i in range(HEAD_TILES + 9):
                if i < HEAD_TILES:
                    b, nk = i % BUFS, keys_of(i)
                    dve.wait_ge(scores_ready, i + 1)
                    then(nc.vector.tensor_reduce(smax[:, b, 0:2],
                                                 ps[:, b, :].rearrange("p (c n) -> p c n", c=2)[:, :, 0:nk],
                                                 AX_X, ALU.max))
                    nc.vector.tensor_scalar(smax[:, b, 2:4], smax[:, b, 0:2], -SCALE, None,
                                            ALU.mult).then_inc(shift_ready, 1)
                if 1 <= i < HEAD_TILES + 1:
                    softmax_end(i - 1)
                if i >= 9 and (i - 9) % 4 == 0 and (i - 9) // 4 < 4:
                    m = (i - 9) // 4
                    dve.wait_ge(o_squares, 4 * (m + 1))
                    mean_of(80 + 4 * m, 4, 2 * DH).then_inc(o_mean, 1)
                if i >= 10 and (i - 10) % 4 == 0 and (i - 10) // 4 < 4:
                    m = (i - 10) // 4
                    dve.wait_ge(o_rstd, m + 1)
                    at = D + 512 * (m % 2)
                    o = qkv[:, m // 2, at:at + 512].rearrange("p (h d) -> p h d", h=4)
                    scale = rstd[:, 80 + 4 * m:84 + 4 * m].unsqueeze(2).to_broadcast([P, 4, 2 * DH])
                    nc.vector.tensor_tensor(o, o, scale, ALU.mult).then_inc(o_normed, 1)
                if i >= 12 and (i - 12) % 4 == 0:
                    m = (i - 12) // 4
                    dve.wait_ge(o_hi_ready, m + 1)
                    nc.vector.scalar_tensor_tensor(out=quarter(a_lo, m // 2, m % 2), in0=bank4(3), scalar=sub_gain[:, 0:1],
                                                   in1=quarter(a_hi, m // 2, m % 2).bitcast(F32), op0=ALU.mult,
                                                   op1=ALU.subtract).then_inc(o_lo_ready, 1)
                if i == HEAD_TILES + 1:
                    split_lo(U_WO + AHEAD)
            for u in range(U_WO + 1, U_FFN):
                split_lo(u + AHEAD)
                if u % 2:
                    nb = (u - U_WO) // 2
                    for tt in range(TT):
                        if nb == 1 and tt == 0:
                            dve.wait_ge(tile0_used, 1)
                        else:
                            used(u)
                        r = resid[:, tt, 512 * nb:512 * nb + 512]
                        nc.vector.tensor_tensor(r, r, ps[:, WO_BANKS[nb][tt], :], ALU.add).then_inc(resid_ready, 1)

            def hiddens(g, u, k=0):
                used(u, k)
                dve.wait_ge(silu_ready, g + 1 + FB * k)
                if g:
                    dve.wait_ge(hidden_transposed, g + FB * k)
                nc.vector.tensor_tensor(hidden, silu, ps[:, 1, :], ALU.mult).then_inc(hidden_ready, 1)

            def hidden_lo(g, k=0):
                dve.wait_ge(ht_hi_ready, g + 1 + FB * k)
                nc.vector.tensor_tensor(h_t_lo[:, :], ps[:, 2, :], h_t_hi[:, :].bitcast(F32),
                                        ALU.subtract).then_inc(ht_lo_ready, 1)

            norm_rows(1)
            transposed_lo(1)
            for j in range(JF):
                u = dense_group(j)
                split_lo(u + AHEAD)
                split_lo(u + 1 + AHEAD)
                hiddens(j, u + 1)
                if j:
                    split_lo(u + 2 + AHEAD)
                hidden_lo(j)
            split_lo(dense_down(JF - 1) + AHEAD)
            for tt in range(TT):
                if tt == 0:
                    dve.wait_ge(tile0_used, 2)
                else:
                    used(dense_down(JF - 1))
                for half in range(2):
                    r = resid[:, tt, 512 * half:512 * half + 512]
                    nc.vector.tensor_tensor(r, r, ps[:, 4 + 2 * tt + half, :], ALU.add).then_inc(resid_ready, 1)

            def add_gated(layer, n):
                for tt in range(TT):
                    q = 2 * n + tt
                    dve.wait_ge(sig_ready, 4 * layer + q + 1)
                    nc.vector.tensor_tensor(sig[tt], sig[tt], ps[:, PROJ_BANKS[layer][2 * tt + n], :],
                                            ALU.mult).then_inc(projected, 1)
                    dve.wait_ge(projected, 4 * layer + q + 1)
                    r = resid[:, tt, 512 * n:512 * n + 512]
                    nc.vector.tensor_tensor(r, r, sig[tt], ALU.add).then_inc(resid_ready, 1)

            norm_rows(2)
            split_lo(U_PLE0 + AHEAD)
            transposed_lo(2)
            for n in range(2):
                split_lo(U_PLE0 + 1 + 2 * n + AHEAD)
                split_lo(U_PLE0 + 2 + 2 * n + AHEAD)
                add_gated(0, n)

            norm_rows(3)
            for q in (2, 3):
                cols = slice(512 * q, 512 * q + 512)
                dve.wait_ge(rows_hi, q + 1)
                nc.vector.tensor_tensor(a_lo[:, cols], xs_flat[:, cols], a_hi[:, cols].bitcast(F32),
                                        ALU.subtract).then_inc(rows_lo, 1)
            for g in range(4):
                dve.wait_ge(pool_hi, g + 1)
                nc.vector.tensor_tensor(pool_half(y_lo, a_lo, g), ps[:, 4 + g, :], pool_half(y_hi, a_hi, g).bitcast(F32),
                                        ALU.subtract).then_inc(pool_lo, 1)
            split_lo(U_POOL + AHEAD)
            for q in range(4):
                tt, half = q // 2, slice(512 * (q % 2), 512 * (q % 2) + 512)
                if tt == 0:
                    dve.wait_ge(tile0_used, 4)
                else:
                    used(U_POOL)
                dve.wait_ge(biased, q + 1)
                nc.vector.tensor_tensor(resid[:, tt, half], resid[:, tt, half], ps[:, q, :],
                                        ALU.add).then_inc(resid_ready, 1)

            norm_rows(4)
            transposed_lo(4)
            split_lo(U_MOE + AHEAD)

            dve.wait_ge(logits_ready, 1)
            then(nc.vector.tensor_copy(logits[:, :, :].rearrange("p t e -> p (t e)"), ps[:, 2, 0:TT * NE]))
            for tt in range(TT):
                then(nc.vector.max(top_v[:, tt, :], logits[:, tt, :]))
                then(nc.vector.max_index(top_i[:, tt, :], top_v[:, tt, :], logits[:, tt, :]))
            nc.vector.tensor_tensor(top_w[:, :, 0:1], top_v[:, :, 1:2], top_v[:, :, 0:1],
                                    ALU.subtract).then_inc(gap_ready, 1)
            then(nc.vector.tensor_copy(top_f[:, :, :], top_i[:, :, :]))
            for tt in range(TT):
                for n in range(2):
                    last = nc.vector.tensor_scalar(chose[:, tt, n, :], iota_expert[:, :], top_f[:, tt, n:n + 1], None,
                                                   ALU.is_equal)
            then(last)
            then(nc.vector.tensor_tensor(mask[:, 0:TT, :], chose[:, :, 0, :], chose[:, :, 1, :], ALU.add))
            nc.vector.tensor_tensor(mask[:, 2, :], mask[:, 0, :], mask[:, 1, :], ALU.add).then_inc(mask_ready, 1)
            dve.wait_ge(counted, 1)
            nc.vector.memset(place[:, :, 2 * NE:2 * NE + 1], -1.0)
            then(nc.vector.scalar_tensor_tensor(out=place[:, :, 0:NE],
                                                in0=ps[:, 1, 0:TT * NE].rearrange("p (t e) -> p t e", t=TT), scalar=1.0,
                                                in1=mask[:, 0:TT, :], op0=ALU.add, op1=ALU.mult))
            then(nc.vector.tensor_scalar(place[:, :, 0:NE], place[:, :, 0:NE], 1.0, None, ALU.subtract))
            then(nc.vector.tensor_scalar(place[:, :, NE:2 * NE], place[:, :, 0:NE], float(SLOTS), None, ALU.subtract))
            then(nc.vector.tensor_reduce(tokens[:, 0:1], ps[:, 1, 2 * NE:3 * NE], AX_X, ALU.max))
            nc.vector.tensor_scalar(more[:, :], tokens[:, 0:1], float(SLOTS), float(NE), ALU.is_gt,
                                    ALU.mult).then_inc(more_ready, 1)

            def picks(t, k=0):
                if t:
                    dve.wait_ge(pick_transposed, t + k)
                for tt in range(TT):
                    last = nc.vector.tensor_scalar(pick[:, tt * SLOTS:(tt + 1) * SLOTS], iota_slot[:, :],
                                                   place[:, tt, bass.ds(t + k, 1)], None, ALU.is_equal)
                last.then_inc(pick_ready, 1)

            def tokens_lo(t, k=0):
                for b in range(2):
                    dve.wait_ge(xe_hi_ready, 2 * (t + k) + b + 1)
                    cols = slice(512 * b, 512 * b + 512)
                    nc.vector.tensor_tensor(xe_lo[:, cols], ps[:, 5 + b, :], xe_hi[:, cols].bitcast(F32),
                                            ALU.subtract).then_inc(xe_lo_ready, 1)

            def result_lo(t, k=0):
                dve.wait_ge(y_hi_ready, t + 1 + k)
                nc.vector.tensor_tensor(y_lo[:, :].rearrange("p (b n) -> p b n", b=2), ps[:, 3:5, :],
                                        y_hi[:, :].bitcast(F32).rearrange("p (b n) -> p b n", b=2),
                                        ALU.subtract).then_inc(y_lo_ready, 1)

            def add_result(q, t, k=0):
                tt, half = q // 2, q % 2
                dve.wait_ge(scattered, 4 * (t + k) + q + 1)
                r = resid[:, tt, 512 * half:512 * half + 512]
                nc.vector.scalar_tensor_tensor(out=r, in0=ps[:, 5 + q % 2, :], scalar=gate[:, tt, bass.ds(t + k, 1)],
                                               in1=r, op0=ALU.mult, op1=ALU.add).then_inc(added, 1)

            picks(0)
            dve.wait_ge(gap_exp, 1)
            then(nc.vector.tensor_scalar(top_w[:, :, 2:3], top_w[:, :, 1:2], 1.0, None, ALU.add))
            then(nc.vector.reciprocal(top_w[:, :, 2:3], top_w[:, :, 2:3]))
            then(nc.vector.tensor_tensor(top_w[:, :, 3:4], top_w[:, :, 1:2], top_w[:, :, 2:3], ALU.mult))
            for tt in range(TT):
                for at in (0, NE):
                    last = nc.vector.tensor_scalar(gate[:, tt, at:at + NE], chose[:, tt, 0, :], top_w[:, tt, 2:3], None,
                                                   ALU.mult)
            then(last)
            for tt in range(TT):
                for at in (0, NE):
                    last = nc.vector.scalar_tensor_tensor(out=gate[:, tt, at:at + NE], in0=chose[:, tt, 1, :],
                                                          scalar=top_w[:, tt, 3:4], in1=gate[:, tt, at:at + NE],
                                                          op0=ALU.mult, op1=ALU.add)
            then(last)
            tokens_lo(0)

            def turn(t0, k=0):
                for f in range(FB):
                    u, g = turn_unit(t0, f), JF + FB * t0 + f
                    for n in range(0 if f or t0 else 1, 4):
                        split_lo(u + n + AHEAD, k)
                    hiddens(g, u + 3, k)
                    if f == 1 and t0:
                        add_result(0, t0 - 1, k)
                        add_result(1, t0 - 1, k)
                    if f == 2:
                        dve.wait_ge(pick_transposed, t0 + 1 + k)
                        nc.vector.tensor_copy(pick_t[:, :], ps[:, 7, 0:TT * P]).then_inc(pick_t_copied, 1)
                    if f == 3:
                        picks(t0 + 1, k)
                    if f == FB - 1:
                        tokens_lo(t0 + 1, k)
                    if f or t0:
                        split_lo(u + 4 + AHEAD, k)
                        split_lo(u + 5 + AHEAD, k)
                    if f == 1 and t0:
                        add_result(2, t0 - 1, k)
                        add_result(3, t0 - 1, k)
                    hidden_lo(g, k)
                    if f == 0 and t0:
                        result_lo(t0 - 1, k)

            turn(0)
            extra = dve.value_load(more[0:1, 0:1], min_val=0, max_val=NE)
            turns = extra + (NE - 1)
            with dve.Fori(1, turns + 1) as it:
                turn(1, it - 1)
            split_lo(U_TURN + AHEAD, turns)
            split_lo(U_TURN + 1 + AHEAD, turns)
            result_lo(0, turns)
            for q in range(4):
                add_result(q, 0, turns)

            norm_rows(5)
            transposed_lo(5)
            split_lo(U_TURN + 2 + AHEAD, turns)
            for n in range(2):
                if n == 0:
                    split_lo(U_TURN + 3 + AHEAD, turns)
                    split_lo(U_TURN + 4 + AHEAD, turns)
                add_gated(1, n)

        @block.gpsimd
        def _(pool):
            chain = [0]

            def then(ins):
                chain[0] += 1
                ins.then_inc(pool_chain, 1)
                pool.wait_ge(pool_chain, chain[0])

            nc.gpsimd.memset(minus_half[:, :], -0.5)
            nc.gpsimd.memset(ones[:, :], 1.0)
            nc.gpsimd.memset(ones16[:, :], 1.0)
            nc.gpsimd.memset(causal[:, :], 0.0)
            then(nc.gpsimd.memset(ident[:, :], 0.0))
            nc.gpsimd.affine_select(out=ident[:, :], in_=ident[:, :], compare_op=ALU.not_equal, fill=1.0, base=0,
                                    pattern=[[-1, P]], channel_multiplier=1)
            nc.gpsimd.affine_select(out=causal[:, :], in_=causal[:, :], compare_op=ALU.is_ge, fill=MASKED, base=0,
                                    pattern=[[-1, P]], channel_multiplier=1)
            nc.gpsimd.affine_select(out=before[:, :], in_=ones16[:, :], compare_op=ALU.is_gt, fill=0.0, base=0,
                                    pattern=[[1, P]], channel_multiplier=-1)
            nc.gpsimd.iota(iota_slot[:, :], pattern=[[1, SLOTS]], base=0, channel_multiplier=0,
                           allow_small_or_imprecise_dtypes=True)
            nc.gpsimd.iota(inv_count[:, :], pattern=[[1, 16]], base=1, channel_multiplier=0,
                           allow_small_or_imprecise_dtypes=True)
            nc.gpsimd.iota(iota_expert[:, :], pattern=[[1, NE]], base=0, channel_multiplier=0,
                           allow_small_or_imprecise_dtypes=True).then_inc(consts_ready, 1)
            pool.wait_ge(consts_ready, 1)

            def root(at, n):
                return nc.gpsimd.tensor_tensor(rstd[:, at:at + n], mean_sq[:, at:at + n], minus_half[:, 0:n], ALU.pow)

            def norm_root(n):
                for tt in range(TT):
                    pool.wait_ge(mean_ready, 2 * n + tt + 1)
                    root(8 + tt, 1).then_inc(rstd_ready, 1)

            pool.dma_start(rope[:, :, :, :], dram["rope"].rearrange("(t p) a n -> p t a n", p=P)).then_inc(small_landed, 16)
            for n, name in enumerate(("attn_q_norm", "attn_k_norm")):
                pool.dma_start(qk_gain[:, n, :], dram[name][0].partition_broadcast(P)).then_inc(small_landed, 16)
            norm_root(0)
            for n, name in enumerate(("attn_lambda_q1", "attn_lambda_k1", "attn_lambda_q2", "attn_lambda_k2")):
                if n == 2:
                    share_lo(0)
                pool.dma_start(lam_in[:, n, :], dram[name][0].partition_broadcast(P)).then_inc(small_landed, 16)
            pool.dma_start(router[:, :].rearrange("p (c e) -> p c e", c=KD),
                           dram["moe_router"][0].rearrange("(c p) e -> p c e", p=P)).then_inc(small_landed, 16)
            pool.dma_start(sub_gain[:, :], dram["attn_subln"].rearrange("a p -> p a"),
                           allow_slow_non_contiguous=True).then_inc(small_landed, 16)
            for layer in range(2):
                pool.dma_start(p_sb[:, layer], dram["p"][layer, 0].rearrange("(t p) n -> p t n", p=P)).then_inc(p_landed, 16)
            nc.gpsimd.memset(router_hi[:, KD * NE:].bitcast(F32), 0.0)
            nc.gpsimd.memset(router_lo[:, KD * NE:].bitcast(F32), 0.0)

            def rotate_half(m):
                s, tt = m // 2, m % 2
                pool.wait_ge(qk_normed, m + 1)
                if m == 0:
                    pool.wait_ge(rope_g_ready, 1)
                else:
                    pool.wait_ge(qk_rotated, m)
                x1 = qkv[:, tt, s * D:(s + 1) * D].rearrange("p (g d) -> p g d", g=SUB)[:, :, 0:32]
                nc.gpsimd.tensor_tensor(turned[1].rearrange("p (g d) -> p g d", g=SUB), x1,
                                        rope_g[:, s, tt, 3, :].unsqueeze(1).to_broadcast([P, SUB, 32]),
                                        ALU.mult).then_inc(qk_half, 1)

            for u in range(U_QKV, U_WO):
                if u + AHEAD in SHARED:
                    share_lo(u + AHEAD)
                if u in MEANS_AT:
                    m = MEANS_AT.index(u)
                    pool.wait_ge(qk_mean, m + 1)
                    root(16 + SUB * m, SUB).then_inc(qk_rstd, 1)
                if u in ROTATE_AT:
                    rotate_half(ROTATE_AT.index(u))
            for m in range(4):
                pool.wait_ge(o_mean, m + 1)
                root(80 + 4 * m, 4).then_inc(o_rstd, 1)
                if m == 2:
                    share_lo(U_WO + AHEAD)
            for u in range(U_WO + 1, U_FFN):
                if u + AHEAD in SHARED:
                    share_lo(u + AHEAD)


            norm_root(1)
            pool.wait_ge(counts_inverted, 1)
            pool.wait_ge(o_transposed, 4)
            nc.gpsimd.memset(band_own[:, :, 0:P].bitcast(F32), 0.0)
            for g in range(4):
                w = 2 << g
                then(nc.gpsimd.memset(band, 1.0))
                then(nc.gpsimd.affine_select(out=band, in_=band, compare_op=ALU.is_ge, fill=0.0, base=0,
                                             pattern=[[1, SEQ]], channel_multiplier=-1))
                then(nc.gpsimd.affine_select(out=band, in_=band, compare_op=ALU.is_ge, fill=0.0, base=w - 1,
                                             pattern=[[-1, SEQ]], channel_multiplier=1))
                nc.gpsimd.tensor_tensor(band[:, 0:w], band[:, 0:w], inv_count[:, 0:w], ALU.mult)
                then(nc.gpsimd.tensor_scalar(band[:, w:SEQ], band[:, w:SEQ], 1.0 / w, None, ALU.mult))
                then(nc.gpsimd.tensor_tensor(band[:, 0:P], band[:, 0:P], ident[:, :], ALU.subtract))
                then(nc.gpsimd.tensor_copy(band_hi[:, g, :], band))
                nc.gpsimd.tensor_tensor(band_lo[:, g, :], band[:, 0:16], band_hi[:, g, 0:16].bitcast(F32), ALU.subtract)
                then(nc.gpsimd.tensor_copy(band_own[:, g, P + w:SEQ], band[:, w:P]))
                then(nc.gpsimd.memset(band[:, 0:w], 1.0 / w))
                then(nc.gpsimd.affine_select(out=band[:, 0:w], in_=band[:, 0:w], compare_op=ALU.is_ge, fill=0.0, base=0,
                                             pattern=[[1, w]], channel_multiplier=-1))
                then(nc.gpsimd.tensor_tensor(band[:, 0:w], band[:, 0:w], ident[:, 0:w], ALU.subtract))
                then(nc.gpsimd.tensor_copy(band_own[:, g, P:P + w], band[:, 0:w]))
            nc.gpsimd.nop().then_inc(bands_ready, 1)

            pool.wait_ge(scale_landed, 16)
            pool.wait_ge(bias_landed, 16)
            nc.gpsimd.tensor_tensor(bias_bc, bias_bc, scale_bc, ALU.mult).then_inc(mixer_scaled, 1)
            load_wait(pool, U_POOL)
            w = raw_slot(U_POOL).rearrange("p (g c e) -> p g c e", g=4, c=2)
            scale = scale_bc.rearrange("p (g e) -> p g e", g=4).unsqueeze(2).to_broadcast([P, 4, 2, 256])
            nc.gpsimd.tensor_tensor(w, w, scale, ALU.mult).then_inc(mixer_scaled, 1)
            norm_root(2)
            norm_root(3)
            for q in range(2):
                cols = slice(512 * q, 512 * q + 512)
                pool.wait_ge(rows_hi, q + 1)
                nc.gpsimd.tensor_tensor(a_lo[:, cols], xs_flat[:, cols], a_hi[:, cols].bitcast(F32),
                                        ALU.subtract).then_inc(rows_lo0, 1)
            for q in range(4):
                r, half = resid[:, q // 2, 512 * (q % 2):512 * (q % 2) + 512], slice(512 * (q % 2), 512 * (q % 2) + 512)
                pool.wait_ge(xs_ready, 12 + q + 1)
                nc.gpsimd.tensor_tensor(r, r, bias_bc[:, half], ALU.add).then_inc(biased, 1)
            share_lo(U_POOL + AHEAD)
            norm_root(4)
            norm_root(5)


_INS = ["x", "p", "norm_mix", "norm_ffn", "norm_ple", "attn_w_qkv", "attn_w_o", "attn_q_norm", "attn_k_norm",
        "attn_lambda_q1", "attn_lambda_k1", "attn_lambda_q2", "attn_lambda_k2", "attn_subln", "pool_w", "pool_b",
        "pool_scale", "ffn_w_gate", "ffn_w_up", "ffn_w_down", "moe_router", "moe_w_gate", "moe_w_up", "moe_w_down",
        "ple_w_proj", "ple_w_gate"]


def kernel(**inputs):
    import numpy as np
    import concourse.bacc as bacc
    from concourse.bass_utils import run_bass_kernel_spmd

    nc = bacc.Bacc("TRN2", target_bir_lowering=False, num_devices=1)
    inv = (1.0 / (np.float32(10000.0) ** (np.arange(0, DH, 2, dtype=np.float32) / np.float32(DH)))).astype(np.float32)
    angle = np.arange(SEQ, dtype=np.float32)[:, None] * inv[None, :]
    arrays = {"in_rope_dram": np.stack([np.cos(angle), np.sin(angle)], axis=1).astype(np.float32)}
    for name in _INS:
        arrays[f"in_{name}_dram"] = np.ascontiguousarray(inputs[name])
    dram = {}
    for key, a in arrays.items():
        dram[key[3:-5]] = nc.dram_tensor(key, a.shape, mybir.dt.from_np(a.dtype), kind="ExternalInput").ap()
    dram["out"] = nc.dram_tensor("out_0_dram", (1, SEQ, D), F32, kind="ExternalOutput").ap()
    trunk(nc, dram)
    r = run_bass_kernel_spmd(nc, [arrays], core_ids=[0])
    return r.results[0]["out_0_dram"]
```
